# Optimizing a Trainium2 kernel written in Bass

```python
import functools
import jax, jax.numpy as jnp
from jax import lax
import numpy as np
import math

D_MODEL = 1024
BATCH = 1
SEQ = 256
DEPTH = 2

CHUNK = 64
Q_BLOCK = 128
MLA_HEADS = 8
MLA_NOPE = 64
MLA_ROPE = 32
MLA_V = 64
Q_LORA = 384
KV_LORA = 256
ROPE_THETA = 10000.0
SB_HEADS = 8
SB_DIM = 64
C_HEADS = 16
C_DIM = 64
LEFT_CHUNKS = 8
BAND = (LEFT_CHUNKS + 1) * CHUNK
REL_CLIP = 256
D_FF = -(-8 * D_MODEL // (3 * 256)) * 256
EVEN_IN = Q_LORA + KV_LORA + MLA_ROPE + 3 * SB_HEADS * SB_DIM
MIX_EVEN = MLA_HEADS * MLA_V + SB_HEADS * SB_DIM
MIX_ODD = C_HEADS * C_DIM
N_EVEN = (DEPTH + 1) // 2
N_ODD = DEPTH // 2
RMS_EPS = 1e-6


def rms_norm(x, g):
    x32 = x.astype(jnp.float32)
    y = x32 * lax.rsqrt(jnp.mean(x32 * x32, axis=-1, keepdims=True) + RMS_EPS)
    return (y * g.astype(jnp.float32)).astype(x.dtype)

def rope_tables(seq, dim):
    pos = jnp.arange(seq, dtype=jnp.float32)
    inv_freq = ROPE_THETA ** (-jnp.arange(0, dim, 2, dtype=jnp.float32) / dim)
    ang = pos[:, None] * inv_freq[None, :]
    return jnp.cos(ang), jnp.sin(ang)

def apply_rope(x, cos, sin):
    half = x.shape[-1] // 2
    c, s = cos.astype(x.dtype), sin.astype(x.dtype)
    x1, x2 = x[..., :half], x[..., half:]
    return jnp.concatenate([x1 * c - x2 * s, x2 * c + x1 * s], axis=-1)

def swiglu(u, w_gate, w_up, w_down):
    return (jax.nn.silu(u @ w_gate) * (u @ w_up)) @ w_down

def mla_stick_breaking_mixer(u, w_in, g_cq, w_uq, g_ckv, w_ukv, w_out):
    bsz, seq, _ = u.shape
    proj = u @ w_in
    o1 = Q_LORA
    o2 = o1 + KV_LORA
    o3 = o2 + MLA_ROPE
    nb = SB_HEADS * SB_DIM
    c_q, c_kv, k_r = proj[..., :o1], proj[..., o1:o2], proj[..., o2:o3]
    q_b = proj[..., o3:o3 + nb].reshape(bsz, seq, SB_HEADS, SB_DIM)
    k_b = proj[..., o3 + nb:o3 + 2 * nb].reshape(bsz, seq, SB_HEADS, SB_DIM)
    v_b = proj[..., o3 + 2 * nb:].reshape(bsz, seq, SB_HEADS, SB_DIM)

    cos, sin = rope_tables(seq, MLA_ROPE)
    q_a = (rms_norm(c_q, g_cq) @ w_uq).reshape(bsz, seq, MLA_HEADS, MLA_NOPE + MLA_ROPE)
    q_a = jnp.concatenate([q_a[..., :MLA_NOPE],
                           apply_rope(q_a[..., MLA_NOPE:], cos[:, None, :], sin[:, None, :])], axis=-1)
    kv = (rms_norm(c_kv, g_ckv) @ w_ukv).reshape(bsz, seq, MLA_HEADS, MLA_NOPE + MLA_V)
    k_rope = apply_rope(k_r, cos, sin)
    k_a = jnp.concatenate([kv[..., :MLA_NOPE],
                           jnp.broadcast_to(k_rope[:, :, None, :], (bsz, seq, MLA_HEADS, MLA_ROPE))], axis=-1)
    v_a = kv[..., MLA_NOPE:]
    scale_a = (MLA_NOPE + MLA_ROPE) ** -0.5
    scale_b = SB_DIM ** -0.5

    outs_a, outs_b = [], []
    for blk in range(seq // Q_BLOCK):
        t0 = blk * Q_BLOCK
        kend = t0 + Q_BLOCK
        t_pos = t0 + jnp.arange(Q_BLOCK)[:, None]
        s_pos = jnp.arange(kend)[None, :]
        s_a = jnp.einsum('bqhd,bkhd->bhqk', q_a[:, t0:kend], k_a[:, :kend]).astype(jnp.float32) * scale_a
        chunk_ok = (s_pos // CHUNK) <= (t_pos // CHUNK)
        p_a = jax.nn.softmax(jnp.where(chunk_ok, s_a, -jnp.inf), axis=-1)
        outs_a.append(jnp.einsum('bhqk,bkhd->bqhd', p_a.astype(v_a.dtype), v_a[:, :kend]))
        z = jnp.einsum('bqhd,bkhd->bhqk', q_b[:, t0:kend], k_b[:, :kend]).astype(jnp.float32) * scale_b
        before = s_pos < t_pos
        log_keep = jnp.where(before, jax.nn.log_sigmoid(-z), 0.0)
        log_between = lax.cumsum(log_keep, axis=3, reverse=True) - log_keep
        w_b = jnp.where(before, jnp.exp(jax.nn.log_sigmoid(z) + log_between), 0.0)
        outs_b.append(jnp.einsum('bhqk,bkhd->bqhd', w_b.astype(v_b.dtype), v_b[:, :kend]))

    o_a = jnp.concatenate(outs_a, axis=1).reshape(bsz, seq, MLA_HEADS * MLA_V)
    o_b = jnp.concatenate(outs_b, axis=1).reshape(bsz, seq, SB_HEADS * SB_DIM)
    return jnp.concatenate([o_a, o_b], axis=-1) @ w_out

def chunk_band_mixer(u, w_qkv, rel_bias, w_out):
    bsz, seq, _ = u.shape
    n_chunks = seq // CHUNK
    qkv = (u @ w_qkv).reshape(bsz, n_chunks, CHUNK, 3, C_HEADS, C_DIM)
    q, k, v = qkv[:, :, :, 0], qkv[:, :, :, 1], qkv[:, :, :, 2]
    pad = ((0, 0), (LEFT_CHUNKS, 0), (0, 0), (0, 0), (0, 0))
    k_p = jnp.pad(k, pad)
    v_p = jnp.pad(v, pad)
    scores = jnp.concatenate(
        [jnp.einsum('bnqhd,bnkhd->bnhqk', q, k_p[:, i:i + n_chunks]) for i in range(LEFT_CHUNKS + 1)],
        axis=-1).astype(jnp.float32) * (C_DIM ** -0.5)
    q_in = jnp.arange(CHUNK)[:, None]
    j = jnp.arange(BAND)[None, :]
    rel = (LEFT_CHUNKS - j // CHUNK) * CHUNK + q_in - j % CHUNK
    bias = rel_bias[:, jnp.clip(rel, -REL_CLIP, REL_CLIP) + REL_CLIP]
    valid = (jnp.arange(n_chunks)[:, None] - LEFT_CHUNKS + j // CHUNK) >= 0
    scores = scores + bias.astype(jnp.float32)[None, None]
    p = jax.nn.softmax(jnp.where(valid[None, :, None, None, :], scores, -jnp.inf), axis=-1).astype(v.dtype)
    parts = [jnp.einsum('bnhqk,bnkhd->bnqhd', p[..., i * CHUNK:(i + 1) * CHUNK], v_p[:, i:i + n_chunks])
             for i in range(LEFT_CHUNKS + 1)]
    o = functools.reduce(jnp.add, parts)
    return o.reshape(bsz, seq, MIX_ODD) @ w_out

def first_inputs(seed: int = 0) -> dict:
    key = jax.random.key(seed)
    ks = jax.random.split(key, 17)
    f32 = jnp.float32

    def nrm(k, shape, fan_in):
        return jax.random.normal(k, shape, f32) * (fan_in ** -0.5)

    def gain(k, shape):
        return 1.0 + 0.05 * jax.random.normal(k, shape, f32)

    return {
        "x": jax.random.normal(ks[0], (BATCH, SEQ, D_MODEL), f32),
        "ev_w_in": nrm(ks[1], (N_EVEN, D_MODEL, EVEN_IN), D_MODEL),
        "ev_g_cq": gain(ks[2], (N_EVEN, Q_LORA)),
        "ev_w_uq": nrm(ks[3], (N_EVEN, Q_LORA, MLA_HEADS * (MLA_NOPE + MLA_ROPE)), Q_LORA),
        "ev_g_ckv": gain(ks[4], (N_EVEN, KV_LORA)),
        "ev_w_ukv": nrm(ks[5], (N_EVEN, KV_LORA, MLA_HEADS * (MLA_NOPE + MLA_V)), KV_LORA),
        "ev_w_out": nrm(ks[6], (N_EVEN, MIX_EVEN, D_MODEL), MIX_EVEN),
        "od_w_qkv": nrm(ks[7], (N_ODD, D_MODEL, 3 * MIX_ODD), D_MODEL),
        "od_rel_bias": 0.1 * jax.random.normal(ks[8], (N_ODD, C_HEADS, 2 * REL_CLIP + 1), f32),
        "od_w_out": nrm(ks[9], (N_ODD, MIX_ODD, D_MODEL), MIX_ODD),
        "g_mix": gain(ks[10], (DEPTH, D_MODEL)),
        "g_ffn": gain(ks[11], (DEPTH, D_MODEL)),
        "w_gate": nrm(ks[12], (DEPTH, D_MODEL, D_FF), D_MODEL),
        "w_up": nrm(ks[13], (DEPTH, D_MODEL, D_FF), D_MODEL),
        "w_down": nrm(ks[14], (DEPTH, D_FF, D_MODEL), D_FF),
        "g_final": gain(ks[15], (D_MODEL,)),
    }

def first_block(x, ev_w_in, ev_g_cq, ev_w_uq, ev_g_ckv, ev_w_ukv, ev_w_out,
              od_w_qkv, od_rel_bias, od_w_out, g_mix, g_ffn, w_gate, w_up, w_down, g_final):
    h = x
    for layer in range(DEPTH):
        u = rms_norm(h, g_mix[layer])
        if layer % 2 == 0:
            i = layer // 2
            h = h + mla_stick_breaking_mixer(u, ev_w_in[i], ev_g_cq[i], ev_w_uq[i],
                                             ev_g_ckv[i], ev_w_ukv[i], ev_w_out[i])
        else:
            i = layer // 2
            h = h + chunk_band_mixer(u, od_w_qkv[i], od_rel_bias[i], od_w_out[i])
        u = rms_norm(h, g_ffn[layer])
        h = h + swiglu(u, w_gate[layer], w_up[layer], w_down[layer])
    return rms_norm(h, g_final)


DEPTH_2 = 1

HEAD_DIM = 64
W_BR = D_MODEL // 2
N_BRANCH = 3
H_A = W_BR // HEAD_DIM
MOBA_BLOCK = 256
MOBA_TOPK = 3
MOBA_QCHUNK = 32
DIL_PAIRS = ((128, 1), (512, 4), (2048, 16))
N_DIL = len(DIL_PAIRS)
H_B = W_BR // HEAD_DIM
DIL_QCHUNK = 64
H_C = W_BR // HEAD_DIM
KV_C = 2
SWA_WINDOW = 128
N_BUCKETS = 32
REL_MAX_DIST = 2048
H_TOT = H_A + N_DIL * H_B + H_C
OFF_A = 0
OFF_B = H_A
OFF_C = H_A + N_DIL * H_B

EPS = 1e-6
NEG_INF = -1e30

SPLIT_SIZES = ([W_BR] * 4
               + [N_DIL * W_BR] * 3 + [W_BR]
               + [W_BR, KV_C * HEAD_DIM, KV_C * HEAD_DIM, W_BR]
               + [N_BRANCH * D_MODEL])
C_IN = int(sum(SPLIT_SIZES))
SPLIT_POINTS = [int(v) for v in np.cumsum(SPLIT_SIZES)[:-1]]


def rms_norm_2(x, g):
    x32 = x.astype(jnp.float32)
    y = x32 * lax.rsqrt(jnp.mean(x32 * x32, axis=-1, keepdims=True) + EPS)
    return (y * g.astype(jnp.float32)).astype(x.dtype)

def rel_bucket(dist):
    dist = jnp.maximum(dist, 0)
    max_exact = N_BUCKETS // 2
    log_ratio = jnp.log(jnp.maximum(dist, 1).astype(jnp.float32) / max_exact) / math.log(REL_MAX_DIST / max_exact)
    large = max_exact + (log_ratio * (N_BUCKETS - max_exact)).astype(jnp.int32)
    large = jnp.minimum(large, N_BUCKETS - 1)
    return jnp.where(dist < max_exact, dist, large)

def moba_attention(q, k, v, bias_tab):
    b, s, h, dh = q.shape
    s_pad = -(-s // MOBA_BLOCK) * MOBA_BLOCK
    pad = ((0, 0), (0, s_pad - s), (0, 0), (0, 0))
    qh, kh, vh = [jnp.pad(t, pad).transpose(0, 2, 1, 3) for t in (q, k, v)]
    nb = s_pad // MOBA_BLOCK
    kb = kh.reshape(b, h, nb, MOBA_BLOCK, dh)
    vb = vh.reshape(b, h, nb, MOBA_BLOCK, dh)
    k_mean = jnp.mean(kb.astype(jnp.float32), axis=3)
    gate = jnp.einsum('bhsd,bhnd->bhsn', qh.astype(jnp.float32), k_mean)
    q_blk = jnp.arange(s_pad) // MOBA_BLOCK
    past = jnp.arange(nb)[None, :] < q_blk[:, None]
    gate = jnp.where(past, gate, NEG_INF)
    n_sel = min(MOBA_TOPK, max(nb - 1, 1))
    _, top_idx = lax.top_k(gate, n_sel)
    sel_valid = jnp.arange(n_sel)[None, :] < jnp.minimum(q_blk, MOBA_TOPK)[:, None]
    scale = dh ** -0.5
    bias_tab = bias_tab.astype(jnp.float32)
    b_idx = jnp.arange(b)[:, None, None, None]
    h_idx = jnp.arange(h)[None, :, None, None]
    h_idx5 = jnp.arange(h)[None, :, None, None, None]
    blk_off = jnp.arange(MOBA_BLOCK)

    def chunk(c):
        t0 = c * MOBA_QCHUNK
        t = t0 + jnp.arange(MOBA_QCHUNK)
        q_c = lax.dynamic_slice_in_dim(qh, t0, MOBA_QCHUNK, axis=2)
        idx_c = lax.dynamic_slice_in_dim(top_idx, t0, MOBA_QCHUNK, axis=2)
        valid_c = lax.dynamic_slice_in_dim(sel_valid, t0, MOBA_QCHUNK, axis=0)
        k_sel = kb[b_idx, h_idx, idx_c]
        v_sel = vb[b_idx, h_idx, idx_c]
        s_sel = jnp.einsum('bhqd,bhqjkd->bhqjk', q_c, k_sel,
                           preferred_element_type=jnp.float32) * scale
        key_pos = idx_c[..., None] * MOBA_BLOCK + blk_off
        dist = t[:, None, None] - key_pos
        bias_sel = bias_tab[h_idx5, rel_bucket(dist)]
        s_sel = jnp.where(valid_c[:, :, None], s_sel + bias_sel, NEG_INF)
        n_own = t0 // MOBA_BLOCK
        k_own = lax.dynamic_index_in_dim(kb, n_own, axis=2, keepdims=False)
        v_own = lax.dynamic_index_in_dim(vb, n_own, axis=2, keepdims=False)
        s_own = jnp.einsum('bhqd,bhkd->bhqk', q_c, k_own,
                           preferred_element_type=jnp.float32) * scale
        dist_own = t[:, None] - (n_own * MOBA_BLOCK + blk_off)[None, :]
        s_own = jnp.where(dist_own >= 0, s_own + bias_tab[:, rel_bucket(dist_own)], NEG_INF)
        n_s = n_sel * MOBA_BLOCK
        logits = jnp.concatenate([s_sel.reshape(b, h, MOBA_QCHUNK, n_s), s_own], axis=-1)
        p = jax.nn.softmax(logits, axis=-1)
        p_sel = p[..., :n_s].reshape(b, h, MOBA_QCHUNK, n_sel, MOBA_BLOCK).astype(v.dtype)
        p_own = p[..., n_s:].astype(v.dtype)
        out = (jnp.einsum('bhqjk,bhqjkd->bhqd', p_sel, v_sel, preferred_element_type=jnp.float32)
               + jnp.einsum('bhqk,bhkd->bhqd', p_own, v_own, preferred_element_type=jnp.float32))
        return out.astype(v.dtype)

    out = lax.map(chunk, jnp.arange(s_pad // MOBA_QCHUNK))
    out = out.transpose(1, 0, 3, 2, 4).reshape(b, s_pad, h, dh)
    return out[:, :s]

def dilated_attention(q, k, v, bias_tab):
    b, s, _, h, dh = q.shape
    scale = dh ** -0.5
    bias_tab = bias_tab.astype(jnp.float32)
    n_keys = [w // d + 1 for (w, d) in DIL_PAIRS]
    k_pads = [jnp.pad(k[:, :, gi], ((0, 0), (w, 0), (0, 0), (0, 0))) for gi, (w, d) in enumerate(DIL_PAIRS)]
    v_pads = [jnp.pad(v[:, :, gi], ((0, 0), (w, 0), (0, 0), (0, 0))) for gi, (w, d) in enumerate(DIL_PAIRS)]
    bias_g = [bias_tab[gi * h:(gi + 1) * h][:, rel_bucket(d * jnp.arange(n_keys[gi]))]
              for gi, (w, d) in enumerate(DIL_PAIRS)]

    def chunk(c):
        t0 = c * DIL_QCHUNK
        t = t0 + jnp.arange(DIL_QCHUNK)
        q_c = lax.dynamic_slice_in_dim(q, t0, DIL_QCHUNK, axis=1)
        outs, lses = [], []
        for gi, (w, d) in enumerate(DIL_PAIRS):
            steps = jnp.arange(n_keys[gi]) * d
            idx = t[:, None] + w - steps[None, :]
            k_g = k_pads[gi][:, idx]
            v_g = v_pads[gi][:, idx]
            logits = jnp.einsum('bqhd,bqjhd->bhqj', q_c[:, :, gi], k_g,
                                preferred_element_type=jnp.float32) * scale + bias_g[gi][:, None, :]
            logits = jnp.where((t[:, None] - steps[None, :]) >= 0, logits, NEG_INF)
            lse = jax.nn.logsumexp(logits, axis=-1)
            p = jnp.exp(logits - lse[..., None]).astype(v.dtype)
            outs.append(jnp.einsum('bhqj,bqjhd->bqhd', p, v_g, preferred_element_type=jnp.float32))
            lses.append(lse)
        wts = jax.nn.softmax(jnp.stack(lses, axis=0), axis=0)
        out = sum(wts[gi].transpose(0, 2, 1)[..., None] * outs[gi] for gi in range(N_DIL))
        return out.astype(v.dtype)

    out = lax.map(chunk, jnp.arange(s // DIL_QCHUNK))
    return out.transpose(1, 0, 2, 3, 4).reshape(b, s, h, dh)

def swa_sink_attention(q, k, v, sinks, bias_tab):
    b, s, h, dh = q.shape
    kvh = k.shape[2]
    rep = h // kvh
    W = SWA_WINDOW
    nb = s // W
    scale = dh ** -0.5
    qb = q.reshape(b, nb, W, kvh, rep, dh)
    kb = k.reshape(b, nb, W, kvh, dh)
    vb = v.reshape(b, nb, W, kvh, dh)

    def with_prev(t):
        prev = jnp.pad(t, ((0, 0), (1, 0), (0, 0), (0, 0), (0, 0)))[:, :-1]
        return jnp.concatenate([prev, t], axis=2)

    kk, vv = with_prev(kb), with_prev(vb)
    logits = jnp.einsum('bnqgrd,bnkgd->bngrqk', qb, kk,
                        preferred_element_type=jnp.float32) * scale
    i = jnp.arange(W)
    j = jnp.arange(2 * W)
    dist = i[:, None] + W - j[None, :]
    key_pos = jnp.arange(nb)[:, None] * W - W + j[None, :]
    valid = ((dist >= 0) & (dist < W))[None] & (key_pos >= 0)[:, None, :]
    bias = bias_tab.astype(jnp.float32)[:, rel_bucket(dist)].reshape(kvh, rep, W, 2 * W)
    logits = jnp.where(valid[None, :, None, None], logits + bias, NEG_INF)
    sink = sinks.astype(jnp.float32).reshape(kvh, rep)[None, None, :, :, None, None]
    m = jnp.maximum(jnp.max(logits, axis=-1, keepdims=True), sink)
    e = jnp.exp(logits - m)
    p = e / (jnp.sum(e, axis=-1, keepdims=True) + jnp.exp(sink - m))
    out = jnp.einsum('bngrqk,bnkgd->bnqgrd', p.astype(v.dtype), vv, preferred_element_type=jnp.float32)
    return out.reshape(b, s, h, dh).astype(v.dtype)

def second_inputs(seed: int = 0) -> dict:
    key = jax.random.key(seed)
    ks = jax.random.split(key, 8)
    x = jax.random.normal(ks[0], (BATCH, SEQ, D_MODEL), jnp.float32)
    ln_g = 1.0 + 0.02 * jax.random.normal(ks[1], (DEPTH_2, D_MODEL), jnp.float32)
    w_in = jax.random.normal(ks[2], (DEPTH_2, D_MODEL, C_IN), jnp.float32) * D_MODEL ** -0.5
    qk_g = 1.0 + 0.02 * jax.random.normal(ks[3], (DEPTH_2, 6, HEAD_DIM), jnp.float32)
    sinks = 0.5 * jax.random.normal(ks[4], (DEPTH_2, H_C), jnp.float32)
    w_branch = jax.random.normal(ks[5], (DEPTH_2, N_BRANCH, W_BR, D_MODEL), jnp.float32) * W_BR ** -0.5
    w_out = jax.random.normal(ks[6], (DEPTH_2, D_MODEL, D_MODEL), jnp.float32) * D_MODEL ** -0.5
    rel_bias = 0.2 * jax.random.normal(ks[7], (H_TOT, N_BUCKETS), jnp.float32)
    return {"x": x, "ln_g": ln_g, "w_in": w_in, "qk_g": qk_g, "sinks": sinks,
            "w_branch": w_branch, "w_out": w_out, "rel_bias": rel_bias}

def second_block(x, ln_g, w_in, qk_g, sinks, w_branch, w_out, rel_bias):
    b, s, _ = x.shape
    for l in range(DEPTH_2):
        hn = rms_norm_2(x, ln_g[l])
        proj = jnp.einsum('bsd,dc->bsc', hn, w_in[l])
        (qa, ka, va, ga, qb, kb, vb, gb, qc, kc, vc, gc, gate_logits) = jnp.split(proj, SPLIT_POINTS, axis=-1)
        g = qk_g[l]
        qa = rms_norm_2(qa.reshape(b, s, H_A, HEAD_DIM), g[0])
        ka = rms_norm_2(ka.reshape(b, s, H_A, HEAD_DIM), g[1])
        o_a = moba_attention(qa, ka, va.reshape(b, s, H_A, HEAD_DIM), rel_bias[OFF_A:OFF_A + H_A])
        qb = rms_norm_2(qb.reshape(b, s, N_DIL, H_B, HEAD_DIM), g[2])
        kb = rms_norm_2(kb.reshape(b, s, N_DIL, H_B, HEAD_DIM), g[3])
        o_b = dilated_attention(qb, kb, vb.reshape(b, s, N_DIL, H_B, HEAD_DIM),
                                rel_bias[OFF_B:OFF_B + N_DIL * H_B])
        qc = rms_norm_2(qc.reshape(b, s, H_C, HEAD_DIM), g[4])
        kc = rms_norm_2(kc.reshape(b, s, KV_C, HEAD_DIM), g[5])
        o_c = swa_sink_attention(qc, kc, vc.reshape(b, s, KV_C, HEAD_DIM), sinks[l],
                                 rel_bias[OFF_C:OFF_C + H_C])
        branches = jnp.stack([o_a.reshape(b, s, W_BR) * jax.nn.silu(ga),
                              o_b.reshape(b, s, W_BR) * jax.nn.silu(gb),
                              o_c.reshape(b, s, W_BR) * jax.nn.silu(gc)], axis=2)
        br = jnp.einsum('bsiw,iwd->bsid', branches, w_branch[l])
        gates = jax.nn.sigmoid(gate_logits.reshape(b, s, N_BRANCH, D_MODEL))
        merged = jnp.sum(gates * br, axis=2)
        x = x + jnp.einsum('bsd,de->bse', merged, w_out[l])
    return x


def setup_inputs(seed=0):
    out = dict(first_inputs(seed))
    for name, value in second_inputs(seed + 1).items():
        if name != "x":
            out[name + "_2"] = value
    return out


def reference(
    x, ev_w_in, ev_g_cq, ev_w_uq, ev_g_ckv, ev_w_ukv, ev_w_out, od_w_qkv, od_rel_bias, od_w_out,
    g_mix, g_ffn, w_gate, w_up, w_down, g_final, ln_g_2, w_in_2, qk_g_2, sinks_2, w_branch_2,
    w_out_2, rel_bias_2,
):
    x = first_block(
        x, ev_w_in, ev_g_cq, ev_w_uq, ev_g_ckv, ev_w_ukv, ev_w_out, od_w_qkv, od_rel_bias,
        od_w_out, g_mix, g_ffn, w_gate, w_up, w_down, g_final,
    )
    return second_block(
        x, ln_g_2, w_in_2, qk_g_2, sinks_2, w_branch_2, w_out_2, rel_bias_2,
    )


_drawn_inputs = setup_inputs


def setup_inputs(seed=0):
    import zlib

    import numpy as np

    out = dict(_drawn_inputs(seed))
    spreads = {}
    factors = {'ev_g_cq': 8.0,
     'ev_g_ckv': 6.355,
     'od_rel_bias': 4.66,
     'ln_g_2': 8.0,
     'qk_g_2': 8.0,
     'sinks_2': 189.834,
     'rel_bias_2': 2.863}
    for name, (base, spread) in spreads.items():
        noise = np.random.default_rng([zlib.crc32(name.encode()), seed]).standard_normal(out[name].shape)
        drawn = base * np.exp(spread * noise) if base else spread * noise
        out[name] = __import__('jax').numpy.asarray(drawn.astype(out[name].dtype))
    for name, factor in factors.items():
        out[name] = (out[name] * factor).astype(out[name].dtype)
    return out
```

```python
import math
from contextlib import ExitStack

import numpy as np

import concourse.bass as bass
from concourse import mybir

P = 128
TB = 2
S = TB * P
D = 1024
KT = D // P
FF = 2816
FT = 256
NF = FF // FT
UNIT = 2048
RING = 3
HD = 64
MLA_QK = 96
BR = 512
REL = 383
MASKED = -1e30
EPS = 1e-6
HEAD0 = (0, 8, 32)
CONSTS = 19 * 16
LN_EXP_TABLES = 6


class Ordinals:

    def __init__(self):
        self.unit = 0
        self.slot = 0
        self.chunk = 0
        self.pair = 0
        self.turn = 0
        self.bank = 0
        self.proj = 0
        self.written = 0

    def next_unit(self):
        self.unit = self.unit + 1
        self.slot = (self.slot + 1) % RING


def build_program(nc, x, w_in0, g_cq, w_uq, g_ckv, w_ukv, w_out0, w_qkv, rel_band, w_out1, g_mix, g_ffn,
                  w_gate, w_up, w_down, g_final, g_ln2, w_in2, qk_g, sinks, w_branch, w_out2, rel_bias2,
                  identity, strict_mask, chunk_mask, keep_mask, rope, bucket_onehot, dist_mask, out):
    f32, f32r = mybir.dt.float32, mybir.dt.float32r
    ALU, ACT, AX = mybir.AluOpType, mybir.ActivationFunctionType, mybir.AxisListType

    rel_rows = nc.dram_tensor("rel_rows", [40, REL], f32, kind="Internal").ap()

    ctx = ExitStack()
    with ctx:
        def sb(name, shape, dt=f32):
            return ctx.enter_context(nc.sbuf_tensor(name, shape, dt))

        def sem(name):
            return ctx.enter_context(nc.semaphore(name))

        h = sb("h", [P, TB, D])
        uT_hi = sb("uT_hi", [P, KT, S], f32r)
        uT_lo = sb("uT_lo", [P, KT, S], f32r)
        oT_hi = sb("oT_hi", [P, KT, S], f32r)
        oT_lo = sb("oT_lo", [P, KT, S], f32r)
        w_raw = sb("w_raw", [P, RING, UNIT])
        w_hi = sb("w_hi", [P, RING, UNIT], f32r)
        w_lo = sb("w_lo", [P, RING, UNIT], f32r)
        bias = sb("bias", [P, 4, 8, S])
        qkv = sb("qkv", [P, 3, TB, BR])
        qkT = sb("qkT", [P, 4, 512])
        logit = sb("logit", [P, 2, 2, 384])
        prT = sb("prT", [P, 2, 2, 384])
        heads = sb("heads", [P, TB, 40, HD])
        square = sb("square", [P, TB, BR])
        square_flat = square[:, :, :].rearrange("p b c -> p (b c)")
        gain = sb("gain", [P, D])
        ident = sb("ident", [P, P])
        m_chunk = sb("m_chunk", [P, S])
        cs = sb("cs", [P, TB, 2, 16])
        g_col = sb("g_col", [P, 10])
        g_now = sb("g_now", [P, 2])
        sink = sb("sink", [P, 8])
        eps = sb("eps", [P, 1])
        stat = sb("stat", [P, 5, 16])
        negmax8 = sb("negmax8", [P, TB, 8])
        total8 = sb("total8", [P, TB, 8])
        negmax = sb("negmax", [P, TB, 40])
        total = sb("total", [P, TB, 40])
        rtotal = sb("rtotal", [P, TB, 2])
        comb = sb("comb", [P, 8, TB, 8])
        tabT = sb("tabT", [32, 40])

        flat_bias = bias[:, :, :, :].rearrange("p a b c -> p (a b c)")
        flat_heads = heads[:, :, :, :].rearrange("p a b c -> p (a b c)")
        flat_qkv = qkv[:, :, :, :].rearrange("p a b c -> p (a b c)")
        flat_logit = logit[:, :, :, :].rearrange("p a b c -> p (a b c)")
        u = flat_qkv[:, 0:TB * D].rearrange("p (b c) -> p b c", b=TB)
        merged = u
        hid_e = flat_qkv[:, 0:512].rearrange("p (b c) -> p b c", b=TB)
        hid_g = flat_qkv[:, 512:1024].rearrange("p (b c) -> p b c", b=TB)
        hid = flat_qkv[:, 1024:1536].rearrange("p (b c) -> p b c", b=TB)
        ao = flat_bias[:, 0:TB * D].rearrange("p (b c) -> p b c", b=TB)
        ao_h = ao.rearrange("p b (n d) -> p b n d", d=HD)
        sb_tmp = [flat_bias[:, 2048 + 768 * i:2816 + 768 * i].rearrange("p (j c) -> p j c", j=2) for i in range(3)]
        qkT_odd = flat_bias[:, 4352:6400].rearrange("p (t c) -> p t c", t=4)
        k_rot = flat_bias[:, 6400:6464].rearrange("p (b c) -> p b c", b=TB)
        k_rot2 = flat_bias[:, 6464:6528].rearrange("p (b c) -> p b c", b=TB)
        cq = flat_bias[:, 6528:7296].rearrange("p (b c) -> p b c", b=TB)
        ckv = flat_bias[:, 7296:7808].rearrange("p (b c) -> p b c", b=TB)
        q_mla = flat_heads[:, 0:1536].rearrange("p (b n c) -> p b n c", b=TB, c=MLA_QK)
        k_mla = flat_heads[:, 1536:3072].rearrange("p (b n c) -> p b n c", b=TB, c=MLA_QK)
        v_mla = flat_heads[:, 3072:4096].rearrange("p (b c) -> p b c", b=TB)
        swish = flat_bias[:, 2048:5120].rearrange("p (i b c) -> p i b c", i=3, b=TB)
        branch_out = flat_logit[:, 0:1024].rearrange("p (b c) -> p b c", b=TB)
        cs_t = flat_heads[:, 4096:4608].rearrange("p (i n c) -> p i n c", i=4, c=16)
        m_strict = flat_heads[:, 4608:4864]
        m_keep = flat_heads[:, 4864:5120]
        onehot = flat_heads[0:32, 1792:1792 + REL]
        rel_f = flat_heads[0:40, 0:REL]
        dist_m = flat_heads[0:40, 384:384 + REL]

        acc = [ctx.enter_context(nc.psum_tensor(f"acc{i}", [P, 512], f32)) for i in range(4)]
        pair_ps = ctx.enter_context(nc.psum_tensor("pair_ps", [P, 2, 512], f32))
        turn_ps = ctx.enter_context(nc.psum_tensor("turn_ps", [P, 2, 512], f32))
        qkT_ps, out_ps = acc[2], acc[3]

        x_loaded = sem("x_loaded")
        consts = sem("consts")
        raw_full = [sem(f"raw_full{i}") for i in range(RING)]
        hi_done = sem("hi_done")
        lo_done = sem("lo_done")
        unit_used = sem("unit_used")
        blk0_done = sem("blk0_done")
        acc_read = sem("acc_read")
        turned = sem("turned")
        turned_hi = sem("turned_hi")
        turned_lo = sem("turned_lo")
        squared = sem("squared")
        root = sem("root")
        act_self = sem("act_self")
        dve_self = sem("dve_self")
        h_ready = sem("h_ready")
        u_ready = sem("u_ready")
        gain_full = sem("gain_full")
        gain_used = sem("gain_used")
        summed = sem("summed")
        qk_ready = sem("qk_ready")
        qkT_done = sem("qkT_done")
        qkT_read = sem("qkT_read")
        logit_done = sem("logit_done")
        logit_read = sem("logit_read")
        max_done = sem("max_done")
        prob_done = sem("prob_done")
        sb_abs = sem("sb_abs")
        prT_done = sem("prT_done")
        prT_act = sem("prT_act")
        prT_dve = sem("prT_dve")
        out_done = sem("out_done")
        out_read = sem("out_read")
        proj_done = sem("proj_done")
        eps_set = sem("eps_set")
        root_used = sem("root_used")
        swish_done = sem("swish_done")
        gated = sem("gated")
        gate_exp = sem("gate_exp")
        tab_done = sem("tab_done")
        rel_ready = sem("rel_ready")
        rel_stored = sem("rel_stored")
        band_full = sem("band_full")
        band_ready = sem("band_ready")
        bias_full = [sem(f"bias_full{i}") for i in range(5)]
        comb_d = sem("comb_d")
        comb_a = sem("comb_a")
        stored = sem("stored")

        def since(e, s, v):
            if isinstance(v, int) and v <= 0:
                return
            e.wait_ge(s, v)

        def key_cols(blk):
            return (slice(0, 128), slice(128, 256)) if blk == 0 else (slice(128, 384), slice(0, 256))

        def back(cols):
            return slice(S - cols.stop, S - cols.start)

        block = ctx.enter_context(nc.Block())

        @block.sync
        def _(sp):
            n = Ordinals()
            sp.dma_start(h[:, :, :], x[0].rearrange("(b p) c -> p b c", p=P)).then_inc(x_loaded, 16)

            def load(parts):
                since(sp, lo_done, n.unit - (RING - 1))
                for dst, src in parts:
                    sp.dma_start(dst, src).then_inc(raw_full[n.slot], 32 // len(parts))
                n.next_unit()

            def rows(w, kt0, nkt, cols):
                return w[kt0 * P:(kt0 + nkt) * P, cols].rearrange("(k p) c -> p k c", p=P)

            def view(nkt, width):
                return w_raw[:, n.slot, 0:nkt * width].rearrange("p (k c) -> p k c", k=nkt)

            def chunk_units(w, nkt, cols, width):
                for kt0 in range(0, nkt, 4):
                    m = min(4, nkt - kt0)
                    load([(view(m, width), rows(w, kt0, m, cols))])

            def proj_units(w):
                for kt0 in range(0, KT, 2):
                    load([(view(2, D), rows(w, kt0, 2, slice(0, D)))])

            def step_units(layer, c):
                for kt0 in (0, 4):
                    v = view(4, 2 * FT)
                    load([(v[:, :, 0:FT], rows(w_gate[layer], kt0, 4, bass.ds(c * FT, FT))),
                          (v[:, :, FT:2 * FT], rows(w_up[layer], kt0, 4, bass.ds(c * FT, FT)))])

            def down_unit(layer, c):
                src = w_down[layer][bass.ds(c * FT, FT), :].rearrange("(k p) c -> p k c", p=P)
                load([(view(2, D), src)])

            def swiglu_units(layer):
                step_units(layer, 0)
                step_units(layer, 1)
                down_unit(layer, 0)
                u0 = n.unit
                with sp.Fori(2, NF) as c:
                    n.unit = u0 + (c - 2) * 3
                    step_units(layer, c)
                    down_unit(layer, c - 1)
                n.unit = u0 + 3 * (NF - 2)
                down_unit(layer, NF - 1)

            for i in range(3):
                chunk_units(w_in0, KT, slice(672 + 512 * i, 1184 + 512 * i), 512)
            chunk_units(w_in0, KT, slice(0, 384), 384)
            chunk_units(w_in0, KT, slice(384, 672), 288)
            for i in range(2):
                chunk_units(w_uq, 3, slice(384 * i, 384 * i + 384), 384)
            for i in range(2):
                chunk_units(w_ukv, 2, slice(512 * i, 512 * i + 512), 512)
            proj_units(w_out0)
            swiglu_units(0)
            for g in range(2):
                for i in range(3):
                    chunk_units(w_qkv, KT, slice(1024 * i + 512 * g, 1024 * i + 512 * g + 512), 512)
            proj_units(w_out1)
            swiglu_units(1)
            for i in range(3):
                chunk_units(w_in2, KT, slice(512 * i, 512 * i + 512), 512)
            u0 = n.unit
            with sp.Fori(0, 3) as g:
                n.unit = u0 + g * 6
                for i in range(3):
                    chunk_units(w_in2, KT, bass.ds(g * BR + (2048 + 1536 * i), BR), 512)
            n.unit = u0 + 18
            chunk_units(w_in2, KT, slice(7168, 7680), 512)
            chunk_units(w_in2, KT, slice(7680, 7936), 256)
            for c0 in (1536, 6656, 7936):
                chunk_units(w_in2, KT, slice(c0, c0 + 512), 512)
            for i in range(3):
                for half in range(2):
                    c0 = 8448 + D * i + 512 * half
                    chunk_units(w_in2, KT, slice(c0, c0 + 512), 512)
                    chunk_units(w_branch[i], 4, slice(512 * half, 512 * half + 512), 512)
            proj_units(w_out2)
            sp.wait_ge(h_ready, 12)
            sp.dma_start(out[0].rearrange("(b p) c -> p b c", p=P), h[:, :, :]).then_inc(stored, 16)
            sp.wait_ge(stored, 16)

        @block.gpsimd
        def _(pool):
            def load_gain(n, v):
                since(pool, gain_used, n)
                pool.dma_start(gain[:, 0:v.shape[0]], v.partition_broadcast(P)).then_inc(gain_full, 16)

            pool.memset(eps[:, :], EPS).then_inc(eps_set, 1)
            load_gain(0, g_mix[0])
            for dst, src in ((ident[:, :], identity), (m_strict[:, :], strict_mask), (m_keep[:, :], keep_mask),
                             (m_chunk[:, :], chunk_mask), (cs[:, :, :, :], rope),
                             (onehot[:, :], bucket_onehot), (dist_m, dist_mask),
                             (sink[:, :], sinks.partition_broadcast(P))):
                pool.dma_start(dst, src).then_inc(consts, 16)
            with nc.allow_non_contiguous_dma(reason="small tables, once"):
                pool.dma_start(tabT[:, :], rel_bias2.rearrange("n b -> b n")).then_inc(consts, 16)
                for top in (0, HD):
                    for group, row in enumerate((0, 2, 2, 2, 4)):
                        pool.dma_start(g_col[top:top + HD, 2 * group:2 * group + 2],
                                       qk_g[row:row + 2, :].rearrange("g d -> d g")).then_inc(consts, 16)
            pool.wait_ge(rel_ready, 1)
            pool.dma_start(rel_rows[0:40, :], rel_f).then_inc(rel_stored, 16)

            def windows(rows, first, width, count):
                return bass.AP(rows.tensor, first, [[1, P], [width, count], [1, S]])

            pool.wait_ge(rel_stored, 16)
            load_gain(1, g_cq)
            load_gain(2, g_ckv)
            load_gain(3, g_ffn[0])
            pool.wait_ge(h_ready, 2)
            pool.dma_start(bias[:, 2:4, :, :], windows(rel_band, 256 - (P - 1), 513, 16)).then_inc(band_full, 16)
            pool.wait_ge(band_full, 16)
            band = bias[:, 2:4, :, :].rearrange("p a b c -> p (a b) c")
            pool.tensor_tensor(band, band, m_chunk[:, :].unsqueeze(1).broadcast_to([P, 16, S]),
                               ALU.add).then_inc(band_ready, 1)
            load_gain(4, g_mix[1])
            load_gain(5, g_ffn[1])
            pool.wait_ge(h_ready, 6)
            for g in range(4):
                pool.dma_start(bias[:, g, :, :], windows(rel_rows, 8 * g * REL, REL, 8)).then_inc(bias_full[g], 16)
            load_gain(6, g_final)
            load_gain(7, g_ln2)
            pool.wait_ge(max_done, 20)
            pool.dma_start(bias[:, 0, :, :], windows(rel_rows, 32 * REL, REL, 8)).then_inc(bias_full[4], 16)
            pool.wait_ge(bias_full[4], 16)

        @block.tensor
        def _(pe):
            n = Ordinals()
            mm, transpose = nc.tensor.matmul, nc.tensor.transpose

            def tokens(blk):
                return slice(blk * P, blk * P + P)

            def unit_parts(nkt, width):
                return [w[:, n.slot, 0:nkt * width].rearrange("p (k c) -> p k c", k=nkt) for w in (w_hi, w_lo)]

            def half_unit(o, x_hi, x_lo, kts, parts, blk, first, last):
                wh, wl = parts
                for k, kt in enumerate(kts):
                    xh, xl = x_hi[:, kt, tokens(blk)], x_lo[:, kt, tokens(blk)]
                    mm(o, xh, wh[:, k, :], start=first and k == 0, stop=False)
                    mm(o, xh, wl[:, k, :], start=False, stop=False)
                    done = mm(o, xl, wh[:, k, :], start=False, stop=last and k == len(kts) - 1)
                return done

            def chunk_unit(x_hi, x_lo, kts, width, first, last, between=None):
                pe.wait_ge(lo_done, n.unit + 1)
                parts = unit_parts(len(kts), width)
                for blk in range(TB):
                    if between:
                        between(blk)
                    if first:
                        since(pe, acc_read, n.chunk * 2 + (blk - 1))
                    done = half_unit(acc[blk][:, 0:width], x_hi, x_lo, kts, parts, blk, first, last)
                    if blk == 0 and last:
                        done.then_inc(blk0_done, 1)
                done.then_inc(unit_used, 1)
                n.next_unit()
                if last:
                    n.chunk = n.chunk + 1

            def chunk(x_hi, x_lo, nkt, width, x_kt=0):
                for k0 in range(0, nkt, 4):
                    m = min(4, nkt - k0)
                    chunk_unit(x_hi, x_lo, range(x_kt + k0, x_kt + k0 + m), width, k0 == 0, k0 + m == nkt)

            def proj_unit(kts, first, last):
                pe.wait_ge(lo_done, n.unit + 1)
                wh, wl = unit_parts(2, D)
                for blk in range(TB):
                    for k, kt in enumerate(kts):
                        xh, xl = oT_hi[:, kt, tokens(blk)], oT_lo[:, kt, tokens(blk)]
                        for i, (xp, wp) in enumerate(((xh, wh), (xh, wl), (xl, wh))):
                            for half in range(2):
                                done = mm(acc[2 * blk + half][:, :], xp, wp[:, k, 512 * half:512 * half + 512],
                                          start=first and k == 0 and i == 0, stop=last and k == 1 and i == 2)
                    if blk == 0 and last:
                        done.then_inc(proj_done, 1)
                done.then_inc(unit_used, 1)
                n.next_unit()

            def projection():
                for k0 in range(0, KT, 2):
                    proj_unit((k0, k0 + 1), k0 == 0, k0 + 2 == KT)

            def turn_bank(tile, nkt, j):
                for k in range(nkt):
                    for blk in range(TB):
                        done = transpose(turn_ps[:, j, k * S + blk * P:k * S + blk * P + P], tile(k, blk), ident[:, :])
                done.then_inc(turned, 1)
                n.bank = n.bank + 1

            def turn(tile, nkt):
                for k0 in range(0, nkt, 2):
                    since(pe, turned_lo, n.bank - 1)
                    turn_bank(lambda k, blk: tile(k0 + k, blk), min(2, nkt - k0), n.bank % 2)

            def turn_written(tile, nkt):
                n.written += 1
                pe.wait_ge(u_ready, n.written)
                turn(tile, nkt)
                pe.wait_ge(turned_lo, n.bank)

            def u_tile(k, blk):
                return u[:, blk, P * k:P * k + P]

            def turn_pair(kind, t):
                for j in range(2 if kind == "mla" else 1):
                    since(pe, qkT_read, n.turn)
                    for i in range(4):
                        blk = i % 2
                        src = (q_mla, k_mla)[i // 2][:, blk, 2 * t + j, :] if kind == "mla" else \
                            qkv[:, i // 2, blk, P * t:P * t + P]
                        done = transpose(qkT_ps[0:src.shape[1], P * i:P * i + P], src, ident[:, :])
                    done.then_inc(qkT_done, 1)
                    n.turn = n.turn + 1

            def logits(kind, t, pair0, turn0):
                per = 2 if kind == "mla" else 1
                pe.wait_ge(qkT_read, turn0 + per * (t + 1))
                since(pe, logit_read, pair0 + t)
                for j in range(2):
                    src = (qkT, qkT_odd)[j][0:MLA_QK, t, :] if kind == "mla" else qkT[HD * j:HD * j + HD, t, :]
                    mm(pair_ps[:, j, 0:128], src[:, 0:128], src[:, 256:384], start=True, stop=True)
                    done = mm(pair_ps[:, j, 128:384], src[:, 128:256], src[:, 256:512], start=True, stop=True)
                done.then_inc(logit_done, 1)

            def turn_probs(t, pair0):
                pe.wait_ge(prob_done, pair0 + (t + 1))
                since(pe, prT_act, pair0 + t)
                since(pe, prT_dve, pair0 + t)
                for j in range(2):
                    for i in range(3):
                        done = transpose(turn_ps[:, j, P * i:P * i + P], logit[:, t % 2, j, P * i:P * i + P],
                                         ident[:, :])
                done.then_inc(prT_done, 1)

            def values(kind, t, pair0):
                pe.wait_ge(prT_act, pair0 + (t + 1))
                pe.wait_ge(prT_dve, pair0 + (t + 1))
                since(pe, out_read, pair0 + t)
                for j in range(2):
                    c0 = P * t + HD * j
                    v0, v1 = [(v_mla[:, blk, c0:c0 + HD] if kind == "mla" else qkv[:, 2, blk, c0:c0 + HD])
                              for blk in range(TB)]
                    pr = prT[:, t % 2, j, :]
                    o0, o1 = out_ps[:, HD * j:HD * j + HD], out_ps[:, P + HD * j:P + HD * j + HD]
                    mm(o0, pr[:, 0:128], v0, start=True, stop=True)
                    mm(o1, pr[:, 128:256], v0, start=True, stop=False)
                    done = mm(o1, pr[:, 256:384], v1, start=False, stop=True)
                done.then_inc(out_done, 1)

            def attention_step(kind, s, pair0, turn0):
                if s < 4:
                    logits(kind, s, pair0, turn0)
                if 1 <= s < 5:
                    turn_probs(s - 1, pair0)
                if 2 <= s:
                    values(kind, s - 2, pair0)

            def group_ready(qk, copied):
                pe.wait_ge(qk_ready, qk)
                pe.wait_ge(acc_read, copied)

            def attend(kind):
                pair0, turn0 = n.pair, n.turn
                for s in range(6):
                    if s < 2:
                        turn_pair(kind, 2 * s)
                        turn_pair(kind, 2 * s + 1)
                    attention_step(kind, s, pair0, turn0)
                n.pair = pair0 + 4

            def project(widths):
                for width in widths:
                    chunk(uT_hi, uT_lo, KT, width)

            def project_and_attend(widths, kind):
                pair0, turn0 = n.pair, n.turn
                s = 0
                for width in widths:
                    for k0 in (0, 4):
                        def between(blk, s=s):
                            if s < 2:
                                turn_pair(kind, 2 * s + blk)
                            if s == 5 and blk == 1:
                                attention_step(kind, 5, pair0, turn0)
                        chunk_unit(uT_hi, uT_lo, range(k0, k0 + 4), width, k0 == 0, k0 == 4, between)
                        if s < 5:
                            attention_step(kind, s, pair0, turn0)
                        s += 1
                for s in range(s, 6):
                    attention_step(kind, s, pair0, turn0)
                n.pair = pair0 + 4

            def swiglu():
                n0, b0 = n.written, n.bank

                def step_unit(c, k0):
                    pe.wait_ge(lo_done, n.unit + 1)
                    if k0 == 0:
                        since(pe, u_ready, n0 + c)
                    parts = unit_parts(4, 2 * FT)
                    for blk in range(TB):
                        done = half_unit(pair_ps[:, blk, :], uT_hi, uT_lo, range(k0, k0 + 4), parts, blk,
                                         k0 == 0, k0 == 4)
                    done.then_inc(unit_used, 1)
                    n.next_unit()

                def turn_hidden(c):
                    pe.wait_ge(u_ready, n0 + c + 1)
                    since(pe, turned_lo, b0 + c)
                    turn_bank(lambda k, blk: hid[:, blk, P * k:P * k + P], 2, 0)

                def down(c, first, last):
                    pe.wait_ge(turned_lo, b0 + c + 1)
                    proj_unit((0, 1), first, last)

                def step(c, first):
                    step_unit(c, 0)
                    turn_hidden(c - 1)
                    step_unit(c, 4)
                    down(c - 1, first, False)

                step_unit(0, 0)
                step_unit(0, 4)
                step(1, True)
                u0 = n.unit
                with pe.Fori(2, NF) as c:
                    n.unit = u0 + (c - 2) * 3
                    step(c, False)
                n.unit = u0 + 3 * (NF - 2)
                turn_hidden(NF - 1)
                down(NF - 1, False, True)
                n.written, n.bank = n0 + NF, b0 + NF

            pe.wait_ge(consts, CONSTS)
            mm(acc[2][0:40, 0:REL], tabT[:, :], onehot[:, :], start=True, stop=True).then_inc(tab_done, 1)
            turn_written(u_tile, KT)
            project((512, 512, 512))
            group_ready(0, 6)
            pe.wait_ge(rel_ready, 1)
            project_and_attend((384, 288), "sb")
            turn_written(lambda k, blk: cq[:, blk, P * k:P * k + P], 3)
            turn_written(lambda k, blk: ckv[:, blk, P * k:P * k + P], 2)
            for _ in range(2):
                chunk(oT_hi, oT_lo, 3, 384)
            for _ in range(2):
                chunk(oT_hi, oT_lo, 2, 512, x_kt=3)
            group_ready(1, 18)
            attend("mla")
            pe.wait_ge(out_read, n.pair)
            turn(lambda k, blk: ao[:, blk, P * k:P * k + P], KT)
            pe.wait_ge(turned_lo, n.bank)
            projection()
            turn_written(u_tile, KT)
            swiglu()
            turn_written(u_tile, KT)
            project((512, 512, 512))
            group_ready(1, 24)
            project_and_attend((512, 512, 512), "band")
            group_ready(1, 30)
            attend("band")
            pe.wait_ge(out_read, n.pair)
            turn(lambda k, blk: ao[:, blk, P * k:P * k + P], KT)
            pe.wait_ge(turned_lo, n.bank)
            projection()
            turn_written(u_tile, KT)
            swiglu()
            turn_written(u_tile, KT)
            project((512, 512, 512))
            u0, c0, p0, t0 = n.unit, n.chunk, n.pair, n.turn
            with pe.Fori(0, 3) as g:
                n.unit, n.chunk, n.pair, n.turn = u0 + g * 6, c0 + g * 3, p0 + g * 4, t0 + g * 4
                group_ready(g * 2 + 3, g * 6 + 36)
                project_and_attend((512, 512, 512), "last")
            n.unit, n.chunk, n.pair, n.turn = u0 + 18, c0 + 9, p0 + 12, t0 + 12
            group_ready(9, 54)
            project_and_attend((512, 256), "last")
            group_ready(11, 58)
            project_and_attend((512, 512, 512), "last")
            for i in range(3):
                for half in range(2):
                    chunk(uT_hi, uT_lo, KT, 512)
                    if half == 0:
                        o = heads[:, :, HEAD0[i]:HEAD0[i] + 8, :].rearrange("p b n d -> p b (n d)")
                        turn_written(lambda k, blk: o[:, blk, P * k:P * k + P], 4)
                    chunk(oT_hi, oT_lo, 4, 512, x_kt=4 * (i % 2))
            turn_written(lambda k, blk: merged[:, blk, P * k:P * k + P], KT)
            projection()

        @block.scalar
        def _(act):
            n = Ordinals()
            own = [0]
            activation = nc.scalar.activation

            act.add_instruction(mybir.InstLoadActFuncSet(
                name=nc.get_next_instruction_name(), engine=mybir.EngineType.Activation,
                act_func_set_id=LN_EXP_TABLES, ins=[], outs=[]))

            def link(ins):
                own[0] = own[0] + 1
                ins.then_inc(act_self, 1)
                act.wait_ge(act_self, own[0])

            def round_unit(ahead=2, width=UNIT):
                slot = (n.slot + ahead) % RING
                act.wait_ge(raw_full[slot], raw_target(n, ahead))
                since(act, unit_used, n.unit + ahead - (RING - 1))
                activation(w_hi[:, slot, 0:width], w_raw[:, slot, 0:width], ACT.Copy).then_inc(hi_done, 1)

            def raw_target(n, ahead):
                return n.raw_base + ((n.raw_local + ahead) // RING + 1) * 32

            def slot_step(width=UNIT, ahead_exists=True):
                if ahead_exists:
                    round_unit(2, width)
                n.next_unit()
                n.raw_local += 1

            def at_loop(u0, local0, trips_expr, units):
                n.unit = u0 + trips_expr * units
                n.raw_base, n.raw_local = trips_expr * (32 * units // RING), local0

            n.raw_base, n.raw_local = 0, 0

            def split_banks(dst, kt0, nkt):
                for k0 in range(0, nkt, 2):
                    m = min(2, nkt - k0)
                    act.wait_ge(turned, n.bank + 1)
                    activation(dst[:, kt0 + k0:kt0 + k0 + m, :].rearrange("p k t -> p (k t)"),
                               turn_ps[:, n.bank % 2, 0:m * S], ACT.Copy).then_inc(turned_hi, 1)
                    n.bank = n.bank + 1

            def root_of(width, count):
                link(activation(stat[:, 4, 0:width], stat[:, 0, 0:width], ACT.Ln, bias=eps[:, 0:1], scale=1.0 / count))
                activation(stat[:, 2, 0:width], stat[:, 4, 0:width], ACT.Exp, scale=-0.5).then_inc(root, 1)
                n.roots += 1

            n.roots = 0
            n.squares = 0

            def row_norm(tile, width, h_count=None):
                since(act, root_used, n.roots)
                for blk in range(TB):
                    if h_count is not None:
                        since(act, h_ready, h_count + blk + 1)
                    activation(square_flat[:, 0:width], tile[:, blk, 0:width], ACT.Square,
                               accum_out=stat[:, 0, blk:blk + 1]).then_inc(squared, 1)
                    n.squares += 1
                    act.wait_ge(squared, n.squares)
                root_of(2, width)

            def copy_block(blk, copies):
                if blk == 0:
                    act.wait_ge(blk0_done, n.chunk + 1)
                else:
                    act.wait_ge(unit_used, n.unit)
                for i, (dst, src, func, scale) in enumerate(copies):
                    done = activation(dst, src, func, scale=scale)
                done.then_inc(acc_read, 1)

            def copy_chunk(copies):
                for blk in range(TB):
                    copy_block(blk, copies(blk))
                n.chunk = n.chunk + 1

            def plain(dst, width=512):
                return lambda blk: [(dst(blk), acc[blk][:, 0:width], ACT.Copy, 1.0)]

            def copy_pair(kind, t, pair0, gains=None):
                for j in range(2 if kind == "mla" else 1):
                    act.wait_ge(qkT_done, n.turn + 1)
                    if kind == "mla":
                        activation((qkT, qkT_odd)[j][0:MLA_QK, t, :], qkT_ps[0:MLA_QK, :], ACT.Copy)\
                            .then_inc(qkT_read, 1)
                    elif kind == "last":
                        activation(qkT[:, t, 0:S], qkT_ps[:, 0:S], ACT.Copy, scale=g_now[:, 0:1])
                        activation(qkT[:, t, S:2 * S], qkT_ps[:, S:2 * S], ACT.Copy,
                                   scale=g_now[:, 1:2]).then_inc(qkT_read, 1)
                    else:
                        activation(qkT[:, t, :], qkT_ps[:, :], ACT.Copy).then_inc(qkT_read, 1)
                    n.turn = n.turn + 1

            def soft_plus(t, pair0):
                act.wait_ge(logit_done, pair0 + (t + 1))
                since(act, max_done, pair0 + t)
                z = pair_ps[:, :, 0:384]
                activation(sb_tmp[0], z, ACT.Relu, scale=HD ** -0.5)
                link(activation(sb_tmp[1], z, ACT.Abs, scale=HD ** -0.5))
                link(activation(sb_tmp[1], sb_tmp[1], ACT.Exp, scale=-1.0))
                activation(sb_tmp[1], sb_tmp[1], ACT.Ln, bias=1.0).then_inc(sb_abs, 1)

            def exponentiate(kind, t, pair0, head0):
                act.wait_ge(max_done, pair0 + (t + 1))
                pr = logit[:, t % 2, :, :]
                if kind == "sb":
                    activation(pr, pr, ACT.Exp).then_inc(prob_done, 1)
                    return
                for blk in range(TB):
                    cols = key_cols(blk)[0]
                    for j in range(2):
                        head = slice(2 * t + j, 2 * t + j + 1)
                        done = activation(pr[:, j, cols], pr[:, j, cols], ACT.Exp,
                                          bias=negmax8[:, blk, head], accum_out=total8[:, blk, head])
                done.then_inc(prob_done, 1)

            def copy_probs(t, pair0):
                act.wait_ge(prT_done, pair0 + (t + 1))
                activation(prT[:, t % 2, 0, :], turn_ps[:, 0, 0:384], ACT.Copy).then_inc(prT_act, 1)

            def attention_step(kind, s, pair0, head0):
                if kind == "sb" and s < 4:
                    soft_plus(s, pair0)
                if 1 <= s < 5:
                    exponentiate(kind, s - 1, pair0, head0)
                if 2 <= s:
                    copy_probs(s - 2, pair0)

            def attend(kind, head0=0, gains=None):
                pair0 = n.pair
                for s in range(6):
                    if s < 2:
                        copy_pair(kind, 2 * s, pair0, gains)
                        copy_pair(kind, 2 * s + 1, pair0, gains)
                    attention_step(kind, s, pair0, head0)
                n.pair = pair0 + 4

            def project(chunks, prefetch=(UNIT,) * 6):
                s = 0
                for done in chunks:
                    for _ in range(2):
                        slot_step(prefetch[s])
                        s += 1
                    done()

            def project_and_attend(chunks, kind, head0=0, gains=None, prefetch=(UNIT,) * 6):
                pair0 = n.pair
                if kind == "last":
                    link(activation(g_now[:, :], g_col[:, bass.ds(gains, 2)], ACT.Copy))
                s = 0
                for done in chunks:
                    for last in (False, True):
                        slot_step(prefetch[s])
                        if s < 2:
                            copy_pair(kind, 2 * s, pair0, gains)
                            copy_pair(kind, 2 * s + 1, pair0, gains)
                        attention_step(kind, s, pair0, head0)
                        if last and s < 2 * len(chunks) - 1:
                            done()
                        s += 1
                for s in range(s, 6):
                    attention_step(kind, s, pair0, head0)
                chunks[-1]()
                n.pair = pair0 + 4

            def copy_qkv(i):
                def done():
                    if i < 2:
                        since(act, qkT_done, n.turn)
                    else:
                        since(act, out_done, n.used)
                    copy_chunk(plain(lambda blk: qkv[:, i, blk, :]))
                return done

            def head_norm(i):
                since(act, summed, n.sums)
                act.wait_ge(acc_read, n.chunk * 2)
                activation(square[:, :, :], qkv[:, i, :, :], ACT.Square).then_inc(squared, 1)
                n.squares = n.squares + 1
                n.sums = n.sums + 1
                act.wait_ge(summed, n.sums)
                root_of(16, HD)

            n.sums = 0

            def copy_and_norm(i):
                def done():
                    copy_qkv(i)()
                    head_norm(i)
                return done

            def window_kv():
                since(act, qkT_done, n.turn)
                since(act, out_done, n.used)
                def copies(blk):
                    def four(dst, c0):
                        return (dst.rearrange("p (g r d) -> p g r d", g=2, r=4),
                                acc[blk][:, c0:c0 + 128].rearrange("p (g d) -> p g d", g=2)
                                .unsqueeze(2).broadcast_to([P, 2, 4, HD]), ACT.Copy, 1.0)
                    return [four(qkv[:, 1, blk, :], 0), four(qkv[:, 2, blk, :], 128)]
                copy_chunk(copies)
                head_norm(1)

            def swiglu():
                n0, b0 = n.written, n.bank

                def gate(c):
                    act.wait_ge(unit_used, n.unit)
                    since(act, u_ready, n0 + c)
                    activation(hid_e, pair_ps[:, :, 0:FT], ACT.Exp, scale=-1.0).then_inc(gate_exp, 1)

                def split_hidden(c):
                    act.wait_ge(turned, b0 + c + 1)
                    activation(oT_hi[:, 0:2, :].rearrange("p k t -> p (k t)"), turn_ps[:, 0, :], ACT.Copy)\
                        .then_inc(turned_hi, 1)

                def step(c):
                    slot_step()
                    split_hidden(c - 1)
                    slot_step()
                    gate(c)
                    slot_step()

                slot_step()
                slot_step()
                gate(0)
                step(1)
                u0, local0, base0 = n.unit, n.raw_local, n.raw_base
                with act.Fori(2, NF) as c:
                    n.unit = u0 + (c - 2) * 3
                    n.raw_base, n.raw_local = (c - 2) * 32 + base0, local0
                    step(c)
                trips = NF - 2
                n.unit = u0 + 3 * trips
                n.raw_base, n.raw_local = base0, local0 + 3 * trips
                split_hidden(NF - 1)
                slot_step()
                n.written, n.bank = n0 + NF, b0 + NF

            act.wait_ge(eps_set, 1)
            act.wait_ge(consts, CONSTS)
            round_unit(0)
            round_unit(1)
            act.wait_ge(x_loaded, 16)
            row_norm(h, D)
            n.written += 1
            split_banks(uT_hi, 0, KT)
            n.used = 0
            project([copy_qkv(i) for i in range(3)], (UNIT,) * 4 + (1536, 1536))
            project_and_attend([lambda: copy_chunk(plain(lambda blk: cq[:, blk, :], 384)),
                                lambda: copy_chunk(lambda blk: [
                                    (ckv[:, blk, :], acc[blk][:, 0:256], ACT.Copy, 1.0),
                                    (k_rot[:, blk, :], acc[blk][:, 256:288], ACT.Copy, 1.0)])],
                               "sb", prefetch=(1152, 1152, 1152, 1152))
            row_norm(cq, 384)
            split_banks(oT_hi, 0, 3)
            row_norm(ckv, 256)
            split_banks(oT_hi, 3, 2)
            n.written += 2
            for i in range(2):
                slot_step(1024)
                copy_chunk(lambda blk: [(q_mla[:, blk, 4 * i:4 * i + 4, :].rearrange("p n c -> p (n c)"),
                                         acc[blk][:, 0:384], ACT.Copy, 1.0)])
            for i in range(2):
                slot_step()
                def kv(blk):
                    src = acc[blk][:, :].rearrange("p (n c) -> p n c", c=128)
                    return [(k_mla[:, blk, 4 * i:4 * i + 4, 0:HD], src[:, :, 0:HD], ACT.Copy, 1.0),
                            (v_mla[:, blk, 256 * i:256 * i + 256].rearrange("p (n c) -> p n c", c=HD),
                             src[:, :, HD:128], ACT.Copy, 1.0)]
                copy_chunk(kv)
            attend("mla")
            split_banks(oT_hi, 0, KT)
            for _ in range(4):
                slot_step()
            row_norm(h, D, 0)
            n.written += 1
            split_banks(uT_hi, 0, KT)
            swiglu()
            row_norm(h, D, 2)
            n.written += 1
            split_banks(uT_hi, 0, KT)
            n.used = 8
            project([copy_qkv(i) for i in range(3)])
            n.used = 12
            project_and_attend([copy_qkv(i) for i in range(3)], "band", 0)
            attend("band", 8)
            split_banks(oT_hi, 0, KT)
            for _ in range(4):
                slot_step()
            row_norm(h, D, 4)
            n.written += 1
            split_banks(uT_hi, 0, KT)
            swiglu()
            row_norm(h, D, 6)
            row_norm(h, D, 8)
            n.written += 1
            split_banks(uT_hi, 0, KT)
            n.used = n.pair
            project([copy_and_norm(0), copy_and_norm(1), copy_qkv(2)])
            u0, c0, p0, t0, local0, base0 = n.unit, n.chunk, n.pair, n.turn, n.raw_local, n.raw_base
            own0, s0, q0, r0 = own[0], n.sums, n.squares, n.roots
            with act.Fori(0, 3) as g:
                n.unit, n.chunk, n.pair, n.turn = u0 + g * 6, c0 + g * 3, p0 + g * 4, t0 + g * 4
                n.used = p0 + g * 4 + 4
                n.raw_base, n.raw_local = g * 64 + base0, local0
                own[0], n.sums, n.squares = own0 + g * 3, s0 + g * 2, q0 + g * 2
                project_and_attend([copy_and_norm(0), copy_and_norm(1), copy_qkv(2)], "last", g * 8, g * 2)
            n.unit, n.chunk, n.pair, n.turn = u0 + 18, c0 + 9, p0 + 12, t0 + 12
            n.raw_base, n.raw_local = base0, local0 + 18
            own[0], n.sums, n.squares, n.roots = own0 + 9, s0 + 6, q0 + 6, r0 + 6
            n.used = p0 + 16
            project_and_attend([copy_and_norm(0), window_kv], "last", 24, 6)

            def swish_gate(i):
                def done():
                    if i == 0:
                        act.wait_ge(max_done, 32)
                    since(act, swish_done, i)
                    copy_chunk(lambda blk: [(square[:, blk, :], acc[blk][:, :], ACT.Exp, -1.0),
                                            (swish[:, i, blk, :], acc[blk][:, :], ACT.Copy, 1.0)])
                return done
            project_and_attend([swish_gate(i) for i in range(3)], "last", 32, 8)
            act.wait_ge(comb_d, 1)
            activation(comb[:, 1:4, :, :], comb[:, 1:4, :, :], ACT.Exp)
            activation(comb[:, 5:7, :, :], comb[:, 5:7, :, :], ACT.Exp).then_inc(comb_a, 1)
            for i in range(3):
                for half in range(2):
                    step = 2 * i + half
                    for _ in range(2):
                        slot_step()
                    since(act, swish_done, 3) if step == 0 else act.wait_ge(gated, step)
                    copy_chunk(lambda blk: [(square[:, blk, :], acc[blk][:, :], ACT.Exp, -1.0)])
                    if half == 0:
                        split_banks(oT_hi, 4 * (i % 2), 4)
                    slot_step()
                    copy_chunk(plain(lambda blk: branch_out[:, blk, :]))
            split_banks(oT_hi, 0, KT)
            for left in (4, 3, 2, 1):
                slot_step(ahead_exists=left > 2)

        @block.vector
        def _(dve):
            n = Ordinals()
            own = [0]
            v = nc.vector
            n.roots = n.squares = n.gains = n.h = n.exps = n.chunk = 0

            def link(ins):
                own[0] = own[0] + 1
                ins.then_inc(dve_self, 1)
                dve.wait_ge(dve_self, own[0])

            def split_unit(ahead=2, width=UNIT):
                slot = (n.slot + ahead) % RING
                dve.wait_ge(hi_done, n.unit + (ahead + 1))
                v.tensor_tensor(w_lo[:, slot, 0:width], w_raw[:, slot, 0:width],
                                w_hi[:, slot, 0:width].bitcast(f32), ALU.subtract).then_inc(lo_done, 1)

            def slot_step(width=UNIT, ahead_exists=True):
                if ahead_exists:
                    split_unit(2, width)
                n.next_unit()

            def split_banks(hi, lo, kt0, nkt):
                for k0 in range(0, nkt, 2):
                    m = min(2, nkt - k0)
                    dve.wait_ge(turned_hi, n.bank + 1)
                    a, b = [t[:, kt0 + k0:kt0 + k0 + m, :].rearrange("p k t -> p (k t)") for t in (lo, hi)]
                    v.tensor_tensor(a, turn_ps[:, n.bank % 2, 0:m * S], b.bitcast(f32), ALU.subtract)\
                        .then_inc(turned_lo, 1)
                    n.bank = n.bank + 1

            def sharpen(width, count):
                a, y, t = [stat[:, i, 0:width] for i in (1, 2, 3)]
                link(v.tensor_scalar(a, stat[:, 0, 0:width], 1.0 / count, EPS, ALU.mult, ALU.add))
                n.roots = n.roots + 1
                dve.wait_ge(root, n.roots)
                link(v.scalar_tensor_tensor(t, y, -0.5, y, ALU.mult, ALU.mult))
                link(v.tensor_tensor(t, t, a, ALU.mult))
                link(v.scalar_tensor_tensor(y, t, 1.5, y, ALU.add, ALU.mult))

            def row_norm(src, dst, width, signal, per_blk=False):
                n.squares = n.squares + 2
                dve.wait_ge(squared, n.squares)
                sharpen(2, width)
                n.gains += 1
                dve.wait_ge(gain_full, 16 * n.gains)
                for blk in range(TB):
                    done = v.scalar_tensor_tensor(dst[:, blk, 0:width], src[:, blk, 0:width], stat[:, 2, blk:blk + 1],
                                                  gain[:, 0:width], ALU.mult, ALU.mult)
                    if per_blk or blk == 1:
                        done.then_inc(signal, 1)
                n.h += 2 * per_blk
                n.handed = n.handed + (not per_blk)
                dve.wait_ge(signal, n.h if per_blk else n.handed)
                v.tensor_copy(stat[:, 3, 0:1], stat[:, 2, 0:1]).then_inc(gain_used, 1)
                dve.wait_ge(gain_used, n.gains)
                v.tensor_copy(stat[:, 3, 0:1], stat[:, 2, 0:1]).then_inc(root_used, 1)

            n.handed = 0

            def add_projection():
                n.proj += 1
                for blk in range(TB):
                    if blk == 0:
                        dve.wait_ge(proj_done, n.proj)
                    else:
                        dve.wait_ge(unit_used, n.unit)
                    for half in range(2):
                        c = slice(512 * half, 512 * half + 512)
                        done = v.tensor_tensor(h[:, blk, c], acc[2 * blk + half][:, :], h[:, blk, c], ALU.add)
                    done.then_inc(h_ready, 1)
                n.h += 2

            def maxima(kind, t, pair0, head0, bias_of):
                pr = logit[:, t % 2, :, :]
                dve.wait_ge(logit_done, pair0 + (t + 1))
                if kind != "sb" or True:
                    since(dve, prT_done, pair0 + (t - 1))
                scale = (MLA_QK if kind == "mla" else HD) ** -0.5
                for blk in range(TB):
                    cols, mask_cols = key_cols(blk)
                    done = v.scalar_tensor_tensor(pr[:, :, cols][:, :, ::-1], pair_ps[:, :, cols][:, :, ::-1], scale,
                                                  bias_of(t, mask_cols), ALU.mult, ALU.add)
                done.then_inc(logit_read, 1)
                dve.wait_ge(logit_read, pair0 + (t + 1))
                for blk in range(TB):
                    done = v.tensor_reduce(negmax8[:, blk, 2 * t:2 * t + 2], pr[:, :, key_cols(blk)[0]],
                                           op=ALU.max, axis=AX.X, negate=True)
                done.then_inc(max_done, 1)

            def stick(t, pair0):
                pr = logit[:, t % 2, :, :]
                dve.wait_ge(sb_abs, pair0 + (t + 1))
                since(dve, prT_done, pair0 + (t - 1))
                link(v.tensor_tensor(sb_tmp[0], sb_tmp[0], sb_tmp[1], ALU.add))
                for blk in range(TB):
                    cols, mask_cols = key_cols(blk)
                    for j in range(2):
                        v.tensor_tensor_scan(sb_tmp[2][:, j, cols][:, ::-1], sb_tmp[0][:, j, cols][:, ::-1],
                                             m_keep[:, mask_cols][:, ::-1], 0.0, ALU.add, ALU.mult)
                    done = v.scalar_tensor_tensor(pr[:, :, cols], pair_ps[:, :, cols], HD ** -0.5,
                                                  m_strict[:, mask_cols].unsqueeze(1).broadcast_to(
                                                      [P, 2, mask_cols.stop - mask_cols.start]), ALU.mult, ALU.add)
                done.then_inc(logit_read, 1)
                dve.wait_ge(logit_read, pair0 + (t + 1))
                v.tensor_tensor(pr, pr, sb_tmp[2], ALU.subtract).then_inc(max_done, 1)

            def copy_probs(t, pair0):
                dve.wait_ge(prT_done, pair0 + (t + 1))
                v.tensor_copy(prT[:, t % 2, 1, :], turn_ps[:, 1, 0:384]).then_inc(prT_dve, 1)

            def outputs(kind, t, pair0, head0):
                o = out_ps[:, 0:S].rearrange("p (b n d) -> p b n d", b=TB, n=2)
                dve.wait_ge(out_done, pair0 + (t + 1))
                if kind == "sb":
                    v.tensor_copy(ao_h[:, :, 8 + 2 * t:10 + 2 * t, :], o).then_inc(out_read, 1)
                elif kind == "last":
                    v.tensor_scalar_mul(heads[:, :, bass.ds(head0 + 2 * t, 2), :], o, 1.0).then_inc(out_read, 1)
                    if t == 3:
                        v.tensor_copy(negmax[:, :, bass.ds(head0, 8)], negmax8[:, :, :])
                        v.tensor_copy(total[:, :, bass.ds(head0, 8)], total8[:, :, :])
                else:
                    hs = slice(head0 + 2 * t, head0 + 2 * t + 2)
                    link(v.reciprocal(rtotal[:, :, :], total8[:, :, 2 * t:2 * t + 2]))
                    v.tensor_tensor(ao_h[:, :, hs, :], o, rtotal[:, :, :].unsqueeze(3).broadcast_to([P, TB, 2, HD]),
                                    ALU.mult).then_inc(out_read, 1)

            def attention_step(kind, s, pair0, head0, bias_of):
                if s < 4:
                    if kind == "sb":
                        stick(s, pair0)
                    else:
                        maxima(kind, s, pair0, head0, bias_of)
                if 1 <= s < 5:
                    copy_probs(s - 1, pair0)
                if 2 <= s:
                    outputs(kind, s - 2, pair0, head0)

            def attend(kind, head0=0, bias_of=None):
                for s in range(6):
                    attention_step(kind, s, n.pair, head0, bias_of)
                n.pair = n.pair + 4

            def project(done, prefetch=(UNIT,) * 6):
                for s in range(6):
                    slot_step(prefetch[s])
                    if s in done:
                        done[s]()

            def project_and_attend(units, kind, head0=0, bias_of=None, done={}, prefetch=(UNIT,) * 6):
                for s in range(6):
                    if s < units:
                        slot_step(prefetch[s])
                    attention_step(kind, s, n.pair, head0, bias_of)
                    if s in done:
                        done[s]()
                n.pair = n.pair + 4

            def head_norm(i):
                def run():
                    n.squares = n.squares + 1
                    dve.wait_ge(squared, n.squares)
                    n.sums = n.sums + 1
                    v.tensor_reduce(stat[:, 0, :], square[:, :, :].rearrange("p b (n d) -> p (b n) d", d=HD),
                                    op=ALU.add, axis=AX.X).then_inc(summed, 1)
                    dve.wait_ge(summed, n.sums)
                    sharpen(16, HD)
                    q = qkv[:, i, :, :].rearrange("p b (n d) -> p (b n) d", d=HD)
                    v.tensor_tensor(q, q, stat[:, 2, :].unsqueeze(2).broadcast_to([P, 16, HD]), ALU.mult)\
                        .then_inc(qk_ready, 1)
                    n.qk = n.qk + 1
                    dve.wait_ge(qk_ready, n.qk)
                return run

            n.sums, n.qk = 0, 0

            def rotate(x, y, heads_n, blk):
                t = [cs_t[:, i, 0:heads_n, :] for i in range(4)]
                c, s = [cs[:, blk, i, :].unsqueeze(1).broadcast_to([P, heads_n, 16]) for i in range(2)]
                x1, x2 = x[:, :, 0:16], x[:, :, 16:32]
                v.tensor_tensor(t[0], x1, c, ALU.mult)
                v.tensor_tensor(t[1], x2, s, ALU.mult)
                v.tensor_tensor(t[2], x2, c, ALU.mult)
                link(v.tensor_tensor(t[3], x1, s, ALU.mult))
                v.tensor_tensor(y[:, :, 0:16], t[0], t[1], ALU.subtract)
                link(v.tensor_tensor(y[:, :, 16:32], t[2], t[3], ALU.add))

            def swiglu():
                n0, b0, e0 = n.handed, n.bank, n.exps
                gate_ps, up_ps = pair_ps[:, :, 0:FT], pair_ps[:, :, FT:2 * FT]

                def gate(c):
                    dve.wait_ge(gate_exp, e0 + c + 1)
                    link(v.tensor_scalar_add(hid_e, hid_e, 1.0))
                    link(v.reciprocal(hid_e, hid_e))
                    link(v.tensor_tensor(hid_g, gate_ps, hid_e, ALU.mult))
                    since(dve, turned, b0 + c)
                    v.tensor_tensor(hid, up_ps, hid_g, ALU.mult).then_inc(u_ready, 1)

                def split_hidden(c):
                    dve.wait_ge(turned_hi, b0 + c + 1)
                    lo, hi = [t[:, 0:2, :].rearrange("p k t -> p (k t)") for t in (oT_lo, oT_hi)]
                    v.tensor_tensor(lo, turn_ps[:, 0, :], hi.bitcast(f32), ALU.subtract).then_inc(turned_lo, 1)

                def step(c):
                    slot_step()
                    split_hidden(c - 1)
                    slot_step()
                    gate(c)
                    slot_step()

                slot_step()
                slot_step()
                gate(0)
                step(1)
                u0, own0 = n.unit, own[0]
                with dve.Fori(2, NF) as c:
                    n.unit = u0 + (c - 2) * 3
                    own[0] = own0 + (c - 2) * 3
                    step(c)
                n.unit, own[0] = u0 + 3 * (NF - 2), own0 + 3 * (NF - 2)
                split_hidden(NF - 1)
                slot_step()
                n.handed, n.bank, n.exps = n0 + NF, b0 + NF, e0 + NF

            dve.wait_ge(consts, CONSTS)
            dve.wait_ge(tab_done, 1)
            v.tensor_tensor(rel_f, acc[2][0:40, 0:REL], dist_m, ALU.add).then_inc(rel_ready, 1)
            split_unit(0)
            split_unit(1)
            row_norm(h, u, D, u_ready)
            split_banks(uT_hi, uT_lo, 0, KT)
            project({}, (UNIT,) * 4 + (1536, 1536))
            project_and_attend(4, "sb", prefetch=(1152, 1152, 1152, 1152))
            dve.wait_ge(acc_read, 10)
            row_norm(cq, cq, 384, u_ready)
            split_banks(oT_hi, oT_lo, 0, 3)
            row_norm(ckv, ckv, 256, u_ready)
            split_banks(oT_hi, oT_lo, 3, 2)
            for width in (1024, 1024, UNIT, UNIT):
                slot_step(width)
            for blk in range(TB):
                rotate(k_rot[:, blk, :].unsqueeze(1), k_rot2[:, blk, :].unsqueeze(1), 1, blk)
            dve.wait_ge(acc_read, 18)
            for blk in range(TB):
                v.tensor_copy(k_mla[:, blk, :, HD:MLA_QK], k_rot2[:, blk, :].unsqueeze(1).broadcast_to([P, 8, 32]))
                q_rot = q_mla[:, blk, :, HD:MLA_QK]
                rotate(q_rot, q_rot, 8, blk)
            v.tensor_copy(stat[:, 3, 0:1], stat[:, 2, 0:1]).then_inc(qk_ready, 1)
            n.qk = 1
            mask = lambda t, cols: m_chunk[:, back(cols)].unsqueeze(1).broadcast_to(
                [P, 2, cols.stop - cols.start])
            attend("mla", 0, mask)
            split_banks(oT_hi, oT_lo, 0, KT)
            for _ in range(4):
                slot_step()
            add_projection()
            row_norm(h, u, D, u_ready)
            split_banks(uT_hi, uT_lo, 0, KT)
            swiglu()
            add_projection()
            row_norm(h, u, D, u_ready)
            split_banks(uT_hi, uT_lo, 0, KT)
            project({})
            dve.wait_ge(band_ready, 1)
            def table(slot):
                return lambda t, cols: bias[:, slot, 2 * t:2 * t + 2, back(cols)]
            project_and_attend(6, "band", 0, table(2))
            attend("band", 8, table(3))
            split_banks(oT_hi, oT_lo, 0, KT)
            for _ in range(4):
                slot_step()
            add_projection()
            row_norm(h, u, D, u_ready)
            split_banks(uT_hi, uT_lo, 0, KT)
            swiglu()
            add_projection()
            row_norm(h, h, D, h_ready, per_blk=True)
            row_norm(h, u, D, u_ready)
            split_banks(uT_hi, uT_lo, 0, KT)
            project({1: head_norm(0), 3: head_norm(1)})
            for g in range(4):
                dve.wait_ge(bias_full[g], 16)
            u0, p0, own0, s0, q0, r0, k0 = n.unit, n.pair, own[0], n.sums, n.squares, n.roots, n.qk
            with dve.Fori(0, 3) as g:
                n.unit, n.pair, own[0] = u0 + g * 6, p0 + g * 4, own0 + g * 8
                n.sums, n.squares, n.roots, n.qk = s0 + g * 2, q0 + g * 2, r0 + g * 2, k0 + g * 2
                def table_g(t, cols):
                    return flat_bias[:, bass.ds(g * 2048 + (2 * t * S), 2 * S)]\
                        .rearrange("p (j c) -> p j c", j=2)[:, :, back(cols)]
                project_and_attend(6, "last", g * 8, table_g, {1: head_norm(0), 3: head_norm(1)})
            n.unit, n.pair, own[0] = u0 + 18, p0 + 12, own0 + 24
            n.sums, n.squares, n.roots, n.qk = s0 + 6, q0 + 6, r0 + 6, k0 + 6
            project_and_attend(4, "last", 24, table(3), {1: head_norm(0), 5: head_norm(1)},
                               prefetch=(1024, 1024, UNIT, UNIT))

            def swish_gate(i):
                def run():
                    dve.wait_ge(acc_read, 60 + 2 * i)
                    link(v.tensor_scalar_add(square[:, :, :], square[:, :, :], 1.0))
                    link(v.reciprocal(square[:, :, :], square[:, :, :]))
                    v.tensor_tensor(swish[:, i, :, :], swish[:, i, :, :], square[:, :, :], ALU.mult)\
                        .then_inc(swish_done, 1)
                return run
            dve.wait_ge(bias_full[4], 16)
            project_and_attend(6, "last", 32, table(0), {1: swish_gate(0), 3: swish_gate(1), 5: swish_gate(2)})
            dve.wait_ge(swish_done, 3)

            def nm(group):
                return negmax[:, :, 8 * group:8 * group + 8]

            def tot(group):
                return total[:, :, 8 * group:8 * group + 8]

            cb = [comb[:, i, :, :] for i in range(8)]
            sinks_b = sink[:, :].unsqueeze(1).broadcast_to([P, TB, 8])
            link(v.tensor_tensor(cb[0], nm(1), nm(2), ALU.min))
            link(v.tensor_tensor(cb[0], cb[0], nm(3), ALU.min))
            for g in (1, 2, 3):
                v.tensor_tensor(cb[g], cb[0], nm(g), ALU.subtract)
            link(v.scalar_tensor_tensor(cb[4], sinks_b, -1.0, nm(4), ALU.mult, ALU.min))
            v.tensor_tensor(cb[5], cb[4], nm(4), ALU.subtract)
            v.tensor_tensor(cb[6], sinks_b, cb[4], ALU.add).then_inc(comb_d, 1)
            dve.wait_ge(comb_a, 1)
            link(v.reciprocal(cb[7], tot(0)))

            def eight(group):
                return heads[:, :, 8 * group:8 * group + 8, :]

            def scaled(group, factor):
                link(v.tensor_tensor(eight(group), eight(group), factor.unsqueeze(3).broadcast_to([P, TB, 8, HD]),
                                     ALU.mult))

            def gate_branch(i, group):
                o = eight(group).rearrange("p b n d -> p b (n d)")
                v.tensor_tensor(o, o, swish[:, i, :, :], ALU.mult).then_inc(u_ready, 1)
                n.handed += 1

            scaled(0, cb[7])
            gate_branch(0, 0)
            link(v.tensor_tensor(cb[0], cb[1], tot(1), ALU.mult))
            for g in (2, 3):
                link(v.tensor_tensor(cb[7], cb[g], tot(g), ALU.mult))
                link(v.tensor_tensor(cb[0], cb[0], cb[7], ALU.add))
            link(v.reciprocal(cb[0], cb[0]))
            for g in (1, 2, 3):
                link(v.tensor_tensor(cb[g], cb[g], cb[0], ALU.mult))
                scaled(g, cb[g])
                if g > 1:
                    link(v.tensor_tensor(eight(1), eight(1), eight(g), ALU.add))
            gate_branch(1, 1)
            link(v.tensor_tensor(cb[4], cb[5], tot(4), ALU.mult))
            link(v.tensor_tensor(cb[4], cb[4], cb[6], ALU.add))
            link(v.reciprocal(cb[4], cb[4]))
            link(v.tensor_tensor(cb[5], cb[5], cb[4], ALU.mult))
            scaled(4, cb[5])
            gate_branch(2, 4)
            for i in range(3):
                for half in range(2):
                    step = 2 * i + half
                    for _ in range(2):
                        slot_step()
                    dve.wait_ge(acc_read, 66 + 4 * step)
                    link(v.tensor_scalar_add(square[:, :, :], square[:, :, :], 1.0))
                    link(v.reciprocal(square[:, :, :], square[:, :, :]))
                    if half == 0:
                        split_banks(oT_hi, oT_lo, 4 * (i % 2), 4)
                    slot_step()
                    dve.wait_ge(acc_read, 68 + 4 * step)
                    m = merged[:, :, 512 * half:512 * half + 512]
                    if i == 0:
                        v.tensor_tensor(m, square[:, :, :], branch_out, ALU.mult).then_inc(gated, 1)
                    else:
                        link(v.tensor_tensor(branch_out, square[:, :, :], branch_out, ALU.mult))
                        v.tensor_tensor(m, m, branch_out, ALU.add).then_inc(gated, 1)
            dve.wait_ge(gated, 6)
            v.tensor_copy(stat[:, 3, 0:1], stat[:, 2, 0:1]).then_inc(u_ready, 1)
            n.handed += 1
            split_banks(oT_hi, oT_lo, 0, KT)
            for left in (4, 3, 2, 1):
                slot_step(ahead_exists=left > 2)
            add_projection()


def shape_constants():
    f = np.float32
    p, j = np.arange(P)[:, None], np.arange(S)[None, :]
    strict = np.where(j < P + p, 0.0, MASKED).astype(f)
    keep = (j < P + p).astype(f)
    chunk = np.where(j // 64 <= (P + p) // 64, 0.0, MASKED).astype(f)
    inv_freq = (np.float32(10000.0) ** (-np.arange(0, 32, 2, dtype=f) / np.float32(32))).astype(f)
    ang = (np.arange(S, dtype=f)[:, None] * inv_freq[None, :]).astype(f)
    rope = np.stack([np.cos(ang), np.sin(ang)], 1).astype(f)
    rope = np.ascontiguousarray(rope.reshape(TB, P, 2, 16).transpose(1, 0, 2, 3))
    dist = np.arange(REL) - (P - 1)
    d0 = np.maximum(dist, 0)
    ratio = np.log(np.maximum(d0, 1).astype(f) / f(16)) / f(math.log(2048 / 16))
    large = np.minimum(16 + (ratio * f(16)).astype(np.int32), 31)
    bucket = np.where(d0 < 16, d0, large)
    onehot = (bucket[None, :] == np.arange(32)[:, None]).astype(f)
    ok = [dist >= 0] + [(dist >= 0) & (dist <= w) & (dist % d == 0) for w, d in ((128, 1), (512, 4), (2048, 16))] \
        + [(dist >= 0) & (dist < 128)]
    dist_mask = np.repeat(np.where(np.stack(ok), 0.0, MASKED).astype(f), 8, axis=0)
    return dict(identity=np.eye(P, dtype=f), strict_mask=strict, chunk_mask=np.ascontiguousarray(chunk[:, ::-1]), keep_mask=keep, rope=rope,
                bucket_onehot=onehot, dist_mask=dist_mask)


def kernel(**inputs):
    import numpy as np
    import concourse.bacc as bacc
    from concourse import mybir
    from concourse.bass_utils import run_bass_kernel_spmd

    first = {"w_in0": "ev_w_in", "g_cq": "ev_g_cq", "w_uq": "ev_w_uq", "g_ckv": "ev_g_ckv", "w_ukv": "ev_w_ukv",
             "w_out0": "ev_w_out", "w_qkv": "od_w_qkv", "rel_band": "od_rel_bias", "w_out1": "od_w_out",
             "g_ln2": "ln_g_2", "w_in2": "w_in_2", "qk_g": "qk_g_2", "sinks": "sinks_2", "w_branch": "w_branch_2",
             "w_out2": "w_out_2"}
    plain = {"x": "x", "g_mix": "g_mix", "g_ffn": "g_ffn", "w_gate": "w_gate", "w_up": "w_up", "w_down": "w_down",
             "g_final": "g_final", "rel_bias2": "rel_bias_2"}
    arrays = {k: np.ascontiguousarray(inputs[v])[0] for k, v in first.items()}
    arrays.update({k: np.ascontiguousarray(inputs[v]) for k, v in plain.items()})
    arrays.update(shape_constants())

    nc = bacc.Bacc("TRN2", target_bir_lowering=False, num_devices=1)
    aps = {k: nc.dram_tensor(f"in_{k}", a.shape, mybir.dt.from_np(a.dtype), kind="ExternalInput").ap()
           for k, a in arrays.items()}
    out = nc.dram_tensor("out_y", (1, S, D), mybir.dt.float32, kind="ExternalOutput").ap()
    build_program(nc, out=out, **aps)
    r = run_bass_kernel_spmd(nc, [{f"in_{k}": a for k, a in arrays.items()}], core_ids=[0])
    return r.results[0]["out_y"]
```

```python
import math
from contextlib import ExitStack

import numpy as np

import concourse.bass as bass
from concourse import mybir

P = 128
TB = 2
S = TB * P
D = 1024
KT = D // P
FF = 2816
FT = 256
NF = FF // FT
UNIT = 2048
RING = 3
HD = 64
MLA_QK = 96
BR = 512
REL = 383
MASKED = -1e30
EPS = 1e-6
HEAD0 = (0, 8, 32)
MIX0, CQ, CKV, FFN0, MIX1, FFN1, FINAL, LN2 = range(8)
GAIN_COL = {MIX0: 0, MIX1: 8, FFN0: 16, FFN1: 24, LN2: 32, CQ: 40, CKV: 43}
QK_COL = 45
GAIN_ROWS = QK_COL + 6
TABLES = 9 * 16
CONSTS = 7 * 16
LN_EXP_TABLES = 6


class Ordinals:

    def __init__(self):
        self.unit = 0
        self.slot = 0
        self.chunk = 0
        self.pair = 0
        self.turn = 0
        self.bank = 0
        self.proj = 0
        self.written = 0

    def next_unit(self):
        self.unit = self.unit + 1
        self.slot = (self.slot + 1) % RING


def build_program(nc, x, w_in0, g_cq, w_uq, g_ckv, w_ukv, w_out0, w_qkv, rel_band, w_out1, g_mix, g_ffn,
                  w_gate, w_up, w_down, g_final, g_ln2, w_in2, qk_g, sinks, w_branch, w_out2, rel_bias2,
                  identity, strict_mask, chunk_mask, keep_mask, rope, bucket_onehot, dist_mask, out):
    f32, f32r = mybir.dt.float32, mybir.dt.float32r
    ALU, ACT, AX = mybir.AluOpType, mybir.ActivationFunctionType, mybir.AxisListType

    rel_rows = nc.dram_tensor("rel_rows", [40, REL], f32, kind="Internal").ap()

    ctx = ExitStack()
    with ctx:
        def sb(name, shape, dt=f32):
            return ctx.enter_context(nc.sbuf_tensor(name, shape, dt))

        def sem(name):
            return ctx.enter_context(nc.semaphore(name))

        h = sb("h", [P, TB, D])
        uT_hi = sb("uT_hi", [P, KT, S], f32r)
        uT_lo = sb("uT_lo", [P, KT, S], f32r)
        oT_hi = sb("oT_hi", [P, KT, S], f32r)
        oT_lo = sb("oT_lo", [P, KT, S], f32r)
        w_raw = sb("w_raw", [P, RING, UNIT])
        w_hi = sb("w_hi", [P, RING, UNIT], f32r)
        w_lo = sb("w_lo", [P, RING, UNIT], f32r)
        bias = sb("bias", [P, 4, 8, S])
        qkv = sb("qkv", [P, 3, TB, BR])
        qkT = sb("qkT", [P, 4, 512])
        logit = sb("logit", [P, 2, 2, 384])
        prT = sb("prT", [P, 2, 2, 384])
        heads = sb("heads", [P, TB, 40, HD])
        square = sb("square", [P, TB, BR])
        square_flat = square[:, :, :].rearrange("p b c -> p (b c)")
        ident = sb("ident", [P, P])
        m_chunk = sb("m_chunk", [P, S])
        cs = sb("cs", [P, TB, 2, 16])
        g_col = sb("g_col", [P, 10])
        g_now = sb("g_now", [P, 2])
        gain_T = sb("gain_T", [P, GAIN_ROWS])
        norms = sb("norms", [P, 8, 8, TB])
        sink = sb("sink", [P, 8])
        eps = sb("eps", [P, 1])
        stat = sb("stat", [P, 5, 16])
        negmax8 = sb("negmax8", [P, TB, 8])
        total8 = sb("total8", [P, TB, 8])
        negmax = sb("negmax", [P, TB, 40])
        total = sb("total", [P, TB, 40])
        rtotal = sb("rtotal", [P, TB, 2])
        comb = sb("comb", [P, 8, TB, 8])
        tabT = sb("tabT", [32, 40])

        flat_bias = bias[:, :, :, :].rearrange("p a b c -> p (a b c)")
        flat_heads = heads[:, :, :, :].rearrange("p a b c -> p (a b c)")
        flat_qkv = qkv[:, :, :, :].rearrange("p a b c -> p (a b c)")
        flat_logit = logit[:, :, :, :].rearrange("p a b c -> p (a b c)")
        u = flat_qkv[:, 0:TB * D].rearrange("p (b c) -> p b c", b=TB)
        merged = u
        gain = flat_qkv[:, 2048:3072]
        hid_e = flat_qkv[:, 0:512].rearrange("p (b c) -> p b c", b=TB)
        hid_g = flat_qkv[:, 512:1024].rearrange("p (b c) -> p b c", b=TB)
        hid = flat_qkv[:, 1024:1536].rearrange("p (b c) -> p b c", b=TB)
        ao = flat_bias[:, 0:TB * D].rearrange("p (b c) -> p b c", b=TB)
        ao_h = ao.rearrange("p b (n d) -> p b n d", d=HD)
        sb_tmp = [flat_bias[:, 2048 + 768 * i:2816 + 768 * i].rearrange("p (j c) -> p j c", j=2) for i in range(3)]
        qkT_odd = flat_bias[:, 4352:6400].rearrange("p (t c) -> p t c", t=4)
        k_rot = flat_bias[:, 6400:6464].rearrange("p (b c) -> p b c", b=TB)
        k_rot2 = flat_bias[:, 6464:6528].rearrange("p (b c) -> p b c", b=TB)
        cq = flat_bias[:, 6528:7296].rearrange("p (b c) -> p b c", b=TB)
        ckv = flat_bias[:, 7296:7808].rearrange("p (b c) -> p b c", b=TB)
        q_mla = flat_heads[:, 0:1536].rearrange("p (b n c) -> p b n c", b=TB, c=MLA_QK)
        k_mla = flat_heads[:, 1536:3072].rearrange("p (b n c) -> p b n c", b=TB, c=MLA_QK)
        v_mla = flat_heads[:, 3072:4096].rearrange("p (b c) -> p b c", b=TB)
        swish = flat_bias[:, 2048:5120].rearrange("p (i b c) -> p i b c", i=3, b=TB)
        branch_out = flat_logit[:, 0:1024].rearrange("p (b c) -> p b c", b=TB)
        gain_rows = flat_logit[0:GAIN_ROWS, 0:P]
        tab = flat_logit[0:40, P:P + 32]
        cs_t = flat_heads[:, 4096:4608].rearrange("p (i n c) -> p i n c", i=4, c=16)
        m_strict = flat_heads[:, 4608:4864]
        m_keep = flat_heads[:, 4864:5120]
        onehot = flat_heads[0:32, 1792:1792 + REL]
        rel_f = flat_heads[0:40, 0:REL]
        dist_m = flat_heads[0:40, 384:384 + REL]

        acc = [ctx.enter_context(nc.psum_tensor(f"acc{i}", [P, 512], f32)) for i in range(4)]
        pair_ps = ctx.enter_context(nc.psum_tensor("pair_ps", [P, 2, 512], f32))
        turn_ps = ctx.enter_context(nc.psum_tensor("turn_ps", [P, 2, 512], f32))
        qkT_ps, out_ps = acc[2], acc[3]
        turn_banks = [turn_ps[:, 0, :], turn_ps[:, 1, :]]
        pair_banks = [pair_ps[:, 0, :], pair_ps[:, 1, :]]
        acc_banks = [acc[0][:, :], acc[1][:, :]]
        stream_banks = {norm: turn_banks + (acc_banks if norm in (FFN0, FFN1) else pair_banks)
                        for norm in (MIX0, FFN0, MIX1, FFN1, LN2)}
        latent_banks = [acc[2][:, :]] + pair_banks

        x_loaded = sem("x_loaded")
        tables = sem("tables")
        tables_T = sem("tables_T")
        gains_set = sem("gains_set")
        consts = sem("consts")
        row_scale = sem("row_scale")
        raw_full = [sem(f"raw_full{i}") for i in range(RING)]
        hi_done = sem("hi_done")
        lo_done = sem("lo_done")
        unit_used = sem("unit_used")
        blk0_done = sem("blk0_done")
        acc_read = sem("acc_read")
        turned = sem("turned")
        turned_hi = sem("turned_hi")
        turned_lo = sem("turned_lo")
        squared = sem("squared")
        root = sem("root")
        act_self = sem("act_self")
        dve_self = sem("dve_self")
        h_ready = sem("h_ready")
        u_ready = sem("u_ready")
        gain_full = sem("gain_full")
        summed = sem("summed")
        qk_ready = sem("qk_ready")
        qkT_done = sem("qkT_done")
        qkT_read = sem("qkT_read")
        logit_done = sem("logit_done")
        logit_read = sem("logit_read")
        max_done = sem("max_done")
        prob_done = sem("prob_done")
        sb_abs = sem("sb_abs")
        prT_done = sem("prT_done")
        prT_act = sem("prT_act")
        prT_dve = sem("prT_dve")
        out_done = sem("out_done")
        out_read = sem("out_read")
        proj_done = sem("proj_done")
        eps_set = sem("eps_set")
        swish_done = sem("swish_done")
        gated = sem("gated")
        gate_exp = sem("gate_exp")
        tab_done = sem("tab_done")
        rel_ready = sem("rel_ready")
        rel_stored = sem("rel_stored")
        band_full = sem("band_full")
        band_ready = sem("band_ready")
        bias_full = [sem(f"bias_full{i}") for i in range(5)]
        comb_d = sem("comb_d")
        comb_a = sem("comb_a")
        stored = sem("stored")

        def since(e, s, v):
            if isinstance(v, int) and v <= 0:
                return
            e.wait_ge(s, v)

        def key_cols(blk):
            return (slice(0, 128), slice(128, 256)) if blk == 0 else (slice(128, 384), slice(0, 256))

        def back(cols):
            return slice(S - cols.stop, S - cols.start)

        block = ctx.enter_context(nc.Block())

        @block.sync
        def _(sp):
            n = Ordinals()
            for blk in range(TB):
                sp.dma_start(h[:, blk, :], x[0].rearrange("(b p) c -> p b c", p=P)[:, blk, :]).then_inc(x_loaded, 16)

            def load(parts):
                since(sp, lo_done, n.unit - (RING - 1))
                for dst, src in parts:
                    sp.dma_start(dst, src).then_inc(raw_full[n.slot], 32 // len(parts))
                n.next_unit()

            def rows(w, kt0, nkt, cols):
                return w[kt0 * P:(kt0 + nkt) * P, cols].rearrange("(k p) c -> p k c", p=P)

            def view(nkt, width):
                return w_raw[:, n.slot, 0:nkt * width].rearrange("p (k c) -> p k c", k=nkt)

            def chunk_units(w, nkt, cols, width):
                for kt0 in range(0, nkt, 4):
                    m = min(4, nkt - kt0)
                    load([(view(m, width), rows(w, kt0, m, cols))])

            def proj_units(w, order=(0, 2, 4, 6)):
                for kt0 in order:
                    load([(view(2, D), rows(w, kt0, 2, slice(0, D)))])

            def step_units(layer, c):
                for kt0 in (0, 4):
                    v = view(4, 2 * FT)
                    load([(v[:, :, 0:FT], rows(w_gate[layer], kt0, 4, bass.ds(c * FT, FT))),
                          (v[:, :, FT:2 * FT], rows(w_up[layer], kt0, 4, bass.ds(c * FT, FT)))])

            def down_unit(layer, c):
                src = w_down[layer][bass.ds(c * FT, FT), :].rearrange("(k p) c -> p k c", p=P)
                load([(view(2, D), src)])

            def swiglu_units(layer):
                step_units(layer, 0)
                step_units(layer, 1)
                down_unit(layer, 0)
                u0 = n.unit
                with sp.Fori(2, NF) as c:
                    n.unit = u0 + (c - 2) * 3
                    step_units(layer, c)
                    down_unit(layer, c - 1)
                n.unit = u0 + 3 * (NF - 2)
                down_unit(layer, NF - 1)

            for i in range(3):
                chunk_units(w_in0, KT, slice(672 + 512 * i, 1184 + 512 * i), 512)
            chunk_units(w_in0, KT, slice(0, 384), 384)
            chunk_units(w_in0, KT, slice(384, 672), 288)
            for i in range(2):
                chunk_units(w_uq, 3, slice(384 * i, 384 * i + 384), 384)
            for i in range(2):
                chunk_units(w_ukv, 2, slice(512 * i, 512 * i + 512), 512)
            proj_units(w_out0, (4, 6, 0, 2))
            swiglu_units(0)
            for g in range(2):
                for i in range(3):
                    chunk_units(w_qkv, KT, slice(1024 * i + 512 * g, 1024 * i + 512 * g + 512), 512)
            proj_units(w_out1)
            swiglu_units(1)
            for i in range(3):
                chunk_units(w_in2, KT, slice(512 * i, 512 * i + 512), 512)
            u0 = n.unit
            with sp.Fori(0, 3) as g:
                n.unit = u0 + g * 6
                for i in range(3):
                    chunk_units(w_in2, KT, bass.ds(g * BR + (2048 + 1536 * i), BR), 512)
            n.unit = u0 + 18
            chunk_units(w_in2, KT, slice(7168, 7680), 512)
            chunk_units(w_in2, KT, slice(7680, 7936), 256)
            for c0 in (1536, 6656, 7936):
                chunk_units(w_in2, KT, slice(c0, c0 + 512), 512)
            for i in range(3):
                for half in range(2):
                    c0 = 8448 + D * i + 512 * half
                    chunk_units(w_in2, KT, slice(c0, c0 + 512), 512)
                    chunk_units(w_branch[i], 4, slice(512 * half, 512 * half + 512), 512)
            proj_units(w_out2)
            for blk in range(TB):
                sp.wait_ge(h_ready, 11 + blk)
                sp.dma_start(out[0].rearrange("(b p) c -> p b c", p=P)[:, blk, :], h[:, blk, :]).then_inc(stored, 16)
            sp.wait_ge(stored, 16 * TB)

        @block.gpsimd
        def _(pool):
            pool.memset(eps[:, :], EPS).then_inc(eps_set, 1)
            for dst, src in ((onehot[:, :], bucket_onehot), (dist_m, dist_mask),
                             (m_strict[:, :], strict_mask), (m_keep[:, :], keep_mask),
                             (m_chunk[:, :], chunk_mask), (cs[:, :, :, :], rope),
                             (sink[:, :], sinks.partition_broadcast(P))):
                pool.dma_start(dst, src).then_inc(consts, 16)
            pool.wait_ge(rel_ready, 1)
            pool.dma_start(rel_rows[0:40, :], rel_f).then_inc(rel_stored, 16)

            def windows(rows, first, width, count):
                return bass.AP(rows.tensor, first, [[1, P], [width, count], [1, S]])

            pool.wait_ge(h_ready, 2)
            pool.dma_start(bias[:, 2:4, :, :], windows(rel_band, 256 - (P - 1), 513, 16)).then_inc(band_full, 16)
            pool.wait_ge(band_full, 16)
            band = bias[:, 2:4, :, :].rearrange("p a b c -> p (a b) c")
            pool.tensor_tensor(band, band, m_chunk[:, :].unsqueeze(1).broadcast_to([P, 16, S]),
                               ALU.add).then_inc(band_ready, 1)
            pool.wait_ge(rel_stored, 16)
            pool.wait_ge(h_ready, 6)
            pool.dma_start(gain, g_final.partition_broadcast(P)).then_inc(gain_full, 16)
            for g in range(4):
                pool.dma_start(bias[:, g, :, :], windows(rel_rows, 8 * g * REL, REL, 8)).then_inc(bias_full[g], 16)
            pool.wait_ge(max_done, 20)
            pool.dma_start(bias[:, 0, :, :], windows(rel_rows, 32 * REL, REL, 8)).then_inc(bias_full[4], 16)
            pool.wait_ge(bias_full[4], 16)

        @block.tensor
        def _(pe):
            n = Ordinals()
            n.h, n.fresh = 0, None
            mm, transpose = nc.tensor.matmul, nc.tensor.transpose

            def tokens(blk):
                return slice(blk * P, blk * P + P)

            def unit_parts(nkt, width):
                return [w[:, n.slot, 0:nkt * width].rearrange("p (k c) -> p k c", k=nkt) for w in (w_hi, w_lo)]

            def half_unit(o, x_hi, x_lo, kts, parts, blk, first, last):
                wh, wl = parts
                for k, kt in enumerate(kts):
                    if n.fresh is not None and blk == 0 and kt % 2 == 0:
                        pe.wait_ge(turned_lo, n.fresh + kt // 2 + 1)
                    xh, xl = x_hi[:, kt, tokens(blk)], x_lo[:, kt, tokens(blk)]
                    mm(o, xh, wh[:, k, :], start=first and k == 0, stop=False)
                    mm(o, xh, wl[:, k, :], start=False, stop=False)
                    done = mm(o, xl, wh[:, k, :], start=False, stop=last and k == len(kts) - 1)
                if blk == 0 and kt == KT - 1:
                    n.fresh = None
                return done

            def chunk_unit(x_hi, x_lo, kts, width, first, last, between=None):
                pe.wait_ge(lo_done, n.unit + 1)
                parts = unit_parts(len(kts), width)
                for blk in range(TB):
                    if between:
                        between(blk)
                    if first:
                        since(pe, acc_read, n.chunk * 2 + (blk - 1))
                    done = half_unit(acc[blk][:, 0:width], x_hi, x_lo, kts, parts, blk, first, last)
                    if blk == 0 and last:
                        done.then_inc(blk0_done, 1)
                done.then_inc(unit_used, 1)
                n.next_unit()
                if last:
                    n.chunk = n.chunk + 1

            def chunk(x_hi, x_lo, nkt, width, x_kt=0):
                for k0 in range(0, nkt, 4):
                    m = min(4, nkt - k0)
                    chunk_unit(x_hi, x_lo, range(x_kt + k0, x_kt + k0 + m), width, k0 == 0, k0 + m == nkt)

            def proj_unit(kts, first, last):
                pe.wait_ge(lo_done, n.unit + 1)
                wh, wl = unit_parts(2, D)
                for blk in range(TB):
                    for k, kt in enumerate(kts):
                        xh, xl = oT_hi[:, kt, tokens(blk)], oT_lo[:, kt, tokens(blk)]
                        for i, (xp, wp) in enumerate(((xh, wh), (xh, wl), (xl, wh))):
                            for half in range(2):
                                done = mm(acc[2 * blk + half][:, :], xp, wp[:, k, 512 * half:512 * half + 512],
                                          start=first and k == 0 and i == 0, stop=last and k == 1 and i == 2)
                    if blk == 0 and last:
                        done.then_inc(proj_done, 1)
                done.then_inc(unit_used, 1)
                n.next_unit()

            def projection(order=(0, 2, 4, 6), bank0=None):
                for i, k0 in enumerate(order):
                    if bank0 is not None:
                        pe.wait_ge(turned_lo, bank0 + i + 1)
                    proj_unit((k0, k0 + 1), i == 0, i == 3)

            def turn(tile, nkt, banks):
                for k in range(nkt):
                    for blk in range(TB):
                        c0 = (k % 2) * S + blk * P
                        done = transpose(banks[k // 2][:, c0:c0 + P], tile(k, blk), ident[:, :])
                    if k % 2 or k == nkt - 1:
                        done.then_inc(turned, 1)
                        n.bank = n.bank + 1

            def turn_stream(norm):
                for blk in range(TB):
                    if n.h == 0:
                        pe.wait_ge(x_loaded, 16 * TB)
                    else:
                        pe.wait_ge(h_ready, n.h - TB + blk + 1)
                    for kt in range(KT):
                        c0 = (kt % 2) * S + blk * P
                        done = transpose(stream_banks[norm][kt // 2][:, c0:c0 + P], h[:, blk, P * kt:P * kt + P], ident[:, :])
                        if blk == 1 and kt % 2:
                            done.then_inc(turned, 1)
                n.fresh = n.bank
                n.bank = n.bank + 4
                n.h += TB

            def turn_pair(kind, t):
                for j in range(2 if kind == "mla" else 1):
                    since(pe, qkT_read, n.turn)
                    for i in range(4):
                        blk = i % 2
                        src = (q_mla, k_mla)[i // 2][:, blk, 2 * t + j, :] if kind == "mla" else \
                            qkv[:, i // 2, blk, P * t:P * t + P]
                        done = transpose(qkT_ps[0:src.shape[1], P * i:P * i + P], src, ident[:, :])
                    done.then_inc(qkT_done, 1)
                    n.turn = n.turn + 1

            def logits(kind, t, pair0, turn0):
                per = 2 if kind == "mla" else 1
                pe.wait_ge(qkT_read, turn0 + per * (t + 1))
                since(pe, logit_read, pair0 + t)
                for j in range(2):
                    src = (qkT, qkT_odd)[j][0:MLA_QK, t, :] if kind == "mla" else qkT[HD * j:HD * j + HD, t, :]
                    mm(pair_ps[:, j, 0:128], src[:, 0:128], src[:, 256:384], start=True, stop=True)
                    done = mm(pair_ps[:, j, 128:384], src[:, 128:256], src[:, 256:512], start=True, stop=True)
                done.then_inc(logit_done, 1)

            def turn_probs(t, pair0):
                pe.wait_ge(prob_done, pair0 + (t + 1))
                since(pe, prT_act, pair0 + t)
                since(pe, prT_dve, pair0 + t)
                for j in range(2):
                    for i in range(3):
                        done = transpose(turn_ps[:, j, P * i:P * i + P], logit[:, t % 2, j, P * i:P * i + P],
                                         ident[:, :])
                done.then_inc(prT_done, 1)

            def values(kind, t, pair0):
                pe.wait_ge(prT_act, pair0 + (t + 1))
                pe.wait_ge(prT_dve, pair0 + (t + 1))
                since(pe, out_read, pair0 + t)
                for j in range(2):
                    c0 = P * t + HD * j
                    v0, v1 = [(v_mla[:, blk, c0:c0 + HD] if kind == "mla" else qkv[:, 2, blk, c0:c0 + HD])
                              for blk in range(TB)]
                    pr = prT[:, t % 2, j, :]
                    o0, o1 = out_ps[:, HD * j:HD * j + HD], out_ps[:, P + HD * j:P + HD * j + HD]
                    mm(o0, pr[:, 0:128], v0, start=True, stop=True)
                    mm(o1, pr[:, 128:256], v0, start=True, stop=False)
                    done = mm(o1, pr[:, 256:384], v1, start=False, stop=True)
                done.then_inc(out_done, 1)

            def attention_step(kind, s, pair0, turn0):
                if s < 4:
                    logits(kind, s, pair0, turn0)
                if 1 <= s < 5:
                    turn_probs(s - 1, pair0)
                if 2 <= s:
                    values(kind, s - 2, pair0)

            def group_ready(qk, copied):
                pe.wait_ge(qk_ready, qk)
                pe.wait_ge(acc_read, copied)

            def ao_tile(kt0):
                return lambda k, blk: ao[:, blk, P * (kt0 + k):P * (kt0 + k) + P]

            def attend(kind, ready, order):
                pair0, turn0 = n.pair, n.turn
                for s in range(6):
                    if s < 2:
                        turn_pair(kind, 2 * s)
                        turn_pair(kind, 2 * s + 1)
                    attention_step(kind, s, pair0, turn0)
                    if s == 1:
                        turn(ao_tile(ready), 4, acc_banks)
                n.pair = pair0 + 4
                pe.wait_ge(out_read, n.pair)
                turn(ao_tile(4 - ready), 4, pair_banks)
                projection(order, n.bank - 4)

            def project(widths):
                for width in widths:
                    chunk(uT_hi, uT_lo, KT, width)

            def project_and_attend(widths, kind, to=6):
                pair0, turn0 = n.pair, n.turn
                s = 0
                for width in widths:
                    for k0 in (0, 4):
                        def between(blk, s=s):
                            if s < 2:
                                turn_pair(kind, 2 * s + blk)
                            if s == 5 and blk == 1:
                                attention_step(kind, 5, pair0, turn0)
                        chunk_unit(uT_hi, uT_lo, range(k0, k0 + 4), width, k0 == 0, k0 == 4, between)
                        if s < 5:
                            attention_step(kind, s, pair0, turn0)
                        s += 1
                for s in range(s, to):
                    attention_step(kind, s, pair0, turn0)
                n.pair = pair0 + 4

            def swiglu():
                n0, b0 = n.written, n.bank

                def step_unit(c, k0):
                    pe.wait_ge(lo_done, n.unit + 1)
                    if k0 == 0:
                        since(pe, u_ready, n0 + c)
                    parts = unit_parts(4, 2 * FT)
                    for blk in range(TB):
                        done = half_unit(pair_ps[:, blk, :], uT_hi, uT_lo, range(k0, k0 + 4), parts, blk,
                                         k0 == 0, k0 == 4)
                    done.then_inc(unit_used, 1)
                    n.next_unit()

                def turn_hidden(c):
                    pe.wait_ge(u_ready, n0 + c + 1)
                    since(pe, turned_lo, b0 + c)
                    turn(lambda k, blk: hid[:, blk, P * k:P * k + P], 2, turn_banks)

                def down(c, first, last):
                    pe.wait_ge(turned_lo, b0 + c + 1)
                    proj_unit((0, 1), first, last)

                def step(c, first):
                    step_unit(c, 0)
                    turn_hidden(c - 1)
                    step_unit(c, 4)
                    down(c - 1, first, False)

                step_unit(0, 0)
                step_unit(0, 4)
                step(1, True)
                u0 = n.unit
                with pe.Fori(2, NF) as c:
                    n.unit = u0 + (c - 2) * 3
                    step(c, False)
                n.unit = u0 + 3 * (NF - 2)
                turn_hidden(NF - 1)
                down(NF - 1, False, True)
                n.written, n.bank = n0 + NF, b0 + NF

            pe.wait_ge(tables, TABLES)
            transpose(acc[3][:, 0:GAIN_ROWS], gain_rows, ident[0:GAIN_ROWS, 0:GAIN_ROWS])
            transpose(acc[3][0:32, 64:104], tab, ident[0:40, 0:40]).then_inc(tables_T, 1)
            turn_stream(MIX0)
            project((512, 512))
            pe.wait_ge(consts, CONSTS)
            pe.wait_ge(gains_set, 2)
            mm(acc[2][0:40, 0:REL], tabT[:, :], onehot[:, :], start=True, stop=True).then_inc(tab_done, 1)
            project((512,))
            group_ready(0, 6)
            pe.wait_ge(rel_ready, 1)
            pair0, turn0 = n.pair, n.turn
            project_and_attend((384, 288), "sb", to=5)
            pe.wait_ge(acc_read, 10)
            turn(lambda k, blk: cq[:, blk, P * k:P * k + P], 3, latent_banks)
            turn(lambda k, blk: ckv[:, blk, P * k:P * k + P], 2, latent_banks[2:])
            pe.wait_ge(turned_lo, n.bank - 1)
            for _ in range(2):
                chunk(oT_hi, oT_lo, 3, 384)
            attention_step("sb", 5, pair0, turn0)
            pe.wait_ge(turned_lo, n.bank)
            for _ in range(2):
                chunk(oT_hi, oT_lo, 2, 512, x_kt=3)
            group_ready(1, 18)
            pe.wait_ge(out_read, n.pair)
            attend("mla", 4, (4, 6, 0, 2))
            turn_stream(FFN0)
            swiglu()
            turn_stream(MIX1)
            project((512, 512, 512))
            group_ready(1, 24)
            project_and_attend((512, 512, 512), "band")
            group_ready(1, 30)
            pe.wait_ge(out_read, n.pair)
            attend("band", 0, (0, 2, 4, 6))
            turn_stream(FFN1)
            swiglu()
            n.h += TB
            turn_stream(LN2)
            project((512, 512, 512))
            u0, c0, p0, t0 = n.unit, n.chunk, n.pair, n.turn
            with pe.Fori(0, 3) as g:
                n.unit, n.chunk, n.pair, n.turn = u0 + g * 6, c0 + g * 3, p0 + g * 4, t0 + g * 4
                group_ready(g * 2 + 3, g * 6 + 36)
                project_and_attend((512, 512, 512), "last")
            n.unit, n.chunk, n.pair, n.turn = u0 + 18, c0 + 9, p0 + 12, t0 + 12
            group_ready(9, 54)
            project_and_attend((512, 256), "last")
            group_ready(11, 58)
            project_and_attend((512, 512, 512), "last")

            def merged_tile(kt0):
                return lambda k, blk: merged[:, blk, P * (kt0 + k):P * (kt0 + k) + P]
            for i in range(3):
                n.written += 1
                pe.wait_ge(u_ready, n.written)
                o = heads[:, :, HEAD0[i]:HEAD0[i] + 8, :].rearrange("p b n d -> p b (n d)")
                turn(lambda k, blk: o[:, blk, P * k:P * k + P], 4, turn_banks)
                for half in range(2):
                    chunk(uT_hi, uT_lo, KT, 512)
                    pe.wait_ge(turned_lo, n.bank)
                    if i == 2 and half == 1:
                        pe.wait_ge(gated, 5)
                        turn(merged_tile(0), 4, turn_banks)
                    chunk(oT_hi, oT_lo, 4, 512, x_kt=4 * (i % 2))
            pe.wait_ge(acc_read, n.chunk * 2)
            pe.wait_ge(turned_lo, n.bank)
            proj_unit((4, 5), True, False)
            pe.wait_ge(gated, 6)
            turn(merged_tile(4), 4, pair_banks)
            proj_unit((6, 7), False, False)
            pe.wait_ge(turned_lo, n.bank)
            proj_unit((0, 1), False, False)
            proj_unit((2, 3), False, True)

        @block.scalar
        def _(act):
            n = Ordinals()
            own = [0]
            activation = nc.scalar.activation

            def gain_row(norm, count):
                return gain_rows[GAIN_COL[norm]:GAIN_COL[norm] + count, :]
            small = [(ident[:, :], identity),
                     (gain_row(MIX0, 16), g_mix.rearrange("l (k p) -> (l k) p", p=P)),
                     (gain_row(FFN0, 16), g_ffn.rearrange("l (k p) -> (l k) p", p=P)),
                     (gain_row(LN2, 8), g_ln2.rearrange("(k p) -> k p", p=P)),
                     (gain_row(CQ, 3), g_cq.rearrange("(k p) -> k p", p=P)),
                     (gain_row(CKV, 2), g_ckv.rearrange("(k p) -> k p", p=P)),
                     (gain_rows[QK_COL:QK_COL + 6, 0:HD], qk_g), (gain_rows[QK_COL:QK_COL + 6, HD:P], qk_g),
                     (tab, rel_bias2)]
            for dst, src in small:
                act.dma_start(dst, src).then_inc(tables, 16)

            act.add_instruction(mybir.InstLoadActFuncSet(
                name=nc.get_next_instruction_name(), engine=mybir.EngineType.Activation,
                act_func_set_id=LN_EXP_TABLES, ins=[], outs=[]))

            def link(ins):
                own[0] = own[0] + 1
                ins.then_inc(act_self, 1)
                act.wait_ge(act_self, own[0])

            def round_unit(ahead=2, width=UNIT):
                slot = (n.slot + ahead) % RING
                act.wait_ge(raw_full[slot], raw_target(n, ahead))
                since(act, unit_used, n.unit + ahead - (RING - 1))
                activation(w_hi[:, slot, 0:width], w_raw[:, slot, 0:width], ACT.Copy).then_inc(hi_done, 1)

            def raw_target(n, ahead):
                return n.raw_base + ((n.raw_local + ahead) // RING + 1) * 32

            def slot_step(width=UNIT, ahead_exists=True):
                if ahead_exists:
                    round_unit(2, width)
                n.next_unit()
                n.raw_local += 1

            def at_loop(u0, local0, trips_expr, units):
                n.unit = u0 + trips_expr * units
                n.raw_base, n.raw_local = trips_expr * (32 * units // RING), local0

            n.raw_base, n.raw_local = 0, 0

            def split_banks(dst, kt0, nkt, banks, norm=None):
                for k0 in range(0, nkt, 2):
                    m = min(2, nkt - k0)
                    act.wait_ge(turned, n.bank + 1)
                    if norm is None:
                        done = activation(dst[:, kt0 + k0:kt0 + k0 + m, :].rearrange("p k t -> p (k t)"),
                                          banks[k0 // 2][:, 0:m * S], ACT.Copy)
                    else:
                        for k in range(k0, k0 + m):
                            c = GAIN_COL[norm] + k
                            done = activation(dst[:, kt0 + k, :], banks[k0 // 2][:, (k - k0) * S:(k - k0 + 1) * S],
                                              ACT.Copy, scale=gain_T[:, c:c + 1])
                    done.then_inc(turned_hi, 1)
                    n.bank = n.bank + 1

            def root_of(sums, ln, y, count):
                link(activation(ln, sums, ACT.Ln, bias=eps[:, 0:1], scale=1.0 / count))
                activation(y, ln, ACT.Exp, scale=-0.5).then_inc(root, 1)
                n.roots += 1

            n.roots = n.squares = n.scales = n.h = 0

            def row_squares(norm, tile, width, blk):
                activation(square_flat[:, 0:width], tile[:, blk, 0:width], ACT.Square,
                           accum_out=norms[:, norm, 0, blk:blk + 1]).then_inc(squared, 1)
                n.squares += 1
                act.wait_ge(squared, n.squares)

            def row_root(norm, width):
                root_of(norms[:, norm, 0, :], norms[:, norm, 4, :], norms[:, norm, 2, :], width)

            def stream_norm(norm):
                for blk in range(TB):
                    if norm == MIX0:
                        act.wait_ge(x_loaded, 16 * TB)
                    else:
                        act.wait_ge(h_ready, n.h + blk + 1)
                    row_squares(norm, h, D, blk)
                    if blk == 0:
                        split_banks(uT_hi, 0, KT, stream_banks[norm], norm)
                row_root(norm, D)
                n.h += TB * (norm != MIX0)

            def scaled_by(norm):
                n.scales += 1
                act.wait_ge(row_scale, n.scales)
                n.norm = norm

            def scale_of(blk, sign=1):
                i = 5 if sign > 0 else 6
                return norms[:, n.norm, i, blk:blk + 1]

            def copy_block(blk, copies):
                if blk == 0:
                    act.wait_ge(blk0_done, n.chunk + 1)
                else:
                    act.wait_ge(unit_used, n.unit)
                for i, (dst, src, func, scale) in enumerate(copies):
                    done = activation(dst, src, func, scale=scale)
                done.then_inc(acc_read, 1)

            def copy_chunk(copies):
                for blk in range(TB):
                    copy_block(blk, copies(blk))
                n.chunk = n.chunk + 1

            def plain(dst, width=512):
                return lambda blk: [(dst(blk), acc[blk][:, 0:width], ACT.Copy, scale_of(blk))]

            def copy_pair(kind, t, pair0, gains=None):
                for j in range(2 if kind == "mla" else 1):
                    act.wait_ge(qkT_done, n.turn + 1)
                    if kind == "mla":
                        activation((qkT, qkT_odd)[j][0:MLA_QK, t, :], qkT_ps[0:MLA_QK, :], ACT.Copy)\
                            .then_inc(qkT_read, 1)
                    elif kind == "last":
                        activation(qkT[:, t, 0:S], qkT_ps[:, 0:S], ACT.Copy, scale=g_now[:, 0:1])
                        activation(qkT[:, t, S:2 * S], qkT_ps[:, S:2 * S], ACT.Copy,
                                   scale=g_now[:, 1:2]).then_inc(qkT_read, 1)
                    else:
                        activation(qkT[:, t, :], qkT_ps[:, :], ACT.Copy).then_inc(qkT_read, 1)
                    n.turn = n.turn + 1

            def soft_plus(t, pair0):
                act.wait_ge(logit_done, pair0 + (t + 1))
                since(act, max_done, pair0 + t)
                z = pair_ps[:, :, 0:384]
                activation(sb_tmp[0], z, ACT.Relu, scale=HD ** -0.5)
                link(activation(sb_tmp[1], z, ACT.Abs, scale=HD ** -0.5))
                link(activation(sb_tmp[1], sb_tmp[1], ACT.Exp, scale=-1.0))
                activation(sb_tmp[1], sb_tmp[1], ACT.Ln, bias=1.0).then_inc(sb_abs, 1)

            def exponentiate(kind, t, pair0, head0):
                act.wait_ge(max_done, pair0 + (t + 1))
                pr = logit[:, t % 2, :, :]
                if kind == "sb":
                    activation(pr, pr, ACT.Exp).then_inc(prob_done, 1)
                    return
                for blk in range(TB):
                    cols = key_cols(blk)[0]
                    for j in range(2):
                        head = slice(2 * t + j, 2 * t + j + 1)
                        done = activation(pr[:, j, cols], pr[:, j, cols], ACT.Exp,
                                          bias=negmax8[:, blk, head], accum_out=total8[:, blk, head])
                done.then_inc(prob_done, 1)

            def copy_probs(t, pair0):
                act.wait_ge(prT_done, pair0 + (t + 1))
                activation(prT[:, t % 2, 0, :], turn_ps[:, 0, 0:384], ACT.Copy).then_inc(prT_act, 1)

            def attention_step(kind, s, pair0, head0):
                if kind == "sb" and s < 4:
                    soft_plus(s, pair0)
                if 1 <= s < 5:
                    exponentiate(kind, s - 1, pair0, head0)
                if 2 <= s:
                    copy_probs(s - 2, pair0)

            def attend(kind, ready, head0=0):
                pair0 = n.pair
                for s in range(6):
                    if s < 2:
                        copy_pair(kind, 2 * s, pair0)
                        copy_pair(kind, 2 * s + 1, pair0)
                    attention_step(kind, s, pair0, head0)
                    if s == 1:
                        split_banks(oT_hi, ready, 4, acc_banks)
                n.pair = pair0 + 4
                split_banks(oT_hi, 4 - ready, 4, pair_banks)
                for _ in range(4):
                    slot_step()

            def project(chunks, prefetch=(UNIT,) * 6):
                s = 0
                for done in chunks:
                    for _ in range(2):
                        slot_step(prefetch[s])
                        s += 1
                    done()

            def project_and_attend(chunks, kind, head0=0, gains=None, prefetch=(UNIT,) * 6, after={}):
                pair0 = n.pair
                if kind == "last":
                    link(activation(g_now[:, :], g_col[:, bass.ds(gains, 2)], ACT.Copy))
                s = 0
                for done in chunks:
                    for last in (False, True):
                        slot_step(prefetch[s])
                        if s < 2:
                            copy_pair(kind, 2 * s, pair0, gains)
                            copy_pair(kind, 2 * s + 1, pair0, gains)
                        attention_step(kind, s, pair0, head0)
                        if last and (s < 2 * len(chunks) - 1 or kind == "sb"):
                            done()
                        if s in after:
                            after[s]()
                        s += 1
                for s in range(s, 6):
                    attention_step(kind, s, pair0, head0)
                    if s in after:
                        after[s]()
                if kind != "sb":
                    chunks[-1]()
                n.pair = pair0 + 4

            def copy_qkv(i):
                def done():
                    if i < 2:
                        since(act, qkT_done, n.turn)
                    else:
                        since(act, out_done, n.used)
                    copy_chunk(plain(lambda blk: qkv[:, i, blk, :]))
                return done

            def head_norm(i):
                since(act, summed, n.sums)
                act.wait_ge(acc_read, n.chunk * 2)
                activation(square[:, :, :], qkv[:, i, :, :], ACT.Square).then_inc(squared, 1)
                n.squares = n.squares + 1
                n.sums = n.sums + 1
                act.wait_ge(summed, n.sums)
                root_of(stat[:, 0, :], stat[:, 4, :], stat[:, 2, :], HD)

            n.sums = 0

            def copy_and_norm(i):
                def done():
                    copy_qkv(i)()
                    head_norm(i)
                return done

            def window_kv():
                since(act, qkT_done, n.turn)
                since(act, out_done, n.used)
                def copies(blk):
                    def four(dst, c0):
                        return (dst.rearrange("p (g r d) -> p g r d", g=2, r=4),
                                acc[blk][:, c0:c0 + 128].rearrange("p (g d) -> p g d", g=2)
                                .unsqueeze(2).broadcast_to([P, 2, 4, HD]), ACT.Copy, scale_of(blk))
                    return [four(qkv[:, 1, blk, :], 0), four(qkv[:, 2, blk, :], 128)]
                copy_chunk(copies)
                head_norm(1)

            def swiglu():
                n0, b0 = n.written, n.bank

                def gate(c):
                    act.wait_ge(unit_used, n.unit)
                    since(act, u_ready, n0 + c)
                    activation(hid_e[:, 0, :], pair_ps[:, 0, 0:FT], ACT.Exp, scale=scale_of(0, -1))
                    link(activation(hid_e[:, 1, :], pair_ps[:, 1, 0:FT], ACT.Exp, scale=scale_of(1, -1)))
                    link(activation(hid_e, hid_e, ACT.Ln, bias=1.0))
                    activation(hid_e, hid_e, ACT.Exp, scale=-1.0).then_inc(gate_exp, 1)

                def split_hidden(c):
                    act.wait_ge(turned, b0 + c + 1)
                    activation(oT_hi[:, 0:2, :].rearrange("p k t -> p (k t)"), turn_ps[:, 0, :], ACT.Copy)\
                        .then_inc(turned_hi, 1)

                def step(c):
                    slot_step()
                    split_hidden(c - 1)
                    slot_step()
                    gate(c)
                    slot_step()

                slot_step()
                slot_step()
                gate(0)
                step(1)
                u0, local0, base0, own0 = n.unit, n.raw_local, n.raw_base, own[0]
                with act.Fori(2, NF) as c:
                    n.unit = u0 + (c - 2) * 3
                    own[0] = own0 + (c - 2) * 2
                    n.raw_base, n.raw_local = (c - 2) * 32 + base0, local0
                    step(c)
                trips = NF - 2
                n.unit, own[0] = u0 + 3 * trips, own0 + 2 * trips
                n.raw_base, n.raw_local = base0, local0 + 3 * trips
                split_hidden(NF - 1)
                slot_step()
                n.written, n.bank = n0 + NF, b0 + NF

            act.wait_ge(eps_set, 1)
            act.wait_ge(tables_T, 1)
            activation(gain_T[:, :], acc[3][:, 0:GAIN_ROWS], ACT.Copy).then_inc(gains_set, 1)
            activation(tabT[:, :], acc[3][0:32, 64:104], ACT.Copy).then_inc(gains_set, 1)
            act.wait_ge(gains_set, 2)
            for group, row in enumerate((0, 2, 2, 2, 4)):
                done = activation(g_col[:, 2 * group:2 * group + 2], gain_T[:, QK_COL + row:QK_COL + row + 2], ACT.Copy)
            link(done)
            stream_norm(MIX0)
            round_unit(0)
            round_unit(1)
            n.used = 0
            scaled_by(MIX0)
            project([copy_qkv(i) for i in range(3)], (UNIT,) * 4 + (1536, 1536))

            def latents():
                split_banks(oT_hi, 0, 3, latent_banks, CQ)
                split_banks(oT_hi, 3, 2, latent_banks[2:], CKV)
            project_and_attend([lambda: copy_chunk(plain(lambda blk: cq[:, blk, :], 384)),
                                lambda: copy_chunk(lambda blk: [
                                    (ckv[:, blk, :], acc[blk][:, 0:256], ACT.Copy, scale_of(blk)),
                                    (k_rot[:, blk, :], acc[blk][:, 256:288], ACT.Copy, scale_of(blk))])],
                               "sb", prefetch=(1152, 1152, 1152, 1152), after={4: latents})
            act.wait_ge(acc_read, 10)
            for norm, tile, width in ((CQ, cq, 384), (CKV, ckv, 256)):
                for blk in range(TB):
                    row_squares(norm, tile, width, blk)
                row_root(norm, width)
            act.wait_ge(rel_stored, 16)
            for i in range(2):
                slot_step(1024)
                if i == 0:
                    scaled_by(CQ)
                copy_chunk(lambda blk: [(q_mla[:, blk, 4 * i:4 * i + 4, :].rearrange("p n c -> p (n c)"),
                                         acc[blk][:, 0:384], ACT.Copy, scale_of(blk))])
            for i in range(2):
                slot_step()
                if i == 0:
                    scaled_by(CKV)
                def kv(blk):
                    src = acc[blk][:, :].rearrange("p (n c) -> p n c", c=128)
                    return [(k_mla[:, blk, 4 * i:4 * i + 4, 0:HD], src[:, :, 0:HD], ACT.Copy, scale_of(blk)),
                            (v_mla[:, blk, 256 * i:256 * i + 256].rearrange("p (n c) -> p n c", c=HD),
                             src[:, :, HD:128], ACT.Copy, scale_of(blk))]
                copy_chunk(kv)
            attend("mla", 4)
            stream_norm(FFN0)
            scaled_by(FFN0)
            swiglu()
            stream_norm(MIX1)
            scaled_by(MIX1)
            n.used = 8
            project([copy_qkv(i) for i in range(3)])
            n.used = 12
            project_and_attend([copy_qkv(i) for i in range(3)], "band", 0)
            attend("band", 0, 8)
            stream_norm(FFN1)
            scaled_by(FFN1)
            swiglu()
            for blk in range(TB):
                act.wait_ge(h_ready, n.h + blk + 1)
                row_squares(FINAL, h, D, blk)
            row_root(FINAL, D)
            n.h += TB
            stream_norm(LN2)
            scaled_by(LN2)
            n.used = n.pair
            project([copy_and_norm(0), copy_and_norm(1), copy_qkv(2)])
            u0, c0, p0, t0, local0, base0 = n.unit, n.chunk, n.pair, n.turn, n.raw_local, n.raw_base
            own0, s0, q0, r0 = own[0], n.sums, n.squares, n.roots
            with act.Fori(0, 3) as g:
                n.unit, n.chunk, n.pair, n.turn = u0 + g * 6, c0 + g * 3, p0 + g * 4, t0 + g * 4
                n.used = p0 + g * 4 + 4
                n.raw_base, n.raw_local = g * 64 + base0, local0
                own[0], n.sums, n.squares = own0 + g * 3, s0 + g * 2, q0 + g * 2
                project_and_attend([copy_and_norm(0), copy_and_norm(1), copy_qkv(2)], "last", g * 8, g * 2)
            n.unit, n.chunk, n.pair, n.turn = u0 + 18, c0 + 9, p0 + 12, t0 + 12
            n.raw_base, n.raw_local = base0, local0 + 18
            own[0], n.sums, n.squares, n.roots = own0 + 9, s0 + 6, q0 + 6, r0 + 6
            n.used = p0 + 16
            project_and_attend([copy_and_norm(0), window_kv], "last", 24, 6)

            def sigmoid():
                act.wait_ge(acc_read, n.chunk * 2)
                link(activation(square[:, :, :], square[:, :, :], ACT.Ln, bias=1.0))
                activation(square[:, :, :], square[:, :, :], ACT.Exp, scale=-1.0).then_inc(gate_exp, 1)

            def swish_gate(i):
                def done():
                    if i == 0:
                        act.wait_ge(max_done, 32)
                    since(act, swish_done, i)
                    copy_chunk(lambda blk: [(square[:, blk, :], acc[blk][:, :], ACT.Exp, scale_of(blk, -1)),
                                            (swish[:, i, blk, :], acc[blk][:, :], ACT.Copy, scale_of(blk))])
                    sigmoid()
                return done

            def factors(i, lo, hi):
                def run():
                    act.wait_ge(comb_d, i + 1)
                    activation(comb[:, lo:hi, :, :], comb[:, lo:hi, :, :], ACT.Exp).then_inc(comb_a, 1)
                return run
            project_and_attend([swish_gate(i) for i in range(3)], "last", 32, 8, after={3: factors(0, 1, 4)})
            for i in range(3):
                split_banks(oT_hi, 4 * (i % 2), 4, turn_banks)
                for half in range(2):
                    step = 2 * i + half
                    for _ in range(2):
                        slot_step(ahead_exists=True)
                    since(act, swish_done, 3) if step == 0 else act.wait_ge(gated, step)
                    copy_chunk(lambda blk: [(square[:, blk, :], acc[blk][:, :], ACT.Exp, scale_of(blk, -1))])
                    sigmoid()
                    if step == 0:
                        factors(1, 5, 7)()
                    if step == 5:
                        split_banks(oT_hi, 4, 4, turn_banks)
                    slot_step()
                    copy_chunk(lambda blk: [(branch_out[:, blk, :], acc[blk][:, :], ACT.Copy, 1.0)])
            slot_step()
            split_banks(oT_hi, 0, 4, pair_banks)
            for left in (3, 2, 1):
                slot_step(ahead_exists=left > 2)

        @block.vector
        def _(dve):
            n = Ordinals()
            own = [0]
            v = nc.vector
            n.roots = n.squares = n.h = n.exps = n.chunk = 0

            def link(ins):
                own[0] = own[0] + 1
                ins.then_inc(dve_self, 1)
                dve.wait_ge(dve_self, own[0])

            def split_unit(ahead=2, width=UNIT):
                slot = (n.slot + ahead) % RING
                dve.wait_ge(hi_done, n.unit + (ahead + 1))
                v.tensor_tensor(w_lo[:, slot, 0:width], w_raw[:, slot, 0:width],
                                w_hi[:, slot, 0:width].bitcast(f32), ALU.subtract).then_inc(lo_done, 1)

            def slot_step(width=UNIT, ahead_exists=True):
                if ahead_exists:
                    split_unit(2, width)
                n.next_unit()

            def split_banks(hi, lo, kt0, nkt, banks, norm=None):
                for k0 in range(0, nkt, 2):
                    m = min(2, nkt - k0)
                    dve.wait_ge(turned_hi, n.bank + 1)
                    if norm is None:
                        a, b = [t[:, kt0 + k0:kt0 + k0 + m, :].rearrange("p k t -> p (k t)") for t in (lo, hi)]
                        done = v.tensor_tensor(a, banks[k0 // 2][:, 0:m * S], b.bitcast(f32), ALU.subtract)
                    else:
                        for k in range(k0, k0 + m):
                            c = GAIN_COL[norm] + k
                            done = v.scalar_tensor_tensor(
                                lo[:, kt0 + k, :], banks[k0 // 2][:, (k - k0) * S:(k - k0 + 1) * S],
                                gain_T[:, c:c + 1], hi[:, kt0 + k, :].bitcast(f32), ALU.mult, ALU.subtract)
                    done.then_inc(turned_lo, 1)
                    n.bank = n.bank + 1

            def sharpen(sums, a, y, t, count):
                link(v.tensor_scalar(a, sums, 1.0 / count, EPS, ALU.mult, ALU.add))
                n.roots = n.roots + 1
                dve.wait_ge(root, n.roots)
                link(v.scalar_tensor_tensor(t, y, -0.5, y, ALU.mult, ALU.mult))
                link(v.tensor_tensor(t, t, a, ALU.mult))
                link(v.scalar_tensor_tensor(y, t, 1.5, y, ALU.add, ALU.mult))

            def row_scales(norm, width):
                n.squares = n.squares + 2
                dve.wait_ge(squared, n.squares)
                sums, a, y, t, _, y1, minus, twice = [norms[:, norm, i, :] for i in range(8)]
                sharpen(sums, a, y, t, width)
                v.tensor_scalar_mul(minus, y, -1.0)
                v.tensor_tensor(twice, y, y, ALU.mult)
                v.tensor_copy(y1, y).then_inc(row_scale, 1)

            def stream_norm(norm):
                split_banks(uT_hi, uT_lo, 0, KT, stream_banks[norm], norm)
                row_scales(norm, D)

            n.handed = 0

            def add_projection():
                n.proj += 1
                for blk in range(TB):
                    if blk == 0:
                        dve.wait_ge(proj_done, n.proj)
                    else:
                        dve.wait_ge(unit_used, n.unit)
                    for half in range(2):
                        c = slice(512 * half, 512 * half + 512)
                        done = v.tensor_tensor(h[:, blk, c], acc[2 * blk + half][:, :], h[:, blk, c], ALU.add)
                    done.then_inc(h_ready, 1)
                n.h += 2

            def maxima(kind, t, pair0, head0, bias_of):
                pr = logit[:, t % 2, :, :]
                dve.wait_ge(logit_done, pair0 + (t + 1))
                if kind != "sb" or True:
                    since(dve, prT_done, pair0 + (t - 1))
                scale = (MLA_QK if kind == "mla" else HD) ** -0.5
                for blk in range(TB):
                    cols, mask_cols = key_cols(blk)
                    done = v.scalar_tensor_tensor(pr[:, :, cols][:, :, ::-1], pair_ps[:, :, cols][:, :, ::-1], scale,
                                                  bias_of(t, mask_cols), ALU.mult, ALU.add)
                done.then_inc(logit_read, 1)
                dve.wait_ge(logit_read, pair0 + (t + 1))
                for blk in range(TB):
                    done = v.tensor_reduce(negmax8[:, blk, 2 * t:2 * t + 2], pr[:, :, key_cols(blk)[0]],
                                           op=ALU.max, axis=AX.X, negate=True)
                done.then_inc(max_done, 1)

            def stick(t, pair0):
                pr = logit[:, t % 2, :, :]
                dve.wait_ge(sb_abs, pair0 + (t + 1))
                since(dve, prT_done, pair0 + (t - 1))
                link(v.tensor_tensor(sb_tmp[0], sb_tmp[0], sb_tmp[1], ALU.add))
                for blk in range(TB):
                    cols, mask_cols = key_cols(blk)
                    for j in range(2):
                        v.tensor_tensor_scan(sb_tmp[2][:, j, cols][:, ::-1], sb_tmp[0][:, j, cols][:, ::-1],
                                             m_keep[:, mask_cols][:, ::-1], 0.0, ALU.add, ALU.mult)
                    done = v.scalar_tensor_tensor(pr[:, :, cols], pair_ps[:, :, cols], HD ** -0.5,
                                                  m_strict[:, mask_cols].unsqueeze(1).broadcast_to(
                                                      [P, 2, mask_cols.stop - mask_cols.start]), ALU.mult, ALU.add)
                done.then_inc(logit_read, 1)
                dve.wait_ge(logit_read, pair0 + (t + 1))
                v.tensor_tensor(pr, pr, sb_tmp[2], ALU.subtract).then_inc(max_done, 1)

            def copy_probs(t, pair0):
                dve.wait_ge(prT_done, pair0 + (t + 1))
                v.tensor_copy(prT[:, t % 2, 1, :], turn_ps[:, 1, 0:384]).then_inc(prT_dve, 1)

            def outputs(kind, t, pair0, head0):
                o = out_ps[:, 0:S].rearrange("p (b n d) -> p b n d", b=TB, n=2)
                dve.wait_ge(out_done, pair0 + (t + 1))
                if kind == "sb":
                    v.tensor_copy(ao_h[:, :, 8 + 2 * t:10 + 2 * t, :], o).then_inc(out_read, 1)
                elif kind == "last":
                    v.tensor_scalar_mul(heads[:, :, bass.ds(head0 + 2 * t, 2), :], o, 1.0).then_inc(out_read, 1)
                    if t == 3:
                        v.tensor_copy(negmax[:, :, bass.ds(head0, 8)], negmax8[:, :, :])
                        v.tensor_copy(total[:, :, bass.ds(head0, 8)], total8[:, :, :])
                else:
                    hs = slice(head0 + 2 * t, head0 + 2 * t + 2)
                    link(v.reciprocal(rtotal[:, :, :], total8[:, :, 2 * t:2 * t + 2]))
                    v.tensor_tensor(ao_h[:, :, hs, :], o, rtotal[:, :, :].unsqueeze(3).broadcast_to([P, TB, 2, HD]),
                                    ALU.mult).then_inc(out_read, 1)

            def attention_step(kind, s, pair0, head0, bias_of):
                if s < 4:
                    if kind == "sb":
                        stick(s, pair0)
                    else:
                        maxima(kind, s, pair0, head0, bias_of)
                if 1 <= s < 5:
                    copy_probs(s - 1, pair0)
                if 2 <= s:
                    outputs(kind, s - 2, pair0, head0)

            def attend(kind, ready, head0=0, bias_of=None):
                for s in range(6):
                    attention_step(kind, s, n.pair, head0, bias_of)
                    if s == 1:
                        split_banks(oT_hi, oT_lo, ready, 4, acc_banks)
                n.pair = n.pair + 4
                split_banks(oT_hi, oT_lo, 4 - ready, 4, pair_banks)
                for _ in range(4):
                    slot_step()
                add_projection()

            def project(done, prefetch=(UNIT,) * 6):
                for s in range(6):
                    slot_step(prefetch[s])
                    if s in done:
                        done[s]()

            def project_and_attend(units, kind, head0=0, bias_of=None, done={}, prefetch=(UNIT,) * 6):
                for s in range(6):
                    if s < units:
                        slot_step(prefetch[s])
                    attention_step(kind, s, n.pair, head0, bias_of)
                    if s in done:
                        done[s]()
                n.pair = n.pair + 4

            def head_norm(i):
                def run():
                    n.squares = n.squares + 1
                    dve.wait_ge(squared, n.squares)
                    n.sums = n.sums + 1
                    v.tensor_reduce(stat[:, 0, :], square[:, :, :].rearrange("p b (n d) -> p (b n) d", d=HD),
                                    op=ALU.add, axis=AX.X).then_inc(summed, 1)
                    dve.wait_ge(summed, n.sums)
                    sharpen(stat[:, 0, :], stat[:, 1, :], stat[:, 2, :], stat[:, 3, :], HD)
                    q = qkv[:, i, :, :].rearrange("p b (n d) -> p (b n) d", d=HD)
                    v.tensor_tensor(q, q, stat[:, 2, :].unsqueeze(2).broadcast_to([P, 16, HD]), ALU.mult)\
                        .then_inc(qk_ready, 1)
                    n.qk = n.qk + 1
                    dve.wait_ge(qk_ready, n.qk)
                return run

            n.sums, n.qk = 0, 0

            def rotate(x, y, heads_n, blk):
                t = [cs_t[:, i, 0:heads_n, :] for i in range(4)]
                c, s = [cs[:, blk, i, :].unsqueeze(1).broadcast_to([P, heads_n, 16]) for i in range(2)]
                x1, x2 = x[:, :, 0:16], x[:, :, 16:32]
                v.tensor_tensor(t[0], x1, c, ALU.mult)
                v.tensor_tensor(t[1], x2, s, ALU.mult)
                v.tensor_tensor(t[2], x2, c, ALU.mult)
                link(v.tensor_tensor(t[3], x1, s, ALU.mult))
                v.tensor_tensor(y[:, :, 0:16], t[0], t[1], ALU.subtract)
                link(v.tensor_tensor(y[:, :, 16:32], t[2], t[3], ALU.add))

            def swiglu(norm):
                n0, b0, e0 = n.handed, n.bank, n.exps
                gate_ps, up_ps = pair_ps[:, :, 0:FT], pair_ps[:, :, FT:2 * FT]

                def gate(c):
                    dve.wait_ge(gate_exp, e0 + c + 1)
                    for blk in range(TB):
                        done = v.scalar_tensor_tensor(hid_g[:, blk, :], gate_ps[:, blk, :],
                                                      norms[:, norm, 7, blk:blk + 1], hid_e[:, blk, :],
                                                      ALU.mult, ALU.mult)
                    link(done)
                    since(dve, turned, b0 + c)
                    v.tensor_tensor(hid, up_ps, hid_g, ALU.mult).then_inc(u_ready, 1)

                def split_hidden(c):
                    dve.wait_ge(turned_hi, b0 + c + 1)
                    lo, hi = [t[:, 0:2, :].rearrange("p k t -> p (k t)") for t in (oT_lo, oT_hi)]
                    v.tensor_tensor(lo, turn_ps[:, 0, :], hi.bitcast(f32), ALU.subtract).then_inc(turned_lo, 1)

                def step(c):
                    slot_step()
                    split_hidden(c - 1)
                    slot_step()
                    gate(c)
                    slot_step()

                slot_step()
                slot_step()
                gate(0)
                step(1)
                u0, own0 = n.unit, own[0]
                with dve.Fori(2, NF) as c:
                    n.unit = u0 + (c - 2) * 3
                    own[0] = own0 + (c - 2)
                    step(c)
                n.unit, own[0] = u0 + 3 * (NF - 2), own0 + NF - 2
                split_hidden(NF - 1)
                slot_step()
                n.handed, n.bank, n.exps = n0 + NF, b0 + NF, e0 + NF
                add_projection()

            dve.wait_ge(gains_set, 1)
            stream_norm(MIX0)
            split_unit(0)
            split_unit(1)

            def distance_rows():
                dve.wait_ge(consts, CONSTS)
                dve.wait_ge(tab_done, 1)
                v.tensor_tensor(rel_f, acc[2][0:40, 0:REL], dist_m, ALU.add).then_inc(rel_ready, 1)
            project({4: distance_rows}, (UNIT,) * 4 + (1536, 1536))

            def latents():
                split_banks(oT_hi, oT_lo, 0, 3, latent_banks, CQ)
                split_banks(oT_hi, oT_lo, 3, 2, latent_banks[2:], CKV)
                row_scales(CQ, 384)
                row_scales(CKV, 256)
                slot_step(1024)
                slot_step(1024)
            project_and_attend(4, "sb", prefetch=(1152, 1152, 1152, 1152), done={4: latents})
            slot_step()
            slot_step()
            for blk in range(TB):
                rotate(k_rot[:, blk, :].unsqueeze(1), k_rot2[:, blk, :].unsqueeze(1), 1, blk)
            dve.wait_ge(acc_read, 18)
            for blk in range(TB):
                v.tensor_copy(k_mla[:, blk, :, HD:MLA_QK], k_rot2[:, blk, :].unsqueeze(1).broadcast_to([P, 8, 32]))
                q_rot = q_mla[:, blk, :, HD:MLA_QK]
                rotate(q_rot, q_rot, 8, blk)
            v.tensor_copy(norms[:, CQ, 3, 0:1], norms[:, CQ, 2, 0:1]).then_inc(qk_ready, 1)
            n.qk = 1
            mask = lambda t, cols: m_chunk[:, back(cols)].unsqueeze(1).broadcast_to(
                [P, 2, cols.stop - cols.start])
            attend("mla", 4, 0, mask)
            stream_norm(FFN0)
            swiglu(FFN0)
            stream_norm(MIX1)
            project({})
            dve.wait_ge(band_ready, 1)
            def table(slot):
                return lambda t, cols: bias[:, slot, 2 * t:2 * t + 2, back(cols)]
            project_and_attend(6, "band", 0, table(2))
            attend("band", 0, 8, table(3))
            stream_norm(FFN1)
            swiglu(FFN1)
            n.squares = n.squares + 2
            dve.wait_ge(squared, n.squares)
            sharpen(*[norms[:, FINAL, i, :] for i in range(4)], D)
            dve.wait_ge(gain_full, 16)
            for blk in range(TB):
                v.scalar_tensor_tensor(h[:, blk, :], h[:, blk, :], norms[:, FINAL, 2, blk:blk + 1],
                                       gain, ALU.mult, ALU.mult).then_inc(h_ready, 1)
            stream_norm(LN2)
            project({1: head_norm(0), 3: head_norm(1)})
            for g in range(4):
                dve.wait_ge(bias_full[g], 16)
            u0, p0, own0, s0, q0, r0, k0 = n.unit, n.pair, own[0], n.sums, n.squares, n.roots, n.qk
            with dve.Fori(0, 3) as g:
                n.unit, n.pair, own[0] = u0 + g * 6, p0 + g * 4, own0 + g * 8
                n.sums, n.squares, n.roots, n.qk = s0 + g * 2, q0 + g * 2, r0 + g * 2, k0 + g * 2
                def table_g(t, cols):
                    return flat_bias[:, bass.ds(g * 2048 + (2 * t * S), 2 * S)]\
                        .rearrange("p (j c) -> p j c", j=2)[:, :, back(cols)]
                project_and_attend(6, "last", g * 8, table_g, {1: head_norm(0), 3: head_norm(1)})
            n.unit, n.pair, own[0] = u0 + 18, p0 + 12, own0 + 24
            n.sums, n.squares, n.roots, n.qk = s0 + 6, q0 + 6, r0 + 6, k0 + 6
            project_and_attend(4, "last", 24, table(3), {1: head_norm(0), 5: head_norm(1)},
                               prefetch=(1024, 1024, UNIT, UNIT))

            def nm(group):
                return negmax[:, :, 8 * group:8 * group + 8]

            def tot(group):
                return total[:, :, 8 * group:8 * group + 8]

            cb = [comb[:, i, :, :] for i in range(8)]
            sinks_b = sink[:, :].unsqueeze(1).broadcast_to([P, TB, 8])

            def eight(group):
                return heads[:, :, 8 * group:8 * group + 8, :]

            def scaled(group, factor):
                link(v.tensor_tensor(eight(group), eight(group), factor.unsqueeze(3).broadcast_to([P, TB, 8, HD]),
                                     ALU.mult))

            def swish_gate(i):
                n.exps += 1
                dve.wait_ge(gate_exp, n.exps)
                v.tensor_tensor(swish[:, i, :, :], swish[:, i, :, :], square[:, :, :], ALU.mult)\
                    .then_inc(swish_done, 1)

            def gate_branch(i, group):
                dve.wait_ge(swish_done, i + 1)
                o = eight(group).rearrange("p b n d -> p b (n d)")
                v.tensor_tensor(o, o, swish[:, i, :, :], ALU.mult).then_inc(u_ready, 1)
                n.handed += 1

            def full_over_total():
                link(v.reciprocal(cb[7], tot(0)))
                scaled(0, cb[7])

            def first_gate():
                swish_gate(0)
                gate_branch(0, 0)
                link(v.tensor_tensor(cb[0], nm(1), nm(2), ALU.min))
                link(v.tensor_tensor(cb[0], cb[0], nm(3), ALU.min))
                for g in (1, 2, 3):
                    done = v.tensor_tensor(cb[g], cb[0], nm(g), ALU.subtract)
                done.then_inc(comb_d, 1)

            def dilation_weights():
                swish_gate(1)
                dve.wait_ge(comb_a, 1)
                link(v.tensor_tensor(cb[0], cb[1], tot(1), ALU.mult))
                for g in (2, 3):
                    link(v.tensor_tensor(cb[7], cb[g], tot(g), ALU.mult))
                    link(v.tensor_tensor(cb[0], cb[0], cb[7], ALU.add))
                link(v.reciprocal(cb[0], cb[0]))
                for g in (1, 2, 3):
                    link(v.tensor_tensor(cb[g], cb[g], cb[0], ALU.mult))
                scaled(1, cb[1])

            def add_dilation(g):
                scaled(g, cb[g])
                link(v.tensor_tensor(eight(1), eight(1), eight(g), ALU.add))

            def last_gate():
                add_dilation(3)
                gate_branch(1, 1)
                swish_gate(2)
                link(v.scalar_tensor_tensor(cb[4], sinks_b, -1.0, nm(4), ALU.mult, ALU.min))
                v.tensor_tensor(cb[5], cb[4], nm(4), ALU.subtract)
                v.tensor_tensor(cb[6], sinks_b, cb[4], ALU.add).then_inc(comb_d, 1)

            def window_over_total():
                dve.wait_ge(comb_a, 2)
                link(v.tensor_tensor(cb[4], cb[5], tot(4), ALU.mult))
                link(v.tensor_tensor(cb[4], cb[4], cb[6], ALU.add))
                link(v.reciprocal(cb[4], cb[4]))
                link(v.tensor_tensor(cb[5], cb[5], cb[4], ALU.mult))
                scaled(4, cb[5])
                gate_branch(2, 4)

            dve.wait_ge(bias_full[4], 16)
            project_and_attend(6, "last", 32, table(0), {
                0: full_over_total, 2: first_gate, 4: dilation_weights, 5: lambda: add_dilation(2)})
            last_gate()
            for i in range(3):
                split_banks(oT_hi, oT_lo, 4 * (i % 2), 4, turn_banks)
                for half in range(2):
                    step = 2 * i + half
                    for _ in range(2):
                        slot_step()
                    if step == 0:
                        window_over_total()
                    if step == 5:
                        split_banks(oT_hi, oT_lo, 4, 4, turn_banks)
                    slot_step()
                    n.exps += 1
                    dve.wait_ge(gate_exp, n.exps)
                    dve.wait_ge(acc_read, 68 + 4 * step)
                    m = merged[:, :, 512 * half:512 * half + 512]
                    if i == 0:
                        v.tensor_tensor(m, square[:, :, :], branch_out, ALU.mult).then_inc(gated, 1)
                    else:
                        link(v.tensor_tensor(branch_out, square[:, :, :], branch_out, ALU.mult))
                        v.tensor_tensor(m, m, branch_out, ALU.add).then_inc(gated, 1)
            slot_step()
            split_banks(oT_hi, oT_lo, 0, 4, pair_banks)
            for left in (3, 2, 1):
                slot_step(ahead_exists=left > 2)
            add_projection()


def shape_constants():
    f = np.float32
    p, j = np.arange(P)[:, None], np.arange(S)[None, :]
    strict = np.where(j < P + p, 0.0, MASKED).astype(f)
    keep = (j < P + p).astype(f)
    chunk = np.where(j // 64 <= (P + p) // 64, 0.0, MASKED).astype(f)
    inv_freq = (np.float32(10000.0) ** (-np.arange(0, 32, 2, dtype=f) / np.float32(32))).astype(f)
    ang = (np.arange(S, dtype=f)[:, None] * inv_freq[None, :]).astype(f)
    rope = np.stack([np.cos(ang), np.sin(ang)], 1).astype(f)
    rope = np.ascontiguousarray(rope.reshape(TB, P, 2, 16).transpose(1, 0, 2, 3))
    dist = np.arange(REL) - (P - 1)
    d0 = np.maximum(dist, 0)
    ratio = np.log(np.maximum(d0, 1).astype(f) / f(16)) / f(math.log(2048 / 16))
    large = np.minimum(16 + (ratio * f(16)).astype(np.int32), 31)
    bucket = np.where(d0 < 16, d0, large)
    onehot = (bucket[None, :] == np.arange(32)[:, None]).astype(f)
    ok = [dist >= 0] + [(dist >= 0) & (dist <= w) & (dist % d == 0) for w, d in ((128, 1), (512, 4), (2048, 16))] \
        + [(dist >= 0) & (dist < 128)]
    dist_mask = np.repeat(np.where(np.stack(ok), 0.0, MASKED).astype(f), 8, axis=0)
    return dict(identity=np.eye(P, dtype=f), strict_mask=strict, chunk_mask=np.ascontiguousarray(chunk[:, ::-1]), keep_mask=keep, rope=rope,
                bucket_onehot=onehot, dist_mask=dist_mask)


def kernel(**inputs):
    import numpy as np
    import concourse.bacc as bacc
    from concourse import mybir
    from concourse.bass_utils import run_bass_kernel_spmd

    first = {"w_in0": "ev_w_in", "g_cq": "ev_g_cq", "w_uq": "ev_w_uq", "g_ckv": "ev_g_ckv", "w_ukv": "ev_w_ukv",
             "w_out0": "ev_w_out", "w_qkv": "od_w_qkv", "rel_band": "od_rel_bias", "w_out1": "od_w_out",
             "g_ln2": "ln_g_2", "w_in2": "w_in_2", "qk_g": "qk_g_2", "sinks": "sinks_2", "w_branch": "w_branch_2",
             "w_out2": "w_out_2"}
    plain = {"x": "x", "g_mix": "g_mix", "g_ffn": "g_ffn", "w_gate": "w_gate", "w_up": "w_up", "w_down": "w_down",
             "g_final": "g_final", "rel_bias2": "rel_bias_2"}
    arrays = {k: np.ascontiguousarray(inputs[v])[0] for k, v in first.items()}
    arrays.update({k: np.ascontiguousarray(inputs[v]) for k, v in plain.items()})
    arrays.update(shape_constants())

    nc = bacc.Bacc("TRN2", target_bir_lowering=False, num_devices=1)
    aps = {k: nc.dram_tensor(f"in_{k}", a.shape, mybir.dt.from_np(a.dtype), kind="ExternalInput").ap()
           for k, a in arrays.items()}
    out = nc.dram_tensor("out_y", (1, S, D), mybir.dt.float32, kind="ExternalOutput").ap()
    build_program(nc, out=out, **aps)
    r = run_bass_kernel_spmd(nc, [{f"in_{k}": a for k, a in arrays.items()}], core_ids=[0])
    return r.results[0]["out_y"]
```

```python
import math
from contextlib import ExitStack

import numpy as np

import concourse.bass as bass
from concourse import mybir

P = 128
TB = 2
S = TB * P
D = 1024
KT = D // P
FF = 2816
FT = 256
NF = FF // FT
UNIT = 2048
RING = 3
HD = 64
MLA_QK = 96
BR = 512
REL = 383
MASKED = -1e30
EPS = 1e-6
HEAD0 = (0, 8, 32)
MIX0, CQ, CKV, FFN0, MIX1, FFN1, FINAL, LN2 = range(8)
GAIN_COL = {MIX0: 0, MIX1: 8, FFN0: 16, FFN1: 24, LN2: 32, CQ: 40, CKV: 43, FINAL: 51}
QK_COL = 45
GAIN_ROWS = GAIN_COL[FINAL] + 8
TABLES = 10 * 16
CONSTS = 7 * 16
LN_EXP_TABLES = 6


class Ordinals:

    def __init__(self):
        self.unit = 0
        self.slot = 0
        self.chunk = 0
        self.pair = 0
        self.turn = 0
        self.bank = 0
        self.proj = 0
        self.written = 0

    def next_unit(self):
        self.unit = self.unit + 1
        self.slot = (self.slot + 1) % RING


def build_program(nc, x, w_in0, g_cq, w_uq, g_ckv, w_ukv, w_out0, w_qkv, rel_band, w_out1, g_mix, g_ffn,
                  w_gate, w_up, w_down, g_final, g_ln2, w_in2, qk_g, sinks, w_branch, w_out2, rel_bias2,
                  identity, strict_mask, chunk_mask, keep_mask, rope, bucket_onehot, dist_mask, out):
    f32, f32r = mybir.dt.float32, mybir.dt.float32r
    ALU, ACT, AX = mybir.AluOpType, mybir.ActivationFunctionType, mybir.AxisListType

    rel_rows = nc.dram_tensor("rel_rows", [40, REL], f32, kind="Internal").ap()

    ctx = ExitStack()
    with ctx:
        def sb(name, shape, dt=f32):
            return ctx.enter_context(nc.sbuf_tensor(name, shape, dt))

        def sem(name):
            return ctx.enter_context(nc.semaphore(name))

        h = sb("h", [P, TB, D])
        uT_hi = sb("uT_hi", [P, KT, S], f32r)
        uT_lo = sb("uT_lo", [P, KT, S], f32r)
        oT_hi = sb("oT_hi", [P, KT, S], f32r)
        oT_lo = sb("oT_lo", [P, KT, S], f32r)
        w_raw = sb("w_raw", [P, RING, UNIT])
        w_hi = sb("w_hi", [P, RING, UNIT], f32r)
        w_lo = sb("w_lo", [P, RING, UNIT], f32r)
        bias = sb("bias", [P, 4, 8, S])
        qkv = sb("qkv", [P, 3, TB, BR])
        qkT = sb("qkT", [P, 4, 512])
        logit = sb("logit", [P, 3, 2, 384])
        prT = sb("prT", [P, 2, 2, 384])
        heads = sb("heads", [P, TB, 40, HD])
        square = sb("square", [P, TB, BR])
        square_flat = square[:, :, :].rearrange("p b c -> p (b c)")
        ident = sb("ident", [P, P])
        m_chunk = sb("m_chunk", [P, S])
        cs = sb("cs", [P, TB, 2, 16])
        g_col = sb("g_col", [P, 10])
        g_now = sb("g_now", [P, 2])
        gain_T = sb("gain_T", [P, GAIN_ROWS])
        norms = sb("norms", [P, 8, 8, TB])
        sink = sb("sink", [P, 8])
        eps = sb("eps", [P, 1])
        stat = sb("stat", [P, 5, 16])
        negmax8 = sb("negmax8", [P, TB, 8])
        total8 = sb("total8", [P, TB, 8])
        negmax = sb("negmax", [P, TB, 40])
        total = sb("total", [P, TB, 40])
        rtotal = sb("rtotal", [P, TB, 2])
        comb = sb("comb", [P, 8, TB, 8])
        tabT = sb("tabT", [32, 40])

        flat_bias = bias[:, :, :, :].rearrange("p a b c -> p (a b c)")
        flat_heads = heads[:, :, :, :].rearrange("p a b c -> p (a b c)")
        flat_qkv = qkv[:, :, :, :].rearrange("p a b c -> p (a b c)")
        flat_logit = logit[:, :, :, :].rearrange("p a b c -> p (a b c)")
        u = flat_qkv[:, 0:TB * D].rearrange("p (b c) -> p b c", b=TB)
        merged = u
        gain = flat_qkv[:, 2048:3072]
        hid_e = flat_qkv[:, 0:512].rearrange("p (b c) -> p b c", b=TB)
        hid_g = flat_qkv[:, 512:1024].rearrange("p (b c) -> p b c", b=TB)
        hid = flat_qkv[:, 1024:1536].rearrange("p (b c) -> p b c", b=TB)
        sb_tmp = [flat_bias[:, 2048 + 768 * i:2816 + 768 * i].rearrange("p (j c) -> p j c", j=2) for i in range(3)]
        qkT_odd = flat_bias[:, 4352:6400].rearrange("p (t c) -> p t c", t=4)
        k_rot = flat_bias[:, 6400:6464].rearrange("p (b c) -> p b c", b=TB)
        k_rot2 = flat_bias[:, 6464:6528].rearrange("p (b c) -> p b c", b=TB)
        cq = flat_bias[:, 6528:7296].rearrange("p (b c) -> p b c", b=TB)
        ckv = flat_bias[:, 7296:7808].rearrange("p (b c) -> p b c", b=TB)
        q_mla = flat_heads[:, 0:1536].rearrange("p (b n c) -> p b n c", b=TB, c=MLA_QK)
        k_mla = flat_heads[:, 1536:3072].rearrange("p (b n c) -> p b n c", b=TB, c=MLA_QK)
        v_mla = flat_heads[:, 3072:4096].rearrange("p (b c) -> p b c", b=TB)
        swish = flat_bias[:, 2048:5120].rearrange("p (i b c) -> p i b c", i=3, b=TB)
        branch_out = flat_logit[:, 0:1024].rearrange("p (b c) -> p b c", b=TB)
        gain_rows = flat_logit[0:GAIN_ROWS, 0:P]
        tab = flat_logit[0:40, P:P + 32]
        cs_t = flat_heads[:, 4096:4608].rearrange("p (i n c) -> p i n c", i=4, c=16)
        m_strict = flat_heads[:, 4608:4864]
        m_keep = flat_heads[:, 4864:5120]
        onehot = flat_heads[0:32, 1792:1792 + REL]
        rel_f = flat_heads[0:40, 0:REL]
        dist_m = flat_heads[0:40, 384:384 + REL]

        acc = [ctx.enter_context(nc.psum_tensor(f"acc{i}", [P, 512], f32)) for i in range(4)]
        pair_ps = ctx.enter_context(nc.psum_tensor("pair_ps", [P, 2, 512], f32))
        turn_ps = ctx.enter_context(nc.psum_tensor("turn_ps", [P, 2, 512], f32))
        qkT_ps, out_ps = acc[2], acc[3]
        turn_banks = [turn_ps[:, 0, :], turn_ps[:, 1, :]]
        pair_banks = [pair_ps[:, 0, :], pair_ps[:, 1, :]]
        acc_banks = [acc[0][:, :], acc[1][:, :]]
        stream_banks = {norm: acc_banks + pair_banks if norm in (FFN0, FFN1) else turn_banks + pair_banks
                        for norm in (MIX0, FFN0, MIX1, FFN1, LN2)}
        qk_banks = [qkT_ps[:, :]] + acc_banks
        latent_banks = [acc[2][:, :]] + acc_banks

        x_loaded = sem("x_loaded")
        tables = sem("tables")
        tables_T = sem("tables_T")
        gains_set = sem("gains_set")
        gains_merged = sem("gains_merged")
        consts = sem("consts")
        row_scale = sem("row_scale")
        raw_full = [sem(f"raw_full{i}") for i in range(RING)]
        hi_done = sem("hi_done")
        lo_done = sem("lo_done")
        unit_used = sem("unit_used")
        blk0_done = sem("blk0_done")
        acc_read = sem("acc_read")
        turned = sem("turned")
        turned_hi = sem("turned_hi")
        turned_lo = sem("turned_lo")
        squared = sem("squared")
        root = sem("root")
        act_self = sem("act_self")
        dve_self = sem("dve_self")
        h_ready = sem("h_ready")
        u_ready = sem("u_ready")
        gain_full = sem("gain_full")
        summed = sem("summed")
        qk_ready = sem("qk_ready")
        qkT_done = sem("qkT_done")
        qkT_read = sem("qkT_read")
        logit_done = sem("logit_done")
        logit_read = sem("logit_read")
        max_done = sem("max_done")
        prob_done = sem("prob_done")
        sb_read = sem("sb_read")
        sb_abs = sem("sb_abs")
        prT_done = sem("prT_done")
        prT_act = sem("prT_act")
        prT_dve = sem("prT_dve")
        normed = sem("normed")
        out_done = sem("out_done")
        out_hi = sem("out_hi")
        out_read = sem("out_read")
        proj_done = sem("proj_done")
        eps_set = sem("eps_set")
        swish_done = sem("swish_done")
        gated = sem("gated")
        gate_exp = sem("gate_exp")
        tab_done = sem("tab_done")
        rel_ready = sem("rel_ready")
        rel_stored = sem("rel_stored")
        band_full = sem("band_full")
        band_ready = sem("band_ready")
        bias_full = [sem(f"bias_full{i}") for i in range(5)]
        comb_d = sem("comb_d")
        comb_a = sem("comb_a")
        stored = sem("stored")

        def since(e, s, v):
            if isinstance(v, int) and v <= 0:
                return
            e.wait_ge(s, v)

        def key_cols(blk):
            return (slice(0, 128), slice(128, 256)) if blk == 0 else (slice(128, 384), slice(0, 256))

        def back(cols):
            return slice(S - cols.stop, S - cols.start)

        block = ctx.enter_context(nc.Block())

        @block.sync
        def _(sp):
            n = Ordinals()
            for blk in range(TB):
                sp.dma_start(h[:, blk, :], x[0].rearrange("(b p) c -> p b c", p=P)[:, blk, :]).then_inc(x_loaded, 16)

            def load(parts):
                since(sp, lo_done, n.unit - (RING - 1))
                for dst, src in parts:
                    sp.dma_start(dst, src).then_inc(raw_full[n.slot], 32 // len(parts))
                n.next_unit()

            def rows(w, kt0, nkt, cols):
                return w[kt0 * P:(kt0 + nkt) * P, cols].rearrange("(k p) c -> p k c", p=P)

            def view(nkt, width):
                return w_raw[:, n.slot, 0:nkt * width].rearrange("p (k c) -> p k c", k=nkt)

            def chunk_units(w, nkt, cols, width):
                for kt0 in range(0, nkt, 4):
                    m = min(4, nkt - kt0)
                    load([(view(m, width), rows(w, kt0, m, cols))])

            def proj_units(w, order=(0, 2, 4, 6)):
                for kt0 in order:
                    load([(view(2, D), rows(w, kt0, 2, slice(0, D)))])

            def step_units(layer, c):
                for kt0 in (0, 4):
                    v = view(4, 2 * FT)
                    load([(v[:, :, 0:FT], rows(w_gate[layer], kt0, 4, bass.ds(c * FT, FT))),
                          (v[:, :, FT:2 * FT], rows(w_up[layer], kt0, 4, bass.ds(c * FT, FT)))])

            def down_unit(layer, c):
                src = w_down[layer][bass.ds(c * FT, FT), :].rearrange("(k p) c -> p k c", p=P)
                load([(view(2, D), src)])

            def swiglu_units(layer):
                step_units(layer, 0)
                step_units(layer, 1)
                down_unit(layer, 0)
                u0 = n.unit
                with sp.Fori(2, NF) as c:
                    n.unit = u0 + (c - 2) * 3
                    step_units(layer, c)
                    down_unit(layer, c - 1)
                n.unit = u0 + 3 * (NF - 2)
                down_unit(layer, NF - 1)

            sp.wait_ge(tables, TABLES)
            for i in range(3):
                chunk_units(w_in0, KT, slice(672 + 512 * i, 1184 + 512 * i), 512)
            chunk_units(w_in0, KT, slice(0, 384), 384)
            chunk_units(w_in0, KT, slice(384, 672), 288)
            for i in range(2):
                chunk_units(w_uq, 3, slice(384 * i, 384 * i + 384), 384)
            for i in range(2):
                chunk_units(w_ukv, 2, slice(512 * i, 512 * i + 512), 512)
            proj_units(w_out0, (4, 6, 0, 2))
            swiglu_units(0)
            for g in range(2):
                for i in range(3):
                    chunk_units(w_qkv, KT, slice(1024 * i + 512 * g, 1024 * i + 512 * g + 512), 512)
            proj_units(w_out1)
            swiglu_units(1)
            for i in range(3):
                chunk_units(w_in2, KT, slice(512 * i, 512 * i + 512), 512)
            u0 = n.unit
            with sp.Fori(0, 3) as g:
                n.unit = u0 + g * 6
                for i in range(3):
                    chunk_units(w_in2, KT, bass.ds(g * BR + (2048 + 1536 * i), BR), 512)
            n.unit = u0 + 18
            chunk_units(w_in2, KT, slice(7168, 7680), 512)
            chunk_units(w_in2, KT, slice(1536, 2048), 512)
            chunk_units(w_in2, KT, slice(7680, 7936), 256)
            for c0 in (6656, 7936):
                chunk_units(w_in2, KT, slice(c0, c0 + 512), 512)
            for i in range(3):
                for half in range(2):
                    c0 = 8448 + D * i + 512 * half
                    chunk_units(w_in2, KT, slice(c0, c0 + 512), 512)
                    chunk_units(w_branch[i], 4, slice(512 * half, 512 * half + 512), 512)
            proj_units(w_out2)
            for blk in range(TB):
                sp.wait_ge(h_ready, 11 + blk)
                sp.dma_start(out[0].rearrange("(b p) c -> p b c", p=P)[:, blk, :], h[:, blk, :]).then_inc(stored, 16)
            sp.wait_ge(stored, 16 * TB)

        @block.gpsimd
        def _(pool):
            pool.memset(eps[:, :], EPS).then_inc(eps_set, 1)
            for dst, src in ((onehot[:, :], bucket_onehot), (dist_m, dist_mask),
                             (m_strict[:, :], strict_mask), (m_keep[:, :], keep_mask),
                             (m_chunk[:, :], chunk_mask), (cs[:, :, :, :], rope),
                             (sink[:, :], sinks.partition_broadcast(P))):
                pool.dma_start(dst, src).then_inc(consts, 16)
            pool.wait_ge(rel_ready, 1)
            pool.dma_start(rel_rows[0:40, :], rel_f).then_inc(rel_stored, 16)

            def windows(rows, first, width, count):
                return bass.AP(rows.tensor, first, [[1, P], [width, count], [1, S]])

            pool.wait_ge(h_ready, 2)
            pool.dma_start(bias[:, 2:4, :, :], windows(rel_band, 256 - (P - 1), 513, 16)).then_inc(band_full, 16)
            pool.wait_ge(band_full, 16)
            band = bias[:, 2:4, :, :].rearrange("p a b c -> p (a b) c")
            pool.tensor_tensor(band, band, m_chunk[:, :].unsqueeze(1).broadcast_to([P, 16, S]),
                               ALU.add).then_inc(band_ready, 1)
            pool.wait_ge(rel_stored, 16)
            pool.wait_ge(h_ready, 6)
            pool.dma_start(gain, g_final.partition_broadcast(P)).then_inc(gain_full, 16)
            for g in range(4):
                pool.dma_start(bias[:, g, :, :], windows(rel_rows, 8 * g * REL, REL, 8)).then_inc(bias_full[g], 16)
            pool.wait_ge(max_done, 20)
            pool.dma_start(bias[:, 0, :, :], windows(rel_rows, 32 * REL, REL, 8)).then_inc(bias_full[4], 16)
            pool.wait_ge(bias_full[4], 16)

        @block.tensor
        def _(pe):
            n = Ordinals()
            n.h, n.fresh = 0, None
            mm, transpose = nc.tensor.matmul, nc.tensor.transpose

            def tokens(blk):
                return slice(blk * P, blk * P + P)

            def unit_parts(nkt, width):
                return [w[:, n.slot, 0:nkt * width].rearrange("p (k c) -> p k c", k=nkt) for w in (w_hi, w_lo)]

            def half_unit(o, x_hi, x_lo, kts, parts, blk, first, last):
                wh, wl = parts
                for k, kt in enumerate(kts):
                    if n.fresh is not None and blk == 0 and kt % 2 == 0:
                        pe.wait_ge(turned_lo, n.fresh + kt // 2 + 1)
                    xh, xl = x_hi[:, kt, tokens(blk)], x_lo[:, kt, tokens(blk)]
                    mm(o, xh, wh[:, k, :], start=first and k == 0, stop=False)
                    mm(o, xh, wl[:, k, :], start=False, stop=False)
                    done = mm(o, xl, wh[:, k, :], start=False, stop=last and k == len(kts) - 1)
                if blk == 0 and kt == KT - 1:
                    n.fresh = None
                return done

            def chunk_unit(x_hi, x_lo, kts, width, first, last, between=None):
                pe.wait_ge(lo_done, n.unit + 1)
                parts = unit_parts(len(kts), width)
                for blk in range(TB):
                    if between:
                        between(blk)
                    if first:
                        since(pe, acc_read, n.chunk * 2 + (blk - 1))
                    done = half_unit(acc[blk][:, 0:width], x_hi, x_lo, kts, parts, blk, first, last)
                    if blk == 0 and last:
                        done.then_inc(blk0_done, 1)
                done.then_inc(unit_used, 1)
                n.next_unit()
                if last:
                    n.chunk = n.chunk + 1

            def chunk(x_hi, x_lo, nkt, width, x_kt=0):
                for k0 in range(0, nkt, 4):
                    m = min(4, nkt - k0)
                    chunk_unit(x_hi, x_lo, range(x_kt + k0, x_kt + k0 + m), width, k0 == 0, k0 + m == nkt)

            def proj_half(kts, blk, first, last, ahead=0):
                slot = (n.slot + ahead) % RING
                if blk == 0:
                    pe.wait_ge(lo_done, n.unit + (ahead + 1))
                wh, wl = [w[:, slot, :].rearrange("p (k c) -> p k c", k=2) for w in (w_hi, w_lo)]
                for k, kt in enumerate(kts):
                    xh, xl = oT_hi[:, kt, tokens(blk)], oT_lo[:, kt, tokens(blk)]
                    for i, (xp, wp) in enumerate(((xh, wh), (xh, wl), (xl, wh))):
                        for half in range(2):
                            done = mm(acc[2 * blk + half][:, :], xp, wp[:, k, 512 * half:512 * half + 512],
                                      start=first and k == 0 and i == 0, stop=last and k == 1 and i == 2)
                if blk == 0 and last:
                    done.then_inc(proj_done, 1)
                if blk == 1:
                    done.then_inc(unit_used, 1)
                    n.next_unit()

            def proj_unit(kts, first, last):
                for blk in range(TB):
                    proj_half(kts, blk, first, last)

            def turn(tile, nkt, banks):
                for k in range(nkt):
                    for blk in range(TB):
                        c0 = (k % 2) * S + blk * P
                        done = transpose(banks[k // 2][:, c0:c0 + P], tile(k, blk), ident[:, :])
                    if k % 2 or k == nkt - 1:
                        done.then_inc(turned, 1)
                        n.bank = n.bank + 1

            def turn_stream(norm):
                for blk in range(TB):
                    if n.h == 0:
                        pe.wait_ge(x_loaded, 16 * TB)
                    else:
                        pe.wait_ge(h_ready, n.h - TB + blk + 1)
                    for kt in range(KT):
                        c0 = (kt % 2) * S + blk * P
                        done = transpose(stream_banks[norm][kt // 2][:, c0:c0 + P], h[:, blk, P * kt:P * kt + P], ident[:, :])
                        if blk == 1 and kt % 2:
                            done.then_inc(turned, 1)
                n.fresh = n.bank
                n.bank = n.bank + 4
                n.h += TB

            def turn_pair(kind, t, banks=(0,)):
                per = 2 if kind == "mla" else 1
                for j in range(per):
                    qkT_ps = qk_banks[banks[(per * t + j) % len(banks)]]
                    since(pe, qkT_read, n.turn - min(per * t + j, len(banks) - 1))
                    for i in range(4):
                        blk = i % 2
                        src = (q_mla, k_mla)[i // 2][:, blk, 2 * t + j, :] if kind == "mla" else \
                            qkv[:, i // 2, blk, P * t:P * t + P]
                        done = transpose(qkT_ps[0:src.shape[1], P * i:P * i + P], src, ident[:, :])
                    done.then_inc(qkT_done, 1)
                    n.turn = n.turn + 1

            def logits(kind, t, pair0, turn0):
                per = 2 if kind == "mla" else 1
                pe.wait_ge(qkT_read, turn0 + per * (t + 1))
                since(pe, logit_read, pair0 + t)
                for j in range(2):
                    src = (qkT, qkT_odd)[j][0:MLA_QK, t, :] if kind == "mla" else qkT[HD * j:HD * j + HD, t, :]
                    mm(pair_ps[:, j, 0:128], src[:, 0:128], src[:, 256:384], start=True, stop=True)
                    done = mm(pair_ps[:, j, 128:384], src[:, 128:256], src[:, 256:512], start=True, stop=True)
                done.then_inc(logit_done, 1)

            def turn_probs(kind, t, pair0):
                if kind == "mla" or kind == "band":
                    pe.wait_ge(normed, pair0 + (t + 1) - 4)
                else:
                    pe.wait_ge(prob_done, pair0 + (t + 1))
                since(pe, prT_act, pair0 + t)
                since(pe, prT_dve, pair0 + t)
                for j in range(2):
                    for i in range(3):
                        done = transpose(turn_ps[:, j, P * i:P * i + P], logit[:, t % 3, j, P * i:P * i + P],
                                         ident[:, :])
                done.then_inc(prT_done, 1)

            def values(kind, t, pair0):
                pe.wait_ge(prT_act, pair0 + (t + 1))
                pe.wait_ge(prT_dve, pair0 + (t + 1))
                since(pe, out_read, pair0 + t)
                for j in range(2):
                    c0 = P * t + HD * j
                    v0, v1 = [(v_mla[:, blk, c0:c0 + HD] if kind == "mla" else qkv[:, 2, blk, c0:c0 + HD])
                              for blk in range(TB)]
                    pr = prT[:, t % 2, j, :]
                    if kind != "last":
                        o = out_ps[HD * j:HD * j + HD, 0:S]
                        mm(o[:, 0:128], v0, pr[:, 0:128], start=True, stop=True)
                        mm(o[:, 128:256], v0, pr[:, 128:256], start=True, stop=False)
                        done = mm(o[:, 128:256], v1, pr[:, 256:384], start=False, stop=True)
                        continue
                    o0, o1 = out_ps[:, HD * j:HD * j + HD], out_ps[:, P + HD * j:P + HD * j + HD]
                    mm(o0, pr[:, 0:128], v0, start=True, stop=True)
                    mm(o1, pr[:, 128:256], v0, start=True, stop=False)
                    done = mm(o1, pr[:, 256:384], v1, start=False, stop=True)
                done.then_inc(out_done, 1)

            def attention_step(kind, s, pair0, turn0, lag=1):
                if s < 4:
                    logits(kind, s, pair0, turn0)
                if lag <= s < 4 + lag:
                    turn_probs(kind, s - lag, pair0)
                if lag < s:
                    values(kind, s - lag - 1, pair0)

            def group_ready(qk, copied):
                pe.wait_ge(qk_ready, qk)
                pe.wait_ge(acc_read, copied)

            def attend(kind, order):
                pair0, turn0 = n.pair, n.turn
                for s in range(7):
                    if s < 2:
                        turn_pair(kind, 2 * s, (0, 1, 2))
                        turn_pair(kind, 2 * s + 1, (0, 1, 2))
                    attention_step(kind, s, pair0, turn0, lag=2)
                    if s == 3:
                        proj_half((order[0], order[0] + 1), 0, True, False)
                    if s == 5:
                        proj_half((order[1], order[1] + 1), 0, False, False, ahead=1)
                n.pair = pair0 + 4
                pe.wait_ge(out_read, n.pair)
                for i, k0 in enumerate(order[0:2]):
                    proj_half((k0, k0 + 1), 1, i == 0, False)
                for i, k0 in enumerate(order[2:4]):
                    proj_unit((k0, k0 + 1), False, i == 1)

            def project(widths):
                for width in widths:
                    chunk(uT_hi, uT_lo, KT, width)

            def project_and_attend(widths, kind, qk, copied, to=6):
                pair0, turn0 = n.pair, n.turn
                s = 0
                for width in widths:
                    for k0 in (0, 4):
                        def between(blk, s=s):
                            if s == 0 and blk == 1:
                                group_ready(qk, copied)
                                turn_pair(kind, 0)
                            if s == 1:
                                turn_pair(kind, 1 + blk)
                            if s == 5 and blk == 1:
                                attention_step(kind, 5, pair0, turn0)
                        chunk_unit(uT_hi, uT_lo, range(k0, k0 + 4), width, k0 == 0, k0 == 4, between)
                        if s == 1:
                            turn_pair(kind, 3)
                        if kind == "sb" and s == 3:
                            turn_probs(kind, 2, pair0)
                            values(kind, 1, pair0)
                            pe.wait_ge(acc_read, 10)
                            turn(lambda k, blk: cq[:, blk, P * k:P * k + P], 3, latent_banks)
                            turn(lambda k, blk: ckv[:, blk, P * k:P * k + P], 2, latent_banks[2:])
                            logits(kind, 3, pair0, turn0)
                        elif s < 5:
                            attention_step(kind, s, pair0, turn0)
                        s += 1
                for s in range(s, to):
                    attention_step(kind, s, pair0, turn0)
                n.pair = pair0 + 4

            def swiglu():
                n0, b0 = n.written, n.bank

                def step_unit(c, k0):
                    pe.wait_ge(lo_done, n.unit + 1)
                    step_ps = turn_ps if isinstance(c, int) and c == 0 else pair_ps
                    if k0 == 0 and not (isinstance(c, int) and c < 2):
                        pe.wait_ge(u_ready, n0 + c)
                    parts = unit_parts(4, 2 * FT)
                    for blk in range(TB):
                        done = half_unit(step_ps[:, blk, :], uT_hi, uT_lo, range(k0, k0 + 4), parts, blk,
                                         k0 == 0, k0 == 4)
                    done.then_inc(unit_used, 1)
                    n.next_unit()

                def turn_hidden(c):
                    pe.wait_ge(u_ready, n0 + c + 1)
                    since(pe, turned_lo, b0 + c)
                    turn(lambda k, blk: hid[:, blk, P * k:P * k + P], 2, turn_banks)

                def down(c, first, last):
                    pe.wait_ge(turned_lo, b0 + c + 1)
                    proj_unit((0, 1), first, last)

                def step(c, first):
                    step_unit(c, 0)
                    turn_hidden(c - 1)
                    step_unit(c, 4)
                    down(c - 1, first, False)

                step_unit(0, 0)
                step_unit(0, 4)
                step(1, True)
                u0 = n.unit
                with pe.Fori(2, NF) as c:
                    n.unit = u0 + (c - 2) * 3
                    step(c, False)
                n.unit = u0 + 3 * (NF - 2)
                turn_hidden(NF - 1)
                down(NF - 1, False, True)
                n.written, n.bank = n0 + NF, b0 + NF

            pe.wait_ge(tables, TABLES)
            transpose(acc[3][:, 0:GAIN_ROWS], gain_rows, ident[0:GAIN_ROWS, 0:GAIN_ROWS])
            transpose(acc[3][0:32, 64:104], tab, ident[0:40, 0:40]).then_inc(tables_T, 1)
            turn_stream(MIX0)
            project((512, 512))
            pe.wait_ge(consts, CONSTS)
            pe.wait_ge(gains_set, 2)
            mm(acc[2][0:40, 0:REL], tabT[:, :], onehot[:, :], start=True, stop=True).then_inc(tab_done, 1)
            project((512,))
            pe.wait_ge(rel_ready, 1)
            pair0, turn0 = n.pair, n.turn
            project_and_attend((384, 288), "sb", 0, 6, to=4)
            pe.wait_ge(turned_lo, n.bank)
            for s in (4, 5):
                chunk(uT_hi, uT_lo, 3, 384)
                attention_step("sb", s, pair0, turn0)
            for _ in range(2):
                chunk(uT_hi, uT_lo, 2, 512, x_kt=3)
            group_ready(1, 18)
            pe.wait_ge(out_read, n.pair)
            attend("mla", (4, 6, 0, 2))
            turn_stream(FFN0)
            swiglu()
            turn_stream(MIX1)
            project((512, 512, 512))
            project_and_attend((512, 512, 512), "band", 1, 24)
            group_ready(1, 30)
            pe.wait_ge(out_read, n.pair)
            attend("band", (0, 2, 4, 6))
            turn_stream(FFN1)
            swiglu()
            turn_stream(LN2)
            project((512, 512, 512))
            u0, c0, p0, t0 = n.unit, n.chunk, n.pair, n.turn
            with pe.Fori(0, 3) as g:
                n.unit, n.chunk, n.pair, n.turn = u0 + g * 6, c0 + g * 3, p0 + g * 4, t0 + g * 4
                project_and_attend((512, 512, 512), "last", g * 2 + 3, g * 6 + 36)
            n.unit, n.chunk, n.pair, n.turn = u0 + 18, c0 + 9, p0 + 12, t0 + 12
            project_and_attend((512, 512, 256), "last", 9, 54)
            project_and_attend((512, 512, 512), "last", 11, 60)

            def merged_tile(kt0):
                return lambda k, blk: merged[:, blk, P * (kt0 + k):P * (kt0 + k) + P]
            for i in range(3):
                n.written += 1
                pe.wait_ge(u_ready, n.written)
                o = heads[:, :, HEAD0[i]:HEAD0[i] + 8, :].rearrange("p b n d -> p b (n d)")
                turn(lambda k, blk: o[:, blk, P * k:P * k + P], 4, turn_banks)
                for half in range(2):
                    if i or half:
                        chunk(uT_hi, uT_lo, KT, 512)
                    pe.wait_ge(turned_lo, n.bank)
                    if i == 2 and half == 1:
                        pe.wait_ge(gated, 5)
                        turn(merged_tile(0), 4, turn_banks)
                    chunk(oT_hi, oT_lo, 4, 512, x_kt=4 * (i % 2))
            pe.wait_ge(acc_read, n.chunk * 2)
            pe.wait_ge(turned_lo, n.bank)
            proj_unit((4, 5), True, False)
            pe.wait_ge(gated, 6)
            turn(merged_tile(4), 4, pair_banks)
            proj_unit((6, 7), False, False)
            pe.wait_ge(turned_lo, n.bank)
            proj_unit((0, 1), False, False)
            proj_unit((2, 3), False, True)

        @block.scalar
        def _(act):
            n = Ordinals()
            own = [0]
            activation = nc.scalar.activation

            def gain_row(norm, count):
                return gain_rows[GAIN_COL[norm]:GAIN_COL[norm] + count, :]
            small = [(ident[:, :], identity),
                     (gain_row(MIX0, 16), g_mix.rearrange("l (k p) -> (l k) p", p=P)),
                     (gain_row(FFN0, 16), g_ffn.rearrange("l (k p) -> (l k) p", p=P)),
                     (gain_row(LN2, 8), g_ln2.rearrange("(k p) -> k p", p=P)),
                     (gain_row(FINAL, 8), g_final.rearrange("(k p) -> k p", p=P)),
                     (gain_row(CQ, 3), g_cq.rearrange("(k p) -> k p", p=P)),
                     (gain_row(CKV, 2), g_ckv.rearrange("(k p) -> k p", p=P)),
                     (gain_rows[QK_COL:QK_COL + 6, 0:HD], qk_g), (gain_rows[QK_COL:QK_COL + 6, HD:P], qk_g),
                     (tab, rel_bias2)]
            for dst, src in small:
                act.dma_start(dst, src).then_inc(tables, 16)

            act.add_instruction(mybir.InstLoadActFuncSet(
                name=nc.get_next_instruction_name(), engine=mybir.EngineType.Activation,
                act_func_set_id=LN_EXP_TABLES, ins=[], outs=[]))

            def link(ins):
                own[0] = own[0] + 1
                ins.then_inc(act_self, 1)
                act.wait_ge(act_self, own[0])

            def round_unit(ahead=2, width=UNIT):
                slot = (n.slot + ahead) % RING
                act.wait_ge(raw_full[slot], raw_target(n, ahead))
                since(act, unit_used, n.unit + ahead - (RING - 1))
                activation(w_hi[:, slot, 0:width], w_raw[:, slot, 0:width], ACT.Copy).then_inc(hi_done, 1)

            def raw_target(n, ahead):
                return n.raw_base + ((n.raw_local + ahead) // RING + 1) * 32

            def slot_step(width=UNIT, ahead_exists=True):
                if ahead_exists:
                    round_unit(2, width)
                n.next_unit()
                n.raw_local += 1

            def at_loop(u0, local0, trips_expr, units):
                n.unit = u0 + trips_expr * units
                n.raw_base, n.raw_local = trips_expr * (32 * units // RING), local0

            n.raw_base, n.raw_local = 0, 0

            def split_banks(dst, kt0, nkt, banks, norm=None):
                for k0 in range(0, nkt, 2):
                    m = min(2, nkt - k0)
                    act.wait_ge(turned, n.bank + 1)
                    if norm is None:
                        done = activation(dst[:, kt0 + k0:kt0 + k0 + m, :].rearrange("p k t -> p (k t)"),
                                          banks[k0 // 2][:, 0:m * S], ACT.Copy)
                    else:
                        for k in range(k0, k0 + m):
                            c = GAIN_COL[norm] + k
                            done = activation(dst[:, kt0 + k, :], banks[k0 // 2][:, (k - k0) * S:(k - k0 + 1) * S],
                                              ACT.Copy, scale=gain_T[:, c:c + 1])
                    done.then_inc(turned_hi, 1)
                    n.bank = n.bank + 1

            def root_of(sums, ln, y, count):
                link(activation(ln, sums, ACT.Ln, bias=eps[:, 0:1], scale=1.0 / count))
                activation(y, ln, ACT.Exp, scale=-0.5).then_inc(root, 1)
                n.roots += 1

            n.roots = n.squares = n.scales = n.h = 0

            def row_squares(norm, tile, width, blk):
                activation(square_flat[:, 0:width], tile[:, blk, 0:width], ACT.Square,
                           accum_out=norms[:, norm, 0, blk:blk + 1]).then_inc(squared, 1)
                n.squares += 1
                act.wait_ge(squared, n.squares)

            def row_root(norm, width):
                root_of(norms[:, norm, 0, :], norms[:, norm, 4, :], norms[:, norm, 2, :], width)

            def stream_norm(norm, gains=None):
                gains = norm if gains is None else gains
                for blk in range(TB):
                    act.wait_ge(h_ready, n.h + blk + 1)
                    row_squares(norm, h, D, blk)
                    if blk == 0:
                        split_banks(uT_hi, 0, KT, stream_banks[gains], gains)
                row_root(norm, D)
                n.h += TB

            def scaled_by(norm):
                n.scales += 1
                act.wait_ge(row_scale, n.scales)
                n.norm = norm

            def scale_of(blk, sign=1):
                i = 5 if sign > 0 else 6
                return norms[:, n.norm, i, blk:blk + 1]

            def copy_block(blk, copies):
                if blk == 0:
                    act.wait_ge(blk0_done, n.chunk + 1)
                else:
                    act.wait_ge(unit_used, n.unit)
                for i, (dst, src, func, scale) in enumerate(copies):
                    done = activation(dst, src, func, scale=scale)
                done.then_inc(acc_read, 1)

            def copy_chunk(copies):
                for blk in range(TB):
                    copy_block(blk, copies(blk))
                n.chunk = n.chunk + 1

            def plain(dst, width=512):
                return lambda blk: [(dst(blk), acc[blk][:, 0:width], ACT.Copy, scale_of(blk))]

            def copy_pair(kind, t, pair0, banks=(0,)):
                per = 2 if kind == "mla" else 1
                for j in range(per):
                    qkT_ps = qk_banks[banks[(per * t + j) % len(banks)]]
                    act.wait_ge(qkT_done, n.turn + 1)
                    if kind == "mla":
                        activation((qkT, qkT_odd)[j][0:MLA_QK, t, :], qkT_ps[0:MLA_QK, :], ACT.Copy)\
                            .then_inc(qkT_read, 1)
                    elif kind == "last":
                        activation(qkT[:, t, 0:S], qkT_ps[:, 0:S], ACT.Copy, scale=g_now[:, 0:1])
                        activation(qkT[:, t, S:2 * S], qkT_ps[:, S:2 * S], ACT.Copy,
                                   scale=g_now[:, 1:2]).then_inc(qkT_read, 1)
                    else:
                        activation(qkT[:, t, :], qkT_ps[:, :], ACT.Copy).then_inc(qkT_read, 1)
                    n.turn = n.turn + 1

            def soft_plus(t, pair0):
                act.wait_ge(logit_done, pair0 + (t + 1))
                since(act, max_done, pair0 + t)
                z = pair_ps[:, :, 0:384]
                activation(sb_tmp[0], z, ACT.Relu, scale=HD ** -0.5)
                activation(sb_tmp[1], z, ACT.Abs, scale=HD ** -0.5).then_inc(sb_read, 1)
                act.wait_ge(sb_read, pair0 + (t + 1))
                link(activation(sb_tmp[1], sb_tmp[1], ACT.Exp, scale=-1.0))
                activation(sb_tmp[1], sb_tmp[1], ACT.Ln, bias=1.0).then_inc(sb_abs, 1)

            def exponentiate(kind, t, pair0, head0):
                act.wait_ge(max_done, pair0 + (t + 1))
                pr = logit[:, t % 3, :, :]
                if kind == "sb":
                    activation(pr, pr, ACT.Exp).then_inc(prob_done, 1)
                    return
                for blk in range(TB):
                    cols = key_cols(blk)[0]
                    for j in range(2):
                        head = slice(2 * t + j, 2 * t + j + 1)
                        done = activation(pr[:, j, cols], pr[:, j, cols], ACT.Exp,
                                          bias=negmax8[:, blk, head], accum_out=total8[:, blk, head])
                done.then_inc(prob_done, 1)

            def copy_probs(t, pair0):
                act.wait_ge(prT_done, pair0 + (t + 1))
                activation(prT[:, t % 2, 0, :], turn_ps[:, 0, 0:384], ACT.Copy).then_inc(prT_act, 1)

            def round_outputs(t, pair0, kt0):
                act.wait_ge(out_done, pair0 + (t + 1))
                activation(oT_hi[:, kt0 + t, :], out_ps[:, 0:S], ACT.Copy).then_inc(out_hi, 1)

            def attention_step(kind, s, pair0, head0, kt0=None):
                if kt0 is not None and 3 <= s:
                    round_outputs(s - 3, pair0, kt0)
                if 1 <= s < 5:
                    exponentiate(kind, s - 1, pair0, head0)
                if 2 <= s:
                    copy_probs(s - 2, pair0)

            def attend(kind, kt0, head0=0):
                pair0 = n.pair
                for s in range(8):
                    if s < 2:
                        copy_pair(kind, 2 * s, pair0, (0, 1, 2))
                        copy_pair(kind, 2 * s + 1, pair0, (0, 1, 2))
                    if 3 < s:
                        round_outputs(s - 4, pair0, kt0)
                    if 2 <= s < 6:
                        copy_probs(s - 2, pair0)
                    if s < 4:
                        exponentiate(kind, s, pair0, head0)
                n.pair = pair0 + 4
                for _ in range(4):
                    slot_step()

            def project(chunks, prefetch=(UNIT,) * 6):
                s = 0
                later = None
                for done in chunks:
                    for _ in range(2):
                        slot_step(prefetch[s])
                        if later:
                            later()
                        later = None
                        s += 1
                    later = done()

            def project_and_attend(chunks, kind, head0=0, gains=None, prefetch=(UNIT,) * 6, after={}, kt0=None, to=6):
                pair0 = n.pair
                if kind == "last":
                    link(activation(g_now[:, :], g_col[:, bass.ds(gains, 2)], ACT.Copy))
                later = None
                for s in range(to):
                    if s < 2 * len(chunks):
                        slot_step(prefetch[s])
                    if later:
                        later()
                    later = None
                    for t in ((0,), (1, 2, 3))[s] if s < 2 else ():
                        copy_pair(kind, t, pair0)
                    attention_step(kind, s, pair0, head0, kt0)
                    if kind == "sb":
                        if s % 2:
                            chunks[s // 2]()
                        if s == 3:
                            split_banks(uT_hi, 0, 3, latent_banks, CQ)
                            split_banks(uT_hi, 3, 2, latent_banks[2:], CKV)
                        soft_plus(s, pair0)
                    elif s % 2 and s < 2 * len(chunks) - 1:
                        later = chunks[s // 2]()
                    if s in after:
                        after[s]()
                if kind == "band":
                    round_outputs(3, pair0, kt0)
                if kind != "sb":
                    later = chunks[-1]()
                    if later:
                        later()
                n.pair = pair0 + 4

            def copy_qkv(i):
                def done():
                    if i < 2:
                        since(act, qkT_done, n.turn)
                    else:
                        since(act, out_done, n.used)
                    copy_chunk(plain(lambda blk: qkv[:, i, blk, :]))
                return done

            def head_norm(i):
                since(act, summed, n.sums)
                act.wait_ge(acc_read, n.chunk * 2)
                activation(square[:, :, :], qkv[:, i, :, :], ACT.Square).then_inc(squared, 1)
                n.squares = n.squares + 1
                n.sums = n.sums + 1

            def head_root():
                act.wait_ge(summed, n.sums)
                root_of(stat[:, 0, :], stat[:, 4, :], stat[:, 2, :], HD)

            n.sums = 0

            def copy_and_norm(i):
                def done():
                    copy_qkv(i)()
                    head_norm(i)
                    return head_root
                return done

            def window_kv():
                since(act, qkT_done, n.turn)
                since(act, out_done, n.used)
                def copies(blk):
                    def four(dst, c0):
                        return (dst.rearrange("p (g r d) -> p g r d", g=2, r=4),
                                acc[blk][:, c0:c0 + 128].rearrange("p (g d) -> p g d", g=2)
                                .unsqueeze(2).broadcast_to([P, 2, 4, HD]), ACT.Copy, scale_of(blk))
                    return [four(qkv[:, 1, blk, :], 0), four(qkv[:, 2, blk, :], 128)]
                copy_chunk(copies)
                act.wait_ge(swish_done, 1)
                head_norm(1)
                return head_root

            def swiglu():
                n0, b0 = n.written, n.bank

                def gate(c):
                    act.wait_ge(unit_used, n.unit)
                    since(act, u_ready, n0 + c)
                    step_ps = turn_ps if isinstance(c, int) and c == 0 else pair_ps
                    activation(hid_e[:, 0, :], step_ps[:, 0, 0:FT], ACT.Exp, scale=scale_of(0, -1))
                    link(activation(hid_e[:, 1, :], step_ps[:, 1, 0:FT], ACT.Exp, scale=scale_of(1, -1)))
                    link(activation(hid_e, hid_e, ACT.Ln, bias=1.0))
                    activation(hid_e, hid_e, ACT.Exp, scale=-1.0).then_inc(gate_exp, 1)

                def split_hidden(c):
                    act.wait_ge(turned, b0 + c + 1)
                    activation(oT_hi[:, 0:2, :].rearrange("p k t -> p (k t)"), turn_ps[:, 0, :], ACT.Copy)\
                        .then_inc(turned_hi, 1)

                def step(c):
                    slot_step()
                    split_hidden(c - 1)
                    slot_step()
                    gate(c)
                    slot_step()

                slot_step()
                slot_step()
                gate(0)
                step(1)
                u0, local0, base0, own0 = n.unit, n.raw_local, n.raw_base, own[0]
                with act.Fori(2, NF) as c:
                    n.unit = u0 + (c - 2) * 3
                    own[0] = own0 + (c - 2) * 2
                    n.raw_base, n.raw_local = (c - 2) * 32 + base0, local0
                    step(c)
                trips = NF - 2
                n.unit, own[0] = u0 + 3 * trips, own0 + 2 * trips
                n.raw_base, n.raw_local = base0, local0 + 3 * trips
                split_hidden(NF - 1)
                slot_step()
                n.written, n.bank = n0 + NF, b0 + NF

            act.wait_ge(eps_set, 1)
            for blk in range(TB):
                act.wait_ge(x_loaded, 16 * TB)
                row_squares(MIX0, h, D, blk)
            act.wait_ge(tables_T, 1)
            activation(gain_T[:, :], acc[3][:, 0:GAIN_ROWS], ACT.Copy).then_inc(gains_set, 1)
            activation(tabT[:, :], acc[3][0:32, 64:104], ACT.Copy).then_inc(gains_set, 1)
            act.wait_ge(gains_set, 2)
            split_banks(uT_hi, 0, KT, stream_banks[MIX0], MIX0)
            round_unit(0)
            row_root(MIX0, D)
            round_unit(1)
            for group, row in enumerate((0, 2, 2, 2, 4)):
                done = activation(g_col[:, 2 * group:2 * group + 2], gain_T[:, QK_COL + row:QK_COL + row + 2], ACT.Copy)
            link(done)
            n.used = 0
            scaled_by(MIX0)
            project([copy_qkv(i) for i in range(3)], (UNIT,) * 4 + (1536, 1536))

            project_and_attend([lambda: copy_chunk(plain(lambda blk: cq[:, blk, :], 384)),
                                lambda: copy_chunk(lambda blk: [
                                    (ckv[:, blk, :], acc[blk][:, 0:256], ACT.Copy, scale_of(blk)),
                                    (k_rot[:, blk, :], acc[blk][:, 256:288], ACT.Copy, scale_of(blk))])],
                               "sb", prefetch=(1152, 1152, 1152, 1152), kt0=4, to=4)
            pair0 = n.pair - 4
            for norm, tile, width in ((CQ, cq, 384), (CKV, ckv, 256)):
                for blk in range(TB):
                    row_squares(norm, tile, width, blk)
                row_root(norm, width)
            attention_step("sb", 4, pair0, 0, 4)
            act.wait_ge(rel_stored, 16)
            for i in range(2):
                slot_step(1024)
                if i == 0:
                    scaled_by(CQ)
                copy_chunk(lambda blk: [(q_mla[:, blk, 4 * i:4 * i + 4, :].rearrange("p n c -> p (n c)"),
                                         acc[blk][:, 0:384], ACT.Copy, scale_of(blk))])
                if i == 0:
                    attention_step("sb", 5, pair0, 0, 4)
            round_outputs(3, pair0, 4)
            for i in range(2):
                slot_step()
                if i == 0:
                    scaled_by(CKV)
                def kv(blk):
                    src = acc[blk][:, :].rearrange("p (n c) -> p n c", c=128)
                    return [(k_mla[:, blk, 4 * i:4 * i + 4, 0:HD], src[:, :, 0:HD], ACT.Copy, scale_of(blk)),
                            (v_mla[:, blk, 256 * i:256 * i + 256].rearrange("p (n c) -> p n c", c=HD),
                             src[:, :, HD:128], ACT.Copy, scale_of(blk))]
                copy_chunk(kv)
            attend("mla", 0)
            stream_norm(FFN0)
            scaled_by(FFN0)
            swiglu()
            stream_norm(MIX1)
            scaled_by(MIX1)
            n.used = 8
            project([copy_qkv(i) for i in range(3)])
            n.used = 12
            project_and_attend([copy_qkv(i) for i in range(3)], "band", 0, kt0=0)
            attend("band", 4, 8)
            stream_norm(FFN1)
            scaled_by(FFN1)
            swiglu()
            act.wait_ge(gains_merged, 1)
            stream_norm(FINAL, LN2)
            for blk in range(TB):
                act.wait_ge(h_ready, n.h + blk + 1)
                row_squares(LN2, h, D, blk)
            row_root(LN2, D)
            scaled_by(LN2)
            n.used = n.pair
            project([copy_and_norm(0), copy_and_norm(1), copy_qkv(2)])
            u0, c0, p0, t0, local0, base0 = n.unit, n.chunk, n.pair, n.turn, n.raw_local, n.raw_base
            own0, s0, q0, r0 = own[0], n.sums, n.squares, n.roots
            with act.Fori(0, 3) as g:
                n.unit, n.chunk, n.pair, n.turn = u0 + g * 6, c0 + g * 3, p0 + g * 4, t0 + g * 4
                n.used = p0 + g * 4 + 4
                n.raw_base, n.raw_local = g * 64 + base0, local0
                own[0], n.sums, n.squares = own0 + g * 3, s0 + g * 2, q0 + g * 2
                project_and_attend([copy_and_norm(0), copy_and_norm(1), copy_qkv(2)], "last", g * 8, g * 2)
            n.unit, n.chunk, n.pair, n.turn = u0 + 18, c0 + 9, p0 + 12, t0 + 12
            n.raw_base, n.raw_local = base0, local0 + 18
            own[0], n.sums, n.squares, n.roots = own0 + 9, s0 + 6, q0 + 6, r0 + 6
            n.used = p0 + 16
            def sigmoid():
                act.wait_ge(acc_read, n.chunk * 2)
                link(activation(square[:, :, :], square[:, :, :], ACT.Ln, bias=1.0))
                activation(square[:, :, :], square[:, :, :], ACT.Exp, scale=-1.0).then_inc(gate_exp, 1)

            def swish_gate(i):
                def done():
                    if i == 0:
                        act.wait_ge(max_done, 28)
                        act.wait_ge(summed, n.sums)
                    since(act, swish_done, i)
                    copy_chunk(lambda blk: [(square[:, blk, :], acc[blk][:, :], ACT.Exp, scale_of(blk, -1)),
                                            (swish[:, i, blk, :], acc[blk][:, :], ACT.Copy, scale_of(blk))])
                    sigmoid()
                return done

            def factors(i, lo, hi):
                def run():
                    act.wait_ge(comb_d, i + 1)
                    activation(comb[:, lo:hi, :, :], comb[:, lo:hi, :, :], ACT.Exp).then_inc(comb_a, 1)
                return run

            def gate_exponentials(step):
                since(act, swish_done, 3) if step == 0 else act.wait_ge(gated, step)
                copy_chunk(lambda blk: [(square[:, blk, :], acc[blk][:, :], ACT.Exp, scale_of(blk, -1))])
                sigmoid()
            project_and_attend([copy_and_norm(0), swish_gate(0), window_kv], "last", 24, 6,
                               prefetch=(UNIT, UNIT, 1024, 1024, UNIT, UNIT))
            project_and_attend([swish_gate(1), swish_gate(2), lambda: gate_exponentials(0)], "last", 32, 8,
                               after={3: factors(0, 1, 4), 5: lambda: split_banks(oT_hi, 0, 4, turn_banks)})
            for i in range(3):
                if i:
                    split_banks(oT_hi, 4 * (i % 2), 4, turn_banks)
                for half in range(2):
                    step = 2 * i + half
                    if step:
                        for _ in range(2):
                            slot_step()
                        gate_exponentials(step)
                    if step == 1:
                        factors(1, 5, 7)()
                    if step == 5:
                        split_banks(oT_hi, 4, 4, turn_banks)
                    slot_step()
                    copy_chunk(lambda blk: [(branch_out[:, blk, :], acc[blk][:, :], ACT.Copy, 1.0)])
            slot_step()
            split_banks(oT_hi, 0, 4, pair_banks)
            for left in (3, 2, 1):
                slot_step(ahead_exists=left > 2)

        @block.vector
        def _(dve):
            n = Ordinals()
            own = [0]
            v = nc.vector
            n.roots = n.squares = n.h = n.exps = n.chunk = 0

            def link(ins):
                own[0] = own[0] + 1
                ins.then_inc(dve_self, 1)
                dve.wait_ge(dve_self, own[0])

            def split_unit(ahead=2, width=UNIT):
                slot = (n.slot + ahead) % RING
                dve.wait_ge(hi_done, n.unit + (ahead + 1))
                v.tensor_tensor(w_lo[:, slot, 0:width], w_raw[:, slot, 0:width],
                                w_hi[:, slot, 0:width].bitcast(f32), ALU.subtract).then_inc(lo_done, 1)

            def slot_step(width=UNIT, ahead_exists=True):
                if ahead_exists:
                    split_unit(2, width)
                n.next_unit()

            def split_banks(hi, lo, kt0, nkt, banks, norm=None):
                for k0 in range(0, nkt, 2):
                    m = min(2, nkt - k0)
                    dve.wait_ge(turned_hi, n.bank + 1)
                    if norm is None:
                        a, b = [t[:, kt0 + k0:kt0 + k0 + m, :].rearrange("p k t -> p (k t)") for t in (lo, hi)]
                        done = v.tensor_tensor(a, banks[k0 // 2][:, 0:m * S], b.bitcast(f32), ALU.subtract)
                    else:
                        for k in range(k0, k0 + m):
                            c = GAIN_COL[norm] + k
                            done = v.scalar_tensor_tensor(
                                lo[:, kt0 + k, :], banks[k0 // 2][:, (k - k0) * S:(k - k0 + 1) * S],
                                gain_T[:, c:c + 1], hi[:, kt0 + k, :].bitcast(f32), ALU.mult, ALU.subtract)
                    done.then_inc(turned_lo, 1)
                    n.bank = n.bank + 1

            def sharpen(sums, a, y, t, count):
                link(v.tensor_scalar(a, sums, 1.0 / count, EPS, ALU.mult, ALU.add))
                n.roots = n.roots + 1
                dve.wait_ge(root, n.roots)
                link(v.scalar_tensor_tensor(t, y, -0.5, y, ALU.mult, ALU.mult))
                link(v.tensor_tensor(t, t, a, ALU.mult))
                link(v.scalar_tensor_tensor(y, t, 1.5, y, ALU.add, ALU.mult))

            def row_scales(norm, width, times=None):
                n.squares = n.squares + 2
                dve.wait_ge(squared, n.squares)
                sums, a, y, t, _, y1, minus, twice = [norms[:, norm, i, :] for i in range(8)]
                sharpen(sums, a, y, t, width)
                if times is not None:
                    link(v.tensor_tensor(y, y, norms[:, times, 2, :], ALU.mult))
                v.tensor_scalar_mul(minus, y, -1.0)
                v.tensor_tensor(twice, y, y, ALU.mult)
                v.tensor_copy(y1, y).then_inc(row_scale, 1)

            def stream_norm(norm):
                split_banks(uT_hi, uT_lo, 0, KT, stream_banks[norm], norm)
                row_scales(norm, D)

            n.handed = 0

            def add_projection():
                n.proj += 1
                for blk in range(TB):
                    if blk == 0:
                        dve.wait_ge(proj_done, n.proj)
                    else:
                        dve.wait_ge(unit_used, n.unit)
                    for half in range(2):
                        c = slice(512 * half, 512 * half + 512)
                        done = v.tensor_tensor(h[:, blk, c], acc[2 * blk + half][:, :], h[:, blk, c], ALU.add)
                    done.then_inc(h_ready, 1)
                n.h += 2

            def maxima(kind, t, pair0, head0, bias_of):
                pr = logit[:, t % 3, :, :]
                dve.wait_ge(logit_done, pair0 + (t + 1))
                since(dve, prT_done, pair0 + max(t - 2, 0))
                scale = (MLA_QK if kind == "mla" else HD) ** -0.5
                for blk in range(TB):
                    cols, mask_cols = key_cols(blk)
                    done = v.scalar_tensor_tensor(pr[:, :, cols][:, :, ::-1], pair_ps[:, :, cols][:, :, ::-1], scale,
                                                  bias_of(t, mask_cols), ALU.mult, ALU.add)
                done.then_inc(logit_read, 1)
                dve.wait_ge(logit_read, pair0 + (t + 1))
                for blk in range(TB):
                    done = v.tensor_reduce(negmax8[:, blk, 2 * t:2 * t + 2], pr[:, :, key_cols(blk)[0]],
                                           op=ALU.max, axis=AX.X, negate=True)
                done.then_inc(max_done, 1)

            def stick(t, pair0):
                pr = logit[:, t % 3, :, :]
                dve.wait_ge(sb_read, pair0 + (t + 1))
                since(dve, prT_done, pair0 + max(t - 2, 0))
                for blk in range(TB):
                    cols, mask_cols = key_cols(blk)
                    done = v.scalar_tensor_tensor(pr[:, :, cols], pair_ps[:, :, cols], HD ** -0.5,
                                                  m_strict[:, mask_cols].unsqueeze(1).broadcast_to(
                                                      [P, 2, mask_cols.stop - mask_cols.start]), ALU.mult, ALU.add)
                done.then_inc(logit_read, 1)
                dve.wait_ge(sb_abs, pair0 + (t + 1))
                link(v.tensor_tensor(sb_tmp[0], sb_tmp[0], sb_tmp[1], ALU.add))
                for blk in range(TB):
                    cols, mask_cols = key_cols(blk)
                    for j in range(2):
                        done = v.tensor_tensor_scan(sb_tmp[2][:, j, cols][:, ::-1], sb_tmp[0][:, j, cols][:, ::-1],
                                                    m_keep[:, mask_cols][:, ::-1], 0.0, ALU.add, ALU.mult)
                dve.wait_ge(logit_read, pair0 + (t + 1))
                link(done)
                v.tensor_tensor(pr, pr, sb_tmp[2], ALU.subtract).then_inc(max_done, 1)

            def copy_probs(t, pair0):
                dve.wait_ge(prT_done, pair0 + (t + 1))
                v.tensor_copy(prT[:, t % 2, 1, :], turn_ps[:, 1, 0:384]).then_inc(prT_dve, 1)

            def normalise(t, pair0):
                dve.wait_ge(prob_done, pair0 + (t + 1))
                link(v.reciprocal(rtotal[:, :, :], total8[:, :, 2 * t:2 * t + 2]))
                for blk in range(TB):
                    for j in range(2):
                        pr = logit[:, t % 3, j, key_cols(blk)[0]]
                        done = v.tensor_scalar_mul(pr, pr, rtotal[:, blk, j:j + 1])
                done.then_inc(normed, 1)

            def outputs(t, pair0, kt0):
                dve.wait_ge(out_hi, pair0 + (t + 1))
                v.tensor_tensor(oT_lo[:, kt0 + t, :], out_ps[:, 0:S],
                                oT_hi[:, kt0 + t, :].bitcast(f32), ALU.subtract).then_inc(out_read, 1)

            def token_outputs(t, pair0, head0):
                dve.wait_ge(out_done, pair0 + (t + 1))
                o = out_ps[:, 0:S].rearrange("p (b n d) -> p b n d", b=TB, n=2)
                v.tensor_scalar_mul(heads[:, :, bass.ds(head0 + 2 * t, 2), :], o, 1.0).then_inc(out_read, 1)
                if t == 3:
                    v.tensor_copy(negmax[:, :, bass.ds(head0, 8)], negmax8[:, :, :])
                    v.tensor_copy(total[:, :, bass.ds(head0, 8)], total8[:, :, :])

            def attention_step(kind, s, pair0, head0, bias_of):
                if kind != "last" and 3 <= s:
                    outputs(s - 3, pair0, head0)
                if kind == "band" and 1 <= s < 5:
                    normalise(s - 1, pair0)
                if kind == "sb" and s == 3:
                    copy_probs(2, pair0)
                    split_banks(uT_hi, uT_lo, 0, 3, latent_banks, CQ)
                    split_banks(uT_hi, uT_lo, 3, 2, latent_banks[2:], CKV)
                    stick(3, pair0)
                    return
                if s < 4:
                    if kind == "sb":
                        stick(s, pair0)
                    else:
                        maxima(kind, s, pair0, head0, bias_of)
                if 1 <= s < 5:
                    copy_probs(s - 1, pair0)
                if kind == "last" and 2 <= s:
                    token_outputs(s - 2, pair0, head0)

            def attend(kind, kt0, bias_of):
                for s in range(8):
                    if 1 <= s < 5:
                        normalise(s - 1, n.pair)
                    if 3 < s:
                        outputs(s - 4, n.pair, kt0)
                    if s < 4:
                        maxima(kind, s, n.pair, None, bias_of)
                    if 2 <= s < 6:
                        copy_probs(s - 2, n.pair)
                n.pair = n.pair + 4
                for _ in range(4):
                    slot_step()
                add_projection()

            def project(done, prefetch=(UNIT,) * 6, after_unit={}):
                for s in range(6):
                    slot_step(prefetch[s])
                    if s in after_unit:
                        after_unit[s]()
                    if s in done:
                        done[s]()

            def project_and_attend(units, kind, head0=0, bias_of=None, done={}, prefetch=(UNIT,) * 6, after_unit={},
                                   to=6):
                for s in range(to):
                    if s < units:
                        slot_step(prefetch[s])
                    if s in after_unit:
                        after_unit[s]()
                    attention_step(kind, s, n.pair, head0, bias_of)
                    if s in done:
                        done[s]()
                if kind == "band":
                    outputs(3, n.pair, head0)
                n.pair = n.pair + 4

            def head_sums():
                n.squares = n.squares + 1
                dve.wait_ge(squared, n.squares)
                n.sums = n.sums + 1
                v.tensor_reduce(stat[:, 0, :], square[:, :, :].rearrange("p b (n d) -> p (b n) d", d=HD),
                                op=ALU.add, axis=AX.X).then_inc(summed, 1)

            def head_norm(i):
                def run():
                    dve.wait_ge(summed, n.sums)
                    sharpen(stat[:, 0, :], stat[:, 1, :], stat[:, 2, :], stat[:, 3, :], HD)
                    q = qkv[:, i, :, :].rearrange("p b (n d) -> p (b n) d", d=HD)
                    v.tensor_tensor(q, q, stat[:, 2, :].unsqueeze(2).broadcast_to([P, 16, HD]), ALU.mult)\
                        .then_inc(qk_ready, 1)
                    n.qk = n.qk + 1
                    dve.wait_ge(qk_ready, n.qk)
                return run

            n.sums, n.qk = 0, 0

            def rotate(x, y, heads_n, blk):
                t = [cs_t[:, i, 0:heads_n, :] for i in range(4)]
                c, s = [cs[:, blk, i, :].unsqueeze(1).broadcast_to([P, heads_n, 16]) for i in range(2)]
                x1, x2 = x[:, :, 0:16], x[:, :, 16:32]
                v.tensor_tensor(t[0], x1, c, ALU.mult)
                v.tensor_tensor(t[1], x2, s, ALU.mult)
                v.tensor_tensor(t[2], x2, c, ALU.mult)
                link(v.tensor_tensor(t[3], x1, s, ALU.mult))
                v.tensor_tensor(y[:, :, 0:16], t[0], t[1], ALU.subtract)
                link(v.tensor_tensor(y[:, :, 16:32], t[2], t[3], ALU.add))

            def swiglu(norm):
                n0, b0, e0 = n.handed, n.bank, n.exps

                def gate(c):
                    dve.wait_ge(gate_exp, e0 + c + 1)
                    step_ps = turn_ps if isinstance(c, int) and c == 0 else pair_ps
                    gate_ps, up_ps = step_ps[:, :, 0:FT], step_ps[:, :, FT:2 * FT]
                    for blk in range(TB):
                        done = v.scalar_tensor_tensor(hid_g[:, blk, :], gate_ps[:, blk, :],
                                                      norms[:, norm, 7, blk:blk + 1], hid_e[:, blk, :],
                                                      ALU.mult, ALU.mult)
                    link(done)
                    since(dve, turned, b0 + c)
                    v.tensor_tensor(hid, up_ps, hid_g, ALU.mult).then_inc(u_ready, 1)

                def split_hidden(c):
                    dve.wait_ge(turned_hi, b0 + c + 1)
                    lo, hi = [t[:, 0:2, :].rearrange("p k t -> p (k t)") for t in (oT_lo, oT_hi)]
                    v.tensor_tensor(lo, turn_ps[:, 0, :], hi.bitcast(f32), ALU.subtract).then_inc(turned_lo, 1)

                def step(c):
                    slot_step()
                    split_hidden(c - 1)
                    slot_step()
                    gate(c)
                    slot_step()

                slot_step()
                slot_step()
                gate(0)
                step(1)
                u0, own0 = n.unit, own[0]
                with dve.Fori(2, NF) as c:
                    n.unit = u0 + (c - 2) * 3
                    own[0] = own0 + (c - 2)
                    step(c)
                n.unit, own[0] = u0 + 3 * (NF - 2), own0 + NF - 2
                split_hidden(NF - 1)
                slot_step()
                n.handed, n.bank, n.exps = n0 + NF, b0 + NF, e0 + NF
                add_projection()

            dve.wait_ge(gains_set, 1)
            ln2, final = [gain_T[:, GAIN_COL[i]:GAIN_COL[i] + KT] for i in (LN2, FINAL)]
            v.tensor_tensor(ln2, ln2, final, ALU.mult).then_inc(gains_merged, 1)
            split_banks(uT_hi, uT_lo, 0, KT, stream_banks[MIX0], MIX0)
            split_unit(0)
            row_scales(MIX0, D)
            split_unit(1)

            def distance_rows():
                dve.wait_ge(consts, CONSTS)
                dve.wait_ge(tab_done, 1)
                v.tensor_tensor(rel_f, acc[2][0:40, 0:REL], dist_m, ALU.add).then_inc(rel_ready, 1)
            project({4: distance_rows}, (UNIT,) * 4 + (1536, 1536))

            project_and_attend(4, "sb", 4, prefetch=(1152, 1152, 1152, 1152), to=4)
            pair0 = n.pair - 4
            row_scales(CQ, 384)
            row_scales(CKV, 256)
            slot_step(1024)
            attention_step("sb", 4, pair0, 4, None)
            slot_step(1024)
            attention_step("sb", 5, pair0, 4, None)
            dve.wait_ge(rel_stored, 16)
            for blk in range(TB):
                rotate(k_rot[:, blk, :].unsqueeze(1), k_rot2[:, blk, :].unsqueeze(1), 1, blk)
            for blk in range(TB):
                v.tensor_copy(k_mla[:, blk, :, HD:MLA_QK], k_rot2[:, blk, :].unsqueeze(1).broadcast_to([P, 8, 32]))
            dve.wait_ge(acc_read, 14)
            for blk in range(TB):
                q_rot = q_mla[:, blk, :, HD:MLA_QK]
                rotate(q_rot, q_rot, 8, blk)
            v.tensor_copy(norms[:, CQ, 3, 0:1], norms[:, CQ, 2, 0:1]).then_inc(qk_ready, 1)
            outputs(3, pair0, 4)
            slot_step()
            slot_step()
            n.qk = 1
            mask = lambda t, cols: m_chunk[:, back(cols)].unsqueeze(1).broadcast_to(
                [P, 2, cols.stop - cols.start])
            attend("mla", 0, mask)
            stream_norm(FFN0)
            swiglu(FFN0)
            stream_norm(MIX1)
            project({})
            dve.wait_ge(band_ready, 1)
            def table(slot):
                return lambda t, cols: bias[:, slot, 2 * t:2 * t + 2, back(cols)]
            project_and_attend(6, "band", 0, table(2))
            attend("band", 4, table(3))
            stream_norm(FFN1)
            swiglu(FFN1)
            dve.wait_ge(gains_merged, 1)
            split_banks(uT_hi, uT_lo, 0, KT, stream_banks[LN2], LN2)
            n.squares = n.squares + 2
            dve.wait_ge(squared, n.squares)
            sharpen(*[norms[:, FINAL, i, :] for i in range(4)], D)
            dve.wait_ge(gain_full, 16)
            for blk in range(TB):
                v.scalar_tensor_tensor(h[:, blk, :], h[:, blk, :], norms[:, FINAL, 2, blk:blk + 1],
                                       gain, ALU.mult, ALU.mult).then_inc(h_ready, 1)
            row_scales(LN2, D, times=FINAL)
            project({1: head_sums, 3: head_sums}, after_unit={2: head_norm(0), 4: head_norm(1)})
            for g in range(4):
                dve.wait_ge(bias_full[g], 16)
            u0, p0, own0, s0, q0, r0, k0 = n.unit, n.pair, own[0], n.sums, n.squares, n.roots, n.qk
            with dve.Fori(0, 3) as g:
                n.unit, n.pair, own[0] = u0 + g * 6, p0 + g * 4, own0 + g * 8
                n.sums, n.squares, n.roots, n.qk = s0 + g * 2, q0 + g * 2, r0 + g * 2, k0 + g * 2
                def table_g(t, cols):
                    return flat_bias[:, bass.ds(g * 2048 + (2 * t * S), 2 * S)]\
                        .rearrange("p (j c) -> p j c", j=2)[:, :, back(cols)]
                project_and_attend(6, "last", g * 8, table_g, {1: head_sums, 3: head_sums},
                                   after_unit={2: head_norm(0), 4: head_norm(1)})
            n.unit, n.pair, own[0] = u0 + 18, p0 + 12, own0 + 24
            n.sums, n.squares, n.roots, n.qk = s0 + 6, q0 + 6, r0 + 6, k0 + 6

            def swish_gate(i):
                n.exps += 1
                dve.wait_ge(gate_exp, n.exps)
                v.tensor_tensor(swish[:, i, :, :], swish[:, i, :, :], square[:, :, :], ALU.mult)\
                    .then_inc(swish_done, 1)

            def window_keys():
                head_sums()
                head_norm(1)()
            project_and_attend(6, "last", 24, table(3), {1: head_sums, 3: lambda: swish_gate(0), 5: window_keys},
                               prefetch=(UNIT, UNIT, 1024, 1024, UNIT, UNIT), after_unit={2: head_norm(0)})

            def nm(group):
                return negmax[:, :, 8 * group:8 * group + 8]

            def tot(group):
                return total[:, :, 8 * group:8 * group + 8]

            cb = [comb[:, i, :, :] for i in range(8)]
            sinks_b = sink[:, :].unsqueeze(1).broadcast_to([P, TB, 8])

            def eight(group):
                return heads[:, :, 8 * group:8 * group + 8, :]

            def scaled(group, factor):
                link(v.tensor_tensor(eight(group), eight(group), factor.unsqueeze(3).broadcast_to([P, TB, 8, HD]),
                                     ALU.mult))

            def gate_branch(i, group):
                dve.wait_ge(swish_done, i + 1)
                o = eight(group).rearrange("p b n d -> p b (n d)")
                v.tensor_tensor(o, o, swish[:, i, :, :], ALU.mult).then_inc(u_ready, 1)
                n.handed += 1

            def full_over_total():
                link(v.reciprocal(cb[7], tot(0)))
                scaled(0, cb[7])

            def first_gate():
                gate_branch(0, 0)
                link(v.tensor_tensor(cb[0], nm(1), nm(2), ALU.min))
                link(v.tensor_tensor(cb[0], cb[0], nm(3), ALU.min))
                for g in (1, 2, 3):
                    done = v.tensor_tensor(cb[g], cb[0], nm(g), ALU.subtract)
                done.then_inc(comb_d, 1)

            def dilation_weights():
                dve.wait_ge(comb_a, 1)
                link(v.tensor_tensor(cb[0], cb[1], tot(1), ALU.mult))
                for g in (2, 3):
                    link(v.tensor_tensor(cb[7], cb[g], tot(g), ALU.mult))
                    link(v.tensor_tensor(cb[0], cb[0], cb[7], ALU.add))
                link(v.reciprocal(cb[0], cb[0]))
                for g in (1, 2, 3):
                    link(v.tensor_tensor(cb[g], cb[g], cb[0], ALU.mult))
                scaled(1, cb[1])

            def add_dilation(g):
                scaled(g, cb[g])
                link(v.tensor_tensor(eight(1), eight(1), eight(g), ALU.add))

            def last_gate():
                add_dilation(2)
                add_dilation(3)
                gate_branch(1, 1)
                link(v.scalar_tensor_tensor(cb[4], sinks_b, -1.0, nm(4), ALU.mult, ALU.min))
                v.tensor_tensor(cb[5], cb[4], nm(4), ALU.subtract)
                v.tensor_tensor(cb[6], sinks_b, cb[4], ALU.add).then_inc(comb_d, 1)

            def window_over_total():
                dve.wait_ge(comb_a, 2)
                link(v.tensor_tensor(cb[4], cb[5], tot(4), ALU.mult))
                link(v.tensor_tensor(cb[4], cb[4], cb[6], ALU.add))
                link(v.reciprocal(cb[4], cb[4]))
                link(v.tensor_tensor(cb[5], cb[5], cb[4], ALU.mult))
                scaled(4, cb[5])
                gate_branch(2, 4)

            dve.wait_ge(bias_full[4], 16)
            project_and_attend(6, "last", 32, table(0), {
                0: full_over_total, 1: lambda: swish_gate(1), 2: first_gate, 3: lambda: swish_gate(2),
                4: dilation_weights})
            for i in range(3):
                split_banks(oT_hi, oT_lo, 4 * (i % 2), 4, turn_banks)
                for half in range(2):
                    step = 2 * i + half
                    if step:
                        for _ in range(2):
                            slot_step()
                    if step == 1:
                        window_over_total()
                    if step == 5:
                        split_banks(oT_hi, oT_lo, 4, 4, turn_banks)
                    slot_step()
                    if step == 0:
                        last_gate()
                    n.exps += 1
                    dve.wait_ge(gate_exp, n.exps)
                    dve.wait_ge(acc_read, 68 + 4 * step)
                    m = merged[:, :, 512 * half:512 * half + 512]
                    if i == 0:
                        v.tensor_tensor(m, square[:, :, :], branch_out, ALU.mult).then_inc(gated, 1)
                    else:
                        link(v.tensor_tensor(branch_out, square[:, :, :], branch_out, ALU.mult))
                        v.tensor_tensor(m, m, branch_out, ALU.add).then_inc(gated, 1)
            slot_step()
            split_banks(oT_hi, oT_lo, 0, 4, pair_banks)
            for left in (3, 2, 1):
                slot_step(ahead_exists=left > 2)
            add_projection()


def shape_constants():
    f = np.float32
    p, j = np.arange(P)[:, None], np.arange(S)[None, :]
    strict = np.where(j < P + p, 0.0, MASKED).astype(f)
    keep = (j < P + p).astype(f)
    chunk = np.where(j // 64 <= (P + p) // 64, 0.0, MASKED).astype(f)
    inv_freq = (np.float32(10000.0) ** (-np.arange(0, 32, 2, dtype=f) / np.float32(32))).astype(f)
    ang = (np.arange(S, dtype=f)[:, None] * inv_freq[None, :]).astype(f)
    rope = np.stack([np.cos(ang), np.sin(ang)], 1).astype(f)
    rope = np.ascontiguousarray(rope.reshape(TB, P, 2, 16).transpose(1, 0, 2, 3))
    dist = np.arange(REL) - (P - 1)
    d0 = np.maximum(dist, 0)
    ratio = np.log(np.maximum(d0, 1).astype(f) / f(16)) / f(math.log(2048 / 16))
    large = np.minimum(16 + (ratio * f(16)).astype(np.int32), 31)
    bucket = np.where(d0 < 16, d0, large)
    onehot = (bucket[None, :] == np.arange(32)[:, None]).astype(f)
    ok = [dist >= 0] + [(dist >= 0) & (dist <= w) & (dist % d == 0) for w, d in ((128, 1), (512, 4), (2048, 16))] \
        + [(dist >= 0) & (dist < 128)]
    dist_mask = np.repeat(np.where(np.stack(ok), 0.0, MASKED).astype(f), 8, axis=0)
    return dict(identity=np.eye(P, dtype=f), strict_mask=strict, chunk_mask=np.ascontiguousarray(chunk[:, ::-1]), keep_mask=keep, rope=rope,
                bucket_onehot=onehot, dist_mask=dist_mask)


def kernel(**inputs):
    import numpy as np
    import concourse.bacc as bacc
    from concourse import mybir
    from concourse.bass_utils import run_bass_kernel_spmd

    first = {"w_in0": "ev_w_in", "g_cq": "ev_g_cq", "w_uq": "ev_w_uq", "g_ckv": "ev_g_ckv", "w_ukv": "ev_w_ukv",
             "w_out0": "ev_w_out", "w_qkv": "od_w_qkv", "rel_band": "od_rel_bias", "w_out1": "od_w_out",
             "g_ln2": "ln_g_2", "w_in2": "w_in_2", "qk_g": "qk_g_2", "sinks": "sinks_2", "w_branch": "w_branch_2",
             "w_out2": "w_out_2"}
    plain = {"x": "x", "g_mix": "g_mix", "g_ffn": "g_ffn", "w_gate": "w_gate", "w_up": "w_up", "w_down": "w_down",
             "g_final": "g_final", "rel_bias2": "rel_bias_2"}
    arrays = {k: np.ascontiguousarray(inputs[v])[0] for k, v in first.items()}
    arrays.update({k: np.ascontiguousarray(inputs[v]) for k, v in plain.items()})
    arrays.update(shape_constants())

    nc = bacc.Bacc("TRN2", target_bir_lowering=False, num_devices=1)
    aps = {k: nc.dram_tensor(f"in_{k}", a.shape, mybir.dt.from_np(a.dtype), kind="ExternalInput").ap()
           for k, a in arrays.items()}
    out = nc.dram_tensor("out_y", (1, S, D), mybir.dt.float32, kind="ExternalOutput").ap()
    build_program(nc, out=out, **aps)
    r = run_bass_kernel_spmd(nc, [{f"in_{k}": a for k, a in arrays.items()}], core_ids=[0])
    return r.results[0]["out_y"]
```
